# Optimizing a Trainium2 kernel written in Bass

```python
import jax, jax.numpy as jnp
from jax import lax
import numpy as np

D_MODEL = 2048
BATCH = 1
SEQ = 256
DEPTH = 1

CHUNK = 64
EPS = 1e-6

GLA_HEADS = 4
GLA_DK = 128
GLA_DV = 256
GLA_GATE_RANK = 16
GLA_GATE_TAU = 16.0

GDN_HEADS = 8
GDN_DK = 128
GDN_DV = 128
GDN_CONV = 4

MIX_WIDTH = GLA_HEADS * GLA_DV + GDN_HEADS * GDN_DV

GLA_QK = GLA_HEADS * GLA_DK
GLA_V = GLA_HEADS * GLA_DV
GDN_QK = GDN_HEADS * GDN_DK
GDN_V = GDN_HEADS * GDN_DV
SPLIT_SIZES = (GLA_QK, GLA_QK, GLA_V, GLA_GATE_RANK, GLA_V,
               GDN_QK, GDN_QK, GDN_V, GDN_HEADS, GDN_HEADS, GDN_V)
IN_COLS = sum(SPLIT_SIZES)

D_FF = ((8 * D_MODEL // 3 + 255) // 256) * 256

kernel_name = "hybrid_gla_gated_deltanet_block"

def rms_norm(x, w):
    xf = x.astype(jnp.float32)
    y = xf * lax.rsqrt(jnp.mean(xf * xf, axis=-1, keepdims=True) + EPS)
    return y * w.astype(jnp.float32)

def l2_norm(x):
    return x * lax.rsqrt(jnp.sum(x * x, axis=-1, keepdims=True) + EPS)

def to_chunks(t, n_heads):
    b, l, f = t.shape
    d = f // n_heads
    n = l // CHUNK
    return t.reshape(b, n, CHUNK, n_heads, d).transpose(1, 0, 3, 2, 4)

def from_chunks(t):
    n, b, h, c, d = t.shape
    return t.transpose(1, 0, 3, 2, 4).reshape(b, n * c, h, d)

def gla_chunked(q, k, v, log_a):
    _, b, h, c, dk = q.shape
    dv = v.shape[-1]
    causal = jnp.tril(jnp.ones((c, c), bool))

    def step(state, inp):
        qc, kc, vc, gc = inp
        cum = jnp.cumsum(gc, axis=-2)
        diff = cum[..., :, None, :] - cum[..., None, :, :]
        decay = jnp.exp(jnp.where(causal[:, :, None], diff, -jnp.inf))
        scores = jnp.einsum('bhtd,bhsd,bhtsd->bhts', qc, kc, decay)
        o = (jnp.einsum('bhts,bhsv->bhtv', scores, vc)
             + jnp.einsum('bhtd,bhdv->bhtv', qc * jnp.exp(cum), state))
        last = cum[..., -1:, :]
        state = (jnp.exp(last)[..., 0, :, None] * state
                 + jnp.einsum('bhsd,bhsv->bhdv', kc * jnp.exp(last - cum), vc))
        return state, o

    s0 = jnp.zeros((b, h, dk, dv), jnp.float32)
    _, o = lax.scan(step, s0, (q, k, v, log_a))
    return o

def gated_delta_chunked(q, k, v, g, beta):
    _, b, h, c, dk = q.shape
    dv = v.shape[-1]
    cum = jnp.cumsum(g, axis=-1)
    diff = cum[..., :, None] - cum[..., None, :]
    incl = jnp.tril(jnp.ones((c, c), bool))
    strict = jnp.tril(jnp.ones((c, c), bool), -1)
    gamma = jnp.exp(jnp.where(incl, diff, -jnp.inf))
    kb = k * beta[..., None]
    a_low = jnp.where(strict, jnp.einsum('nbhtd,nbhsd->nbhts', kb, k) * gamma, 0.0)
    eye = jnp.eye(c, dtype=a_low.dtype)
    rhs = jnp.concatenate([v * beta[..., None], kb * jnp.exp(cum)[..., None]], axis=-1)
    sol = lax.linalg.triangular_solve(eye + a_low, rhs, left_side=True, lower=True)
    u, w = sol[..., :dv], sol[..., dv:]
    attn = jnp.einsum('nbhtd,nbhsd->nbhts', q, k) * gamma
    qd = q * jnp.exp(cum)[..., None]
    kd = k * jnp.exp(cum[..., -1:] - cum)[..., None]
    g_last = jnp.exp(cum[..., -1])

    def step(state, inp):
        u_c, w_c, attn_c, qd_c, kd_c, gl = inp
        v_new = u_c - jnp.einsum('bhtk,bhkv->bhtv', w_c, state)
        o = (jnp.einsum('bhtk,bhkv->bhtv', qd_c, state)
             + jnp.einsum('bhts,bhsv->bhtv', attn_c, v_new))
        state = gl[..., None, None] * state + jnp.einsum('bhsk,bhsv->bhkv', kd_c, v_new)
        return state, o

    s0 = jnp.zeros((b, h, dk, dv), jnp.float32)
    _, o = lax.scan(step, s0, (u, w, attn, qd, kd, g_last))
    return o

def causal_depthwise_conv(x, w):
    ch = x.shape[-1]
    return lax.conv_general_dilated(
        x, w[:, None, :], window_strides=(1,), padding=[(GDN_CONV - 1, 0)],
        dimension_numbers=('NWC', 'WIO', 'NWC'), feature_group_count=ch)

def setup_inputs(seed: int = 0) -> dict:
    key = jax.random.key(seed)
    ks = jax.random.split(key, 20)
    f32 = jnp.float32

    def nrm(k, shape, scale):
        return jax.random.normal(k, shape, f32) * scale

    def gain(k, n):
        return 1.0 + 0.02 * jax.random.normal(k, (n,), f32)

    dt = jnp.exp(jax.random.uniform(ks[9], (GDN_HEADS,), f32, np.log(1e-3), np.log(1e-1)))
    dt_bias = dt + jnp.log(-jnp.expm1(-dt))
    return {
        "x": jax.random.normal(ks[0], (BATCH, SEQ, D_MODEL), f32),
        "attn_norm_w": gain(ks[1], D_MODEL),
        "w_in": nrm(ks[2], (D_MODEL, IN_COLS), D_MODEL ** -0.5),
        "gla_gate_w2": nrm(ks[3], (GLA_GATE_RANK, GLA_QK), GLA_GATE_RANK ** -0.5),
        "gla_gate_b": nrm(ks[4], (GLA_QK,), 0.01),
        "gla_norm_w": gain(ks[5], GLA_DV),
        "gdn_conv_w": nrm(ks[6], (GDN_CONV, 2 * GDN_QK + GDN_V), GDN_CONV ** -0.5),
        "gdn_a_log": jnp.log(jax.random.uniform(ks[7], (GDN_HEADS,), f32, 1.0, 16.0)),
        "gdn_dt_bias": dt_bias,
        "gdn_norm_w": gain(ks[8], GDN_DV),
        "w_out": nrm(ks[10], (MIX_WIDTH, D_MODEL), MIX_WIDTH ** -0.5),
        "ffn_norm_w": gain(ks[11], D_MODEL),
        "w_gate": nrm(ks[12], (D_MODEL, D_FF), D_MODEL ** -0.5),
        "w_up": nrm(ks[13], (D_MODEL, D_FF), D_MODEL ** -0.5),
        "w_down": nrm(ks[14], (D_FF, D_MODEL), D_FF ** -0.5),
        "final_norm_w": gain(ks[15], D_MODEL),
    }

def reference(x, attn_norm_w, w_in, gla_gate_w2, gla_gate_b, gla_norm_w, gdn_conv_w,
              gdn_a_log, gdn_dt_bias, gdn_norm_w, w_out, ffn_norm_w, w_gate, w_up,
              w_down, final_norm_w):
    f32 = jnp.float32
    bsz, seq, _ = x.shape
    h_res = x.astype(f32)
    for _layer in range(DEPTH):
        h = rms_norm(h_res, attn_norm_w)
        p = h @ w_in.astype(f32)
        idx = np.cumsum(SPLIT_SIZES)[:-1].tolist()
        (a_q, a_k, a_v, a_lr, a_gate,
         b_q, b_k, b_v, b_a, b_b, b_z) = jnp.split(p, idx, axis=-1)

        log_a = jax.nn.log_sigmoid(a_lr @ gla_gate_w2.astype(f32) + gla_gate_b.astype(f32)) / GLA_GATE_TAU
        o_a = gla_chunked(to_chunks(a_q * GLA_DK ** -0.5, GLA_HEADS), to_chunks(a_k, GLA_HEADS),
                          to_chunks(a_v, GLA_HEADS), to_chunks(log_a, GLA_HEADS))
        o_a = rms_norm(from_chunks(o_a), gla_norm_w)
        o_a = o_a.reshape(bsz, seq, GLA_V) * jax.nn.silu(a_gate)

        qkv = jax.nn.silu(causal_depthwise_conv(jnp.concatenate([b_q, b_k, b_v], -1),
                                                gdn_conv_w.astype(f32)))
        cq, ck, cv = jnp.split(qkv, [GDN_QK, 2 * GDN_QK], axis=-1)
        cq = l2_norm(cq.reshape(bsz, seq, GDN_HEADS, GDN_DK)) * GDN_DK ** -0.5
        ck = l2_norm(ck.reshape(bsz, seq, GDN_HEADS, GDN_DK))
        g = -jnp.exp(gdn_a_log.astype(f32)) * jax.nn.softplus(b_a + gdn_dt_bias.astype(f32))
        beta = jax.nn.sigmoid(b_b)
        n_ch = seq // CHUNK
        gc = g.reshape(bsz, n_ch, CHUNK, GDN_HEADS).transpose(1, 0, 3, 2)
        bc = beta.reshape(bsz, n_ch, CHUNK, GDN_HEADS).transpose(1, 0, 3, 2)
        o_b = gated_delta_chunked(to_chunks(cq.reshape(bsz, seq, GDN_QK), GDN_HEADS),
                                  to_chunks(ck.reshape(bsz, seq, GDN_QK), GDN_HEADS),
                                  to_chunks(cv, GDN_HEADS), gc, bc)
        o_b = rms_norm(from_chunks(o_b), gdn_norm_w)
        o_b = o_b.reshape(bsz, seq, GDN_V) * jax.nn.silu(b_z)

        mixed = jnp.concatenate([o_a, o_b], axis=-1)
        h_res = h_res + mixed @ w_out.astype(f32)

        hf = rms_norm(h_res, ffn_norm_w)
        ff = jax.nn.silu(hf @ w_gate.astype(f32)) * (hf @ w_up.astype(f32))
        h_res = h_res + ff @ w_down.astype(f32)

    y = rms_norm(h_res, final_norm_w)
    return y.astype(x.dtype)


_drawn_inputs = setup_inputs


def setup_inputs(seed=0):
    import zlib

    import numpy as np

    out = dict(_drawn_inputs(seed))
    spreads = {}
    factors = {'gla_gate_b': 8.0,
     'gla_norm_w': 6.693,
     'gdn_norm_w': 7.032,
     'ffn_norm_w': 4.437,
     'final_norm_w': 2.746}
    for name, (base, spread) in spreads.items():
        noise = np.random.default_rng([zlib.crc32(name.encode()), seed]).standard_normal(out[name].shape)
        drawn = base * np.exp(spread * noise) if base else spread * noise
        out[name] = __import__('jax').numpy.asarray(drawn.astype(out[name].dtype))
    for name, factor in factors.items():
        out[name] = (out[name] * factor).astype(out[name].dtype)
    return out
```

```python
from contextlib import ExitStack

import concourse.bass as bass
from concourse import mybir

F32 = mybir.dt.float32
F32R = mybir.dt.float32r
ALU = mybir.AluOpType
ACT = mybir.ActivationFunctionType
AX_X = mybir.AxisListType.X

P = 128
T = 256
NB = T // P
D = 2048
KT = D // P
DFF = 5632
FT = DFF // P
EPS = 1e-6
DK = 128
GLA_HEADS, GDN_HEADS, RANK = 4, 8, 16
TAU = 16.0
TAPS = 4

A_Q, A_K, A_V, A_LR, A_GATE = 0, 512, 1024, 2048, 2064
B_Q, B_K, B_V, B_A, B_Z = 3088, 4112, 5136, 6160, 6176

COLS = 256
UNIT = 1024
RING = 4
AHEAD = 2
PHASE_STEPS = 32

IN_BLOCKS = [c for p in range(4) for c in (B_K + COLS * p, B_Q + COLS * p, B_V + COLS * p, B_Z + COLS * p)]
IN_BLOCKS += [c for g in range(2) for c in (A_Q + COLS * g, A_K + COLS * g, A_V + 512 * g, A_V + 512 * g + COLS)]
IN_BLOCKS += [A_GATE + COLS * h for h in range(GLA_HEADS)]
NBLK = len(IN_BLOCKS)
BLK_UNITS = KT * COLS // UNIT
U_OUT = 1 + NBLK * BLK_UNITS
OUT_UNITS = KT * 512 // UNIT
U_GU = U_OUT + 4 * OUT_UNITS
PAIRS = DFF // COLS
GU_UNITS = 2 * BLK_UNITS
U_DOWN = U_GU + PAIRS * GU_UNITS
DOWN_UNITS = FT * 512 // UNIT
U_END = U_DOWN + 4 * DOWN_UNITS
OUT_ORDER = list(range(8, KT)) + list(range(8))


def hybrid_block(nc, x, attn_norm_w, w_in, gla_gate_w2, gla_gate_b, gla_norm_w, gdn_conv_w, gdn_a_log,
                 gdn_dt_bias, gdn_norm_w, w_out, ffn_norm_w, w_gate, w_up, w_down, final_norm_w, out):
    x_tok = x.rearrange("a (b p) d -> p (a b) d", p=P)
    out_tok = out.rearrange("a (b p) d -> p (a b) d", p=P)

    with ExitStack() as ctx:
        def sb(name, words, dt=F32, stack=ctx):
            return stack.enter_context(nc.sbuf_tensor(name, [P, words], dt))

        def sem(name):
            return ctx.enter_context(nc.semaphore(name))

        def cut(t, at, *shape):
            n = 1
            for s in shape:
                n *= s
            v = t[:, at:at + n]
            if len(shape) == 2:
                return v.rearrange("p (a b) -> p a b", a=shape[0])
            if len(shape) == 3:
                return v.rearrange("p (a b c) -> p a b c", a=shape[0], b=shape[1])
            return v

        raw = sb("raw", RING * UNIT)
        whi = sb("whi", RING * UNIT, F32R)
        wlo = sb("wlo", RING * UNIT, F32R)
        hhi_t = sb("hhi", KT * T, F32R)
        hlo_t = sb("hlo", KT * T, F32R)
        big = sb("big", NB * D)
        ident = sb("ident", P)
        ones = sb("ones", P)
        vec_t = sb("vecT", 132)
        cst = sb("cst", 4)
        rb = sb("rb", T)
        stat = sb("stat", 32)
        hhi, hlo = cut(hhi_t, 0, KT, T), cut(hlo_t, 0, KT, T)
        resid = cut(big, 0, NB, D)
        conv_w = vec_t[:, 0:96]
        attn_w, ffn_w = vec_t[:, 96:112], vec_t[:, 112:128]
        gla_w, gdn_w = vec_t[:, 128:130], vec_t[:, 130:131]
        eps_c, dk_eps_c, one_c = cst[:, 0:1], cst[:, 1:2], cst[:, 2:3]

        mix_scope = ExitStack()
        mhi_t = sb("mixhi", KT * T, F32R, mix_scope)
        mlo_t = sb("mixlo", KT * T, F32R, mix_scope)
        mhi, mlo = cut(mhi_t, 0, KT, T), cut(mlo_t, 0, KT, T)
        consts = sb("consts", 17 * P, stack=mix_scope)
        mask = cut(consts, 0, 8, P)
        msum = cut(consts, 8 * P, 9, P)
        after, upto = msum[:, 0, :], msum[:, 8, :]
        kqv = cut(big, 0, 6, T)
        convd = cut(big, 6 * T, 6, T)
        sumsq = cut(big, 12 * T, 4, T)
        gkd = big[:, 0:2048].rearrange("p (b l t) -> p b l t", b=2, l=8)
        gqd = big[:, 2048:4096].rearrange("p (b l t) -> p b l t", b=2, l=8)
        work = sb("work", 2048, stack=mix_scope)
        convin = cut(work, 0, 6, T + TAPS - 1)
        gexp, gprod = cut(work, 0, 8, P), cut(work, 1024, 8, P)
        gdn_a = sb("gdn_a", 2048, stack=mix_scope)
        vtok, ktok = cut(gdn_a, 0, 4, P), cut(gdn_a, 512, 4, P)
        wup, ylow = cut(gdn_a, 1024, 4, P), cut(gdn_a, 1536, 4, P)
        gon = gdn_a[:, 0:2048].rearrange("p (h n) -> p h n", h=4)
        gdn_b = sb("gdn_b", 1024, stack=mix_scope)
        nmask = gdn_b[:, 0:1024].rearrange("p (b j t) -> p b j t", b=2, j=4)
        gattn = gdn_b[:, 0:768].rearrange("p (h i t) -> p h i t", h=2, i=3)
        gdn_c = sb("gdn_c", 5 * 512, stack=mix_scope)
        gam, bgam = cut(gdn_c, 0, 4, P), cut(gdn_c, 512, 4, P)
        attn, nmat, t1 = cut(gdn_c, 1024, 4, P), cut(gdn_c, 1536, 4, P), cut(gdn_c, 2048, 4, P)
        gates, gates2 = gdn_c[:, 0:512], gdn_c[:, 512:1024]
        lowrank = gdn_c[:, 1024:1280]
        w2_sb, gb_sb = gdn_c[0:RANK, 1536:2048], gdn_c[0:1, 2048:2560]
        stage = cut(gdn_c, 0, 2, 512)
        gdn_d = sb("gdn_d", 7 * 256 + 3 * 512, stack=mix_scope)
        z0, z1, z0d = cut(gdn_d, 0, 2, P), cut(gdn_d, 256, 2, P), cut(gdn_d, 512, 2, P)
        state, vnew = cut(gdn_d, 768, 2, P), cut(gdn_d, 1024, 2, P)
        qdec, ecum = cut(gdn_d, 1280, 2, P), cut(gdn_d, 1536, 2, P)
        gz, orms, omix = cut(gdn_d, 1792, 2, T), cut(gdn_d, 2304, 2, T), cut(gdn_d, 2816, 2, T)
        vec_in = gdn_d[:, 0:256].rearrange("p (a b) -> p a b", a=2)
        gq_t = sb("gq", 1024, stack=mix_scope)
        gk_t = sb("gk", 1024, stack=mix_scope)
        gv_t = sb("gv", 2048, stack=mix_scope)
        loga_t = sb("loga", 1024, stack=mix_scope)
        gq, gk = cut(gq_t, 0, 2, 2, T), cut(gk_t, 0, 2, 2, T)
        gv = gv_t[:, :].rearrange("p (h b v) -> p h b v", h=4, b=2)
        loga = cut(loga_t, 0, NB, 512)
        tiny = sb("tiny", 12 * 16, stack=mix_scope)
        ab, gdec, beta, ecol, esuf = (cut(tiny, 32 * 0, 2, 16), cut(tiny, 32, 2, 8), cut(tiny, 48, 2, 8),
                                      cut(tiny, 64, 2, 8), cut(tiny, 80, 2, 8))
        bsuf, necol, tmp_a, tmp_b = cut(tiny, 96, 2, 8), cut(tiny, 112, 2, 8), cut(tiny, 128, 2, 8), cut(tiny, 144, 2, 8)
        alog_b, dtb_b, expa = tiny[:, 160:168], tiny[:, 168:176], tiny[:, 176:184]
        mix_scope.close()

        fhi_t = sb("ffhi", FT * T, F32R)
        flo_t = sb("fflo", FT * T, F32R)
        fhi, flo = cut(fhi_t, 0, FT, T), cut(flo_t, 0, FT, T)
        ffn_tmp = sb("ffn_tmp", 3 * 512)
        fgate, fup = ffn_tmp[:, 0:512], ffn_tmp[:, 512:1024]
        fprod = ffn_tmp[:, 1024:1536]
        final_w = sb("final_w", D)
        rb_col = [final_w[:, b * P:(b + 1) * P] for b in range(NB)]

        psd = [ctx.enter_context(nc.psum_tensor(f"psd{i}", [P, 512], F32)) for i in range(2)]
        psm = [ctx.enter_context(nc.psum_tensor(f"psm{i}", [P, 512], F32)) for i in range(6)]
        bank = psd + psm[4:6]

        raw_in = [sem(f"raw_in{i}") for i in range(RING)]
        hi_done, lo_done, unit_used = sem("hi_done"), sem("lo_done"), sem("unit_used")
        x_in = [sem(f"x_in{i}") for i in range(NB)]
        vec_in_sem, gate_in, tiny_in = sem("vec_in"), sem("gate_in"), sem("tiny_in")
        small_zero, pool_seq, consts_ready, cst_ready = sem("small_zero"), sem("pool_seq"), sem("consts_ready"), sem("cst_ready")
        mask_ready = sem("mask_ready")
        ms_done, rstd_done, x_scaled = sem("ms_done"), sem("rstd_done"), sem("x_scaled")
        vec_ps, vec_done = sem("vec_ps"), sem("vec_done")
        hT_ps, hT_staged, hT_hi, hT_lo = sem("hT_ps"), sem("hT_staged"), sem("hT_hi"), sem("hT_lo")
        evicted = sem("evicted")
        ab_ps, logit_ps, ab_done, abs_done = sem("ab_ps"), sem("logit_ps"), sem("ab_done"), sem("abs_done")
        lnexp, loga_done, gdec_step, act_tiny = sem("lnexp"), sem("loga_done"), sem("gdec_step"), sem("act_tiny")
        cum_ps, cum_exp, tiny_done = sem("cum_ps"), sem("cum_exp"), sem("tiny_done")
        pad_zero, conv_step, silu_done, sq_done = sem("pad_zero"), sem("conv_step"), sem("silu_done"), sem("sq_done")
        nsum_ps, ln_done, rn_done, kq_normed = sem("nsum_ps"), sem("ln_done"), sem("rn_done"), sem("kq_normed")
        gu_done, decay_ps, cumb_ps, gam_done, ecum_done = (sem("gu_done"), sem("decay_ps"), sem("cumb_ps"),
                                                           sem("gam_done"), sem("ecum_done"))
        bgam_done, vT_ps, kT_ps, kk_ps, qk_ps = sem("bgam_done"), sem("vT_ps"), sem("kT_ps"), sem("kk_ps"), sem("qk_ps")
        vtok_done, ktok_done, nmat_done, attn_done, qdec_done = (sem("vtok_done"), sem("ktok_done"), sem("nmat_done"),
                                                                 sem("attn_done"), sem("qdec_done"))
        nmask_done, w_done, wT_ps, y_done = sem("nmask_done"), sem("w_done"), sem("wT_ps"), sem("y_done")
        t1_ps, t1_done, wd_ps, yd_ps = sem("t1_ps"), sem("t1_done"), sem("wd_ps"), sem("yd_ps")
        z0_ps, z0_done, z0d_done, s_ps, s_done = sem("z0_ps"), sem("z0_done"), sem("z0d_done"), sem("s_ps"), sem("s_done")
        ks_ps, vnew_done, z1_ps, z1_done = sem("ks_ps"), sem("vnew_done"), sem("z1_ps"), sem("z1_done")
        o_ps, osq_done, osum_ps, oln_done, orms_done, on_done = (sem("o_ps"), sem("osq_done"), sem("osum_ps"),
                                                                 sem("oln_done"), sem("orms_done"), sem("on_done"))
        omix_done, mix_hi, mix_lo = sem("omix_done"), sem("mix_hi"), sem("mix_lo")
        gsum_ps, gexp_done, gkd_done, gqd_done = sem("gsum_ps"), sem("gexp_done"), sem("gkd_done"), sem("gqd_done")
        score_ps, prod_done, gattn_done, cross_done = sem("score_ps"), sem("prod_done"), sem("gattn_done"), sem("cross_done")
        x_again, res_add, ssq_done, ss_done, r_ln, r_done = (sem("x_again"), sem("res_add"), sem("ssq_done"),
                                                             sem("ss_done"), sem("r_ln"), sem("r_done"))
        rcol_done, rb_ps, rb_done = sem("rcol_done"), sem("rb_ps"), sem("rb_done")
        g_scaled, g_silu, u_scaled, f_done, f_hi, f_lo = (sem("g_scaled"), sem("g_silu"), sem("u_scaled"),
                                                          sem("f_done"), sem("f_hi"), sem("f_lo"))
        fw_in, y_ready, stored = sem("fw_in"), sem("y_ready"), sem("stored")

        block = ctx.enter_context(nc.Block())

        def slot(u):
            return u % RING

        def ring(t, u, k):
            s = slot(u) * UNIT
            return t[:, s:s + UNIT].rearrange("p (k c) -> p k c", k=k)

        @block.sync
        def _(sp):
            def load(u, src, n=None):
                n = u if n is None else n
                sp.wait_ge(lo_done, n - RING + 1)
                sp.dma_start(ring(raw, u, src.shape[1]), src).then_inc(raw_in[slot(u)], 16)

            def rows(w, k0, nk, c0, nc_):
                return w[k0 * P:(k0 + nk) * P, bass.ds(c0, nc_)].rearrange("(k p) c -> p k c", p=P)

            for b in range(NB):
                sp.dma_start(resid[:, b, :], x_tok[:, b, :]).then_inc(x_in[b], 16)
            sp.wait_ge(small_zero, 1)
            small = ring(raw, 0, KT)
            sp.dma_start(small[:, :, 0:RANK], rows(w_in, 0, KT, A_LR, RANK)).then_inc(raw_in[0], 16)
            sp.dma_start(small[:, :, 32:48], rows(w_in, 0, KT, B_A, 16)).then_inc(raw_in[0], 16)
            for u in range(1, U_OUT):
                b, q = divmod(u - 1, BLK_UNITS)
                src = rows(w_in, 4 * q, 4, IN_BLOCKS[b], COLS)
                if u < RING:
                    sp.dma_start(ring(raw, u, 4), src).then_inc(raw_in[slot(u)], 16)
                else:
                    load(u, src)
            sp.wait_ge(score_ps, 8)
            for b in range(NB):
                sp.dma_start(resid[:, b, :], x_tok[:, b, :]).then_inc(x_again, 16)
            for u in range(U_OUT, U_GU):
                c, q = divmod(u - U_OUT, OUT_UNITS)
                load(u, rows(w_out, OUT_ORDER[2 * q], 2, 512 * c, 512))
            with sp.Fori(0, PAIRS) as i:
                for q in range(GU_UNITS):
                    w = w_gate if q < BLK_UNITS else w_up
                    load(U_GU + q, rows(w, 4 * (q % BLK_UNITS), 4, i * COLS, COLS), i * GU_UNITS + (U_GU + q))
            sp.dma_start(final_w[:, :], final_norm_w.partition_broadcast(P)).then_inc(fw_in, 16)
            with sp.Fori(0, 2) as cc:
                for u in range(2 * DOWN_UNITS):
                    c, q = divmod(u, DOWN_UNITS)
                    load(U_DOWN + u, rows(w_down, 2 * q, 2, cc * 1024 + 512 * c, 512),
                         cc * (2 * DOWN_UNITS) + (U_DOWN + u))
            for n in range(4):
                sp.wait_ge(y_ready, n + 1)
                b, h = divmod(n, 2)
                sp.dma_start(out_tok[:, b, 1024 * h:1024 * (h + 1)],
                             resid[:, b, 1024 * h:1024 * (h + 1)]).then_inc(stored, 16)
            sp.wait_ge(stored, 64)

        @block.gpsimd
        def _(pool):
            made = [0]

            def then(ins):
                made[0] += 1
                ins.then_inc(pool_seq, 1)
                pool.wait_ge(pool_seq, made[0])

            def keep(view, op, base, pattern, cm, fill=0.0):
                then(nc.gpsimd.affine_select(out=view, in_=view, compare_op=op, fill=fill, base=base,
                                             pattern=pattern, channel_multiplier=cm))

            nc.gpsimd.memset(raw[:, 0:UNIT], 0.0).then_inc(small_zero, 1)
            then(nc.gpsimd.memset(ident[:, :], 0.0))
            keep(ident[:, :], ALU.not_equal, 0, [[-1, P]], 1, 1.0)
            then(nc.gpsimd.memset(cst[:, 0:1], EPS))
            then(nc.gpsimd.memset(cst[:, 1:2], DK * EPS))
            nc.gpsimd.memset(ones[:, :], 1.0).then_inc(cst_ready, 1)
            then(nc.gpsimd.memset(msum[:, :, :], 1.0))
            keep(after, ALU.is_ge, -1, [[-1, P]], 1)
            keep(upto, ALU.is_ge, 0, [[1, P]], -1)
            nc.gpsimd.memset(convin[:, :, 0:TAPS - 1], 0.0).then_inc(consts_ready, 1)
            then(nc.gpsimd.memset(mask[:, :, :], 0.0))
            for lev in range(7):
                b = 1 << lev
                n = P // (2 * b)
                m = mask[:, lev, :].rearrange("p (n o c) -> p n o c", o=2, c=b)[:, :, 1, :]
                then(nc.gpsimd.memset(m, 1.0))
                keep(m, ALU.is_ge, 0, [[-2 * b, n], [0, b]], 1)
                keep(m, ALU.is_ge, b - 1, [[2 * b, n], [0, b]], -1)
            for lev in range(7):
                b = 1 << lev
                n = P // (2 * b)
                v = msum[:, 1 + lev, :].rearrange("p (n o c) -> p n o c", o=2, c=b)
                keep(v[:, :, 0, :], ALU.is_ge, -1, [[-2 * b, n], [-1, b]], 1)
                keep(v[:, :, 0, :], ALU.is_ge, b - 1, [[2 * b, n], [0, b]], -1)
                keep(v[:, :, 1, :], ALU.is_ge, -b, [[-2 * b, n], [0, b]], 1)
                keep(v[:, :, 1, :], ALU.is_ge, b, [[2 * b, n], [1, b]], -1)
            nc.gpsimd.tensor_copy(mask[:, 7, :], ident[:, :]).then_inc(mask_ready, 1)
            for p in range(4):
                pool.wait_ge(nmat_done, p + 1)
                for lev in range(1, 7):
                    n = 6 * p + lev
                    if n > 2:
                        pool.wait_ge(t1_ps, n - 2)
                    nc.gpsimd.tensor_tensor(nmask[:, lev % 2], nmat, mask[:, lev:lev + 1, :].to_broadcast([P, 4, P]),
                                            ALU.mult).then_inc(nmask_done, 1)

        @block.scalar
        def _(act):
            def split_hi(u, n=None):
                n = u if n is None else n
                if isinstance(n, int):
                    act.wait_ge(raw_in[slot(u)], 16 * (n // RING + 1) + (16 if slot(u) == 0 else 0))
                    if n >= RING:
                        act.wait_ge(unit_used, n - RING + 1)
                nc.scalar.activation(whi[:, slot(u) * UNIT:(slot(u) + 1) * UNIT],
                                     raw[:, slot(u) * UNIT:(slot(u) + 1) * UNIT], ACT.Copy).then_inc(hi_done, 1)

            def split_hi_at(u, rounds, units):
                act.wait_ge(raw_in[slot(u)], rounds * 16 + (16 * (u // RING + 1) + (16 if slot(u) == 0 else 0)))
                act.wait_ge(unit_used, units + (u - RING + 1))
                split_hi(u, units)

            def lnexp_tables():
                nc.scalar.preload_act_table_set("natural_log_exp_and_others")

            def copy(o, i, **kw):
                return nc.scalar.activation(o, i, ACT.Copy, **kw)

            def rsqrt(o, i, tmp, scale, bias, ln_sem, n, done):
                nc.scalar.activation(tmp, i, ACT.Ln, bias=bias, scale=scale).then_inc(ln_sem, 1)
                act.wait_ge(ln_sem, n)
                nc.scalar.activation(o, tmp, ACT.Exp, scale=-0.5).then_inc(done, 1)

            act.dma_start(vec_in[0:96, 0, :], gdn_conv_w.rearrange("j (t p) -> (j t) p", p=P)).then_inc(vec_in_sem, 16)
            act.dma_start(vec_in[96:112, 0, :], attn_norm_w.rearrange("(t p) -> t p", p=P)).then_inc(vec_in_sem, 16)
            act.dma_start(vec_in[112:128, 0, :], ffn_norm_w.rearrange("(t p) -> t p", p=P)).then_inc(vec_in_sem, 16)
            act.dma_start(vec_in[0:2, 1, :], gla_norm_w.rearrange("(t p) -> t p", p=P)).then_inc(vec_in_sem, 16)
            act.dma_start(vec_in[2:3, 1, :], gdn_norm_w.rearrange("(t p) -> t p", p=P)).then_inc(vec_in_sem, 16)
            act.dma_start(w2_sb, gla_gate_w2).then_inc(gate_in, 16)
            act.dma_start(gb_sb, gla_gate_b.rearrange("(a n) -> a n", a=1)).then_inc(gate_in, 16)
            act.dma_start(alog_b, gdn_a_log.partition_broadcast(P)).then_inc(tiny_in, 16)
            act.dma_start(dtb_b, gdn_dt_bias.partition_broadcast(P)).then_inc(tiny_in, 16)
            lnexp_tables()
            act.wait_ge(x_in[0], 16)
            nc.scalar.activation(gv_t[:, 0:2048], resid[:, 0, :], ACT.Square, accum_out=stat[:, 0:1]).then_inc(ms_done, 1)
            act.wait_ge(ms_done, 1)
            act.wait_ge(cst_ready, 1)
            nc.scalar.activation(stat[:, 2:3], stat[:, 0:1], ACT.Ln, bias=eps_c, scale=1.0 / D).then_inc(ms_done, 1)
            act.wait_ge(ms_done, 2)
            nc.scalar.activation(stat[:, 4:5], stat[:, 2:3], ACT.Exp, scale=-0.5).then_inc(rstd_done, 1)
            act.wait_ge(x_in[1], 16)
            nc.scalar.activation(gv_t[:, 0:2048], resid[:, 1, :], ACT.Square, accum_out=stat[:, 1:2]).then_inc(ms_done, 1)
            act.wait_ge(ms_done, 3)
            nc.scalar.activation(stat[:, 3:4], stat[:, 1:2], ACT.Ln, bias=eps_c, scale=1.0 / D).then_inc(ms_done, 1)
            act.wait_ge(ms_done, 4)
            nc.scalar.activation(stat[:, 5:6], stat[:, 3:4], ACT.Exp, scale=-0.5).then_inc(rstd_done, 1)
            act.wait_ge(vec_ps, 1)
            copy(vec_t[:, 0:128], psd[0][:, 0:128]).then_inc(vec_done, 1)
            copy(vec_t[:, 128:131], psd[0][:, 128:131]).then_inc(vec_done, 1)
            act.wait_ge(vec_done, 2)

            def stage_hT(n, w, first):
                act.wait_ge(hT_ps, n + 1)
                if n >= 2:
                    act.wait_ge(hT_lo, n - 1)
                for k in range(2):
                    kt = 2 * (n % 8) + k
                    copy(stage[:, n % 2, k * T:(k + 1) * T], first[:, k * T:(k + 1) * T],
                         scale=w[:, kt:kt + 1]).then_inc(hT_staged, 1)

            for n in range(8):
                if n in (3, 5, 7):
                    split_hi(n // 2 - 1)
                stage_hT(n, attn_w, psm[n % 6])

            def evict(b):
                act.wait_ge(unit_used, 1 + BLK_UNITS * (b + 1))
                ps = psd[b % 2]
                two = ps[:, :].rearrange("p (h t) -> p h t", h=2)
                if b < 0:
                    copy(lowrank[0:64, :], ps[0:64, 0:T]).then_inc(evicted, 1)
                elif b < 16 and b % 4 < 3:
                    p, j = divmod(b, 4)
                    if p:
                        act.wait_ge(conv_step, 24 * (p - 1) + 8 * (j + 1))
                    copy(convin[:, 2 * j:2 * j + 2, TAPS - 1:], two).then_inc(evicted, 1)
                elif b < 16:
                    if b // 4:
                        act.wait_ge(omix_done, b // 4)
                    nc.scalar.activation(gz, two, ACT.Silu).then_inc(evicted, 1)
                elif b < 24:
                    g, j = divmod(b - 16, 4)
                    if j == 0:
                        copy(gq[:, g], two, scale=DK ** -0.5).then_inc(evicted, 1)
                    elif j == 1:
                        copy(gk[:, g], two).then_inc(evicted, 1)
                    else:
                        copy(gv[:, 2 * g + j - 2], two).then_inc(evicted, 1)
                else:
                    act.wait_ge(omix_done, 4 + b - 24)
                    nc.scalar.activation(gz, two, ACT.Silu).then_inc(evicted, 1)

            def setup(s):
                if s == 3:
                    lnexp_tables()
                    act.wait_ge(tiny_in, 32)
                    nc.scalar.activation(expa, alog_b, ACT.Exp).then_inc(act_tiny, 1)
                    act.wait_ge(ab_done, 2)
                    nc.scalar.activation(tmp_a, ab[:, :, 0:8], ACT.Abs).then_inc(act_tiny, 1)
                    act.wait_ge(act_tiny, 2)
                    nc.scalar.activation(tmp_a, tmp_a, ACT.Exp, scale=-1.0).then_inc(act_tiny, 1)
                    nc.scalar.activation(tmp_b, ab[:, :, 8:16], ACT.Exp, scale=-1.0).then_inc(act_tiny, 1)
                    act.wait_ge(act_tiny, 4)
                    nc.scalar.activation(tmp_a, tmp_a, ACT.Ln, bias=ones[:, 0:1]).then_inc(act_tiny, 1)
                if s in (4, 5):
                    b = s - 4
                    act.wait_ge(logit_ps, b + 1)
                    if b:
                        act.wait_ge(loga_done, b)
                    nc.scalar.activation(gates, psm[1 + b][:, :], ACT.Abs).then_inc(lnexp, 1)
                    act.wait_ge(lnexp, 3 * b + 1)
                    nc.scalar.activation(gates2, gates, ACT.Exp, scale=-1.0).then_inc(lnexp, 1)
                    act.wait_ge(lnexp, 3 * b + 2)
                    nc.scalar.activation(gates, gates2, ACT.Ln, bias=ones[:, 0:1]).then_inc(lnexp, 1)
                if s == 7:
                    act.wait_ge(cum_ps, 1)
                    nc.scalar.activation(tiny[:, 64:96], psm[3][:, 0:32], ACT.Exp).then_inc(cum_exp, 1)

            def silu(p, s):
                j = s - 26
                act.wait_ge(conv_step, 24 * p + 8 * (j + 1))
                if p:
                    act.wait_ge(ks_ps, p)
                nc.scalar.activation(kqv[:, 2 * j:2 * j + 2, :], convd[:, 2 * j:2 * j + 2, :], ACT.Silu).then_inc(silu_done, 1)

            def out_norm(n, ps, sum_ps, width, dv, s, s0):
                if s == s0:
                    act.wait_ge(o_ps, n + 1)
                    if n:
                        act.wait_ge(on_done, n)
                    nc.scalar.activation(orms, ps, ACT.Square).then_inc(osq_done, 1)
                if s == s0 + 1:
                    act.wait_ge(osum_ps, n + 1)
                    o = orms.rearrange("p a t -> p (a t)")[:, 0:width]
                    rsqrt(o, sum_ps, o, 1.0 / dv, eps_c, oln_done, n + 1, orms_done)

            def gdn(p, s):
                n = p + 1
                if s == 1:
                    lnexp_tables()
                    act.wait_ge(nsum_ps, 2 * p + 1)
                    rsqrt(sumsq[:, 0:2], psm[0][:, :].rearrange("p (h t) -> p h t", h=2), sumsq[:, 0:2], 1.0, eps_c,
                          ln_done, 2 * p + 1, rn_done)
                    act.wait_ge(nsum_ps, 2 * p + 2)
                    rsqrt(sumsq[:, 2:4], psm[1][:, :].rearrange("p (h t) -> p h t", h=2), sumsq[:, 2:4], float(DK),
                          dk_eps_c, ln_done, 2 * p + 2, rn_done)
                if s == 2:
                    act.wait_ge(decay_ps, n)
                    act.wait_ge(cumb_ps, n)
                    nc.scalar.activation(gam, psm[4][:, :].rearrange("p (j t) -> p j t", j=4), ACT.Exp).then_inc(gam_done, 1)
                    nc.scalar.activation(ecum, psm[5][:, 0:T].rearrange("p (h t) -> p h t", h=2), ACT.Exp).then_inc(ecum_done, 1)
                if s == 3:
                    act.wait_ge(vT_ps, n)
                    copy(vtok, psm[2][:, :].rearrange("p (j t) -> p j t", j=4)).then_inc(vtok_done, 1)
                    act.wait_ge(kT_ps, n)
                    copy(ktok, psm[3][:, :].rearrange("p (j t) -> p j t", j=4)).then_inc(ktok_done, 1)
                if s == 5:
                    act.wait_ge(wT_ps, n)
                    copy(ylow, psm[2][:, :].rearrange("p (j t) -> p j t", j=4)).then_inc(y_done, 1)
                if 6 <= s < 18 and s % 2 == 0:
                    lev = (s - 4) // 2
                    act.wait_ge(t1_ps, 6 * p + lev)
                    copy(t1, psm[3][:, :].rearrange("p (j t) -> p j t", j=4)).then_inc(t1_done, 1)
                if s == 18:
                    act.wait_ge(z0_ps, n)
                    copy(z0, psm[0][:, 0:T].rearrange("p (h t) -> p h t", h=2)).then_inc(z0_done, 1)
                if s == 19:
                    act.wait_ge(s_ps, n)
                    copy(state, psm[1][:, 0:T].rearrange("p (h t) -> p h t", h=2)).then_inc(s_done, 1)
                if s == 21:
                    act.wait_ge(z1_ps, n)
                    copy(z1, psm[3][:, 0:T].rearrange("p (h t) -> p h t", h=2)).then_inc(z1_done, 1)
                out_norm(p, psm[4][:, :].rearrange("p (h t) -> p h t", h=2), psm[5][:, :], 512, DK, s, 22)
                if s == 24:
                    act.wait_ge(omix_done, n)
                    copy(mhi[:, 8 + 2 * p:10 + 2 * p, :], omix).then_inc(mix_hi, 1)

            def gla(g, s):
                for hb in range(4):
                    h, b = divmod(hb, 2)
                    head, n = 2 * g + h, 4 * g + hb
                    s0 = 1 + 6 * hb
                    if s == s0:
                        if hb == 0:
                            lnexp_tables()
                        for k in range(2):
                            act.wait_ge(gsum_ps, 2 * n + k + 1)
                            if n and k == 0:
                                act.wait_ge(gkd_done, n)
                                act.wait_ge(gqd_done, n)
                            nc.scalar.activation(gexp[:, 4 * k:4 * k + 4, :], psm[k][:, :].rearrange("p (l t) -> p l t", l=4),
                                                 ACT.Exp, scale=1.0 / TAU).then_inc(gexp_done, 1)
                    if s == s0 + 4 and b:
                        act.wait_ge(score_ps, n + 1)
                        copy(gattn[:, h, 1, :], psm[4][:, 0:P]).then_inc(cross_done, 1)
                    if b:
                        out_norm(4 + head, psm[5][:, :].rearrange("p (a t) -> p a t", a=2), psm[4][:, T:2 * T], T, 2 * DK,
                                 s, s0 + 6)

            def gate_hi(head):
                act.wait_ge(omix_done, 5 + head)
                copy(mhi[:, 2 * head:2 * head + 2, :], omix).then_inc(mix_hi, 1)

            for ph in range(7):
                for s in range(PHASE_STEPS):
                    u = 1 + 16 * ph + s // 2
                    if s % 2 == 0:
                        split_hi(u + AHEAD)
                        if s % 8 == 0:
                            evict(4 * ph + s // 8 - 1)
                    if ph == 0:
                        setup(s)
                    if ph < 4 and 26 <= s < 29:
                        silu(ph, s)
                    if 1 <= ph <= 4:
                        gdn(ph - 1, s)
                    if ph >= 5:
                        gla(ph - 5, s)
                    if ph == 6 and s in (10, 18, 26):
                        gate_hi(s // 8 - 1)

            evict(27)
            lnexp_tables()

            def chunk_tail(c):
                for b in range(NB):
                    act.wait_ge(res_add, 2 * c + b + 1)
                    if 2 * c + b:
                        act.wait_ge(ssq_done, 2 * c + b)
                    nc.scalar.activation(gz.rearrange("p a t -> p (a t)"), resid[:, b, 512 * c:512 * (c + 1)], ACT.Square,
                                         accum_out=stat[:, 8 + 4 * b + c:9 + 4 * b + c]).then_inc(ssq_done, 1)

            for c in range(4):
                for q in range(OUT_UNITS):
                    split_hi(U_OUT + OUT_UNITS * c + q + AHEAD)
                    if c == 0 and q == 1:
                        gate_hi(3)
                    if c and q == 2:
                        chunk_tail(c - 1)
                    if c and q == 3:
                        for n in range(2):
                            stage_hT(8 + 2 * (c - 1) + n, ffn_w, psm[2 * ((c - 1) % 2) + n])

            def gate_silu(n):
                act.wait_ge(g_scaled, n)
                nc.scalar.activation(fgate, fgate, ACT.Silu).then_inc(g_silu, 1)

            split_hi(U_GU + 2)
            chunk_tail(3)
            for n in range(2):
                stage_hT(14 + n, ffn_w, psm[2 + n])
            act.wait_ge(ss_done, 1)
            nc.scalar.activation(stat[:, 18:20], stat[:, 16:18], ACT.Ln, bias=eps_c, scale=1.0 / D).then_inc(r_ln, 1)
            act.wait_ge(r_ln, 1)
            nc.scalar.activation(stat[:, 20:22], stat[:, 18:20], ACT.Exp, scale=-0.5).then_inc(r_done, 1)
            split_hi(U_GU + 3)
            split_hi(U_GU + 4)
            act.wait_ge(rb_ps, 1)
            copy(rb[:, :], psm[0][:, 0:T]).then_inc(rb_done, 1)
            for q in range(3, GU_UNITS):
                split_hi(U_GU + q + AHEAD)
                if q == 4:
                    gate_silu(1)
            act.wait_ge(f_done, 1)
            copy(fhi[:, 0:2, :], fprod.rearrange("p (a t) -> p a t", a=2)).then_inc(f_hi, 1)
            with act.Fori(1, PAIRS) as i:
                for q in range(GU_UNITS):
                    split_hi_at(U_GU + q + AHEAD, i * (GU_UNITS // RING), i * GU_UNITS)
                    if q == 4:
                        gate_silu(i + 1)
                act.wait_ge(f_done, i + 1)
                copy(fhi_t[:, bass.ds(i * 512, 512)], fprod).then_inc(f_hi, 1)

            lnexp_tables()

            def down_tail(c):
                for b in range(NB):
                    act.wait_ge(res_add, 8 + 2 * c + b + 1)
                    act.wait_ge(ssq_done, 8 + 2 * c + b)
                    nc.scalar.activation(fgate, resid[:, b, 512 * c:512 * (c + 1)], ACT.Square,
                                         accum_out=stat[:, 8 + 4 * b + c:9 + 4 * b + c]).then_inc(ssq_done, 1)

            for c in range(4):
                for q in range(DOWN_UNITS):
                    u = U_DOWN + DOWN_UNITS * c + q + AHEAD
                    if u < U_END:
                        split_hi(u)
                down_tail(c)
            act.wait_ge(ss_done, 2)
            nc.scalar.activation(stat[:, 18:20], stat[:, 16:18], ACT.Ln, bias=eps_c, scale=1.0 / D).then_inc(r_ln, 1)
            act.wait_ge(r_ln, 2)
            nc.scalar.activation(stat[:, 20:22], stat[:, 18:20], ACT.Exp, scale=-0.5).then_inc(r_done, 1)

        @block.vector
        def _(dve):
            def split_lo(u, n=None):
                n = u if n is None else n
                dve.wait_ge(hi_done, n + 1)
                at = slice(slot(u) * UNIT, (slot(u) + 1) * UNIT)
                nc.vector.tensor_tensor(wlo[:, at], raw[:, at], whi[:, at].bitcast(F32), ALU.subtract).then_inc(lo_done, 1)

            for b in range(NB):
                dve.wait_ge(rstd_done, b + 1)
                nc.vector.tensor_scalar(resid[:, b, :], resid[:, b, :], stat[:, 4 + b:5 + b], None, ALU.mult)\
                    .then_inc(x_scaled, 1)

            def split_hT(n):
                k = 2 * (n % 8)
                s = stage[:, n % 2, :].rearrange("p (k t) -> p k t", k=2)
                dve.wait_ge(hT_staged, 2 * n + 2)
                nc.vector.tensor_copy(hhi[:, k:k + 2, :], s).then_inc(hT_hi, 1)
                dve.wait_ge(hT_hi, n + 1)
                nc.vector.tensor_tensor(hlo[:, k:k + 2, :], s, hhi[:, k:k + 2, :].bitcast(F32), ALU.subtract).then_inc(hT_lo, 1)

            for n in range(8):
                if n in (4, 6):
                    split_lo(n // 2 - 2)
                split_hT(n)
            split_lo(2)

            def setup(s):
                if s == 2:
                    dve.wait_ge(ab_ps, 1)
                    nc.vector.tensor_copy(ab, psm[0][:, 0:32].rearrange("p (b c) -> p b c", b=2)).then_inc(ab_done, 1)
                    dve.wait_ge(ab_done, 1)
                    dve.wait_ge(tiny_in, 32)
                    for b in range(NB):
                        ins = nc.vector.tensor_tensor(ab[:, b, 0:8], ab[:, b, 0:8], dtb_b, ALU.add)
                        if b:
                            ins.then_inc(ab_done, 1)
                if s in (4, 5):
                    b = s - 4
                    dve.wait_ge(lnexp, 3 * b + 3)
                    nc.vector.scalar_tensor_tensor(out=loga[:, b, :], in0=psm[1 + b][:, :], scalar=0.0, in1=gates,
                                                   op0=ALU.min, op1=ALU.subtract).then_inc(loga_done, 1)
                if s == 4:
                    dve.wait_ge(act_tiny, 5)
                    nc.vector.scalar_tensor_tensor(out=tmp_a, in0=ab[:, :, 0:8], scalar=0.0, in1=tmp_a,
                                                   op0=ALU.max, op1=ALU.add).then_inc(gdec_step, 1)
                    nc.vector.tensor_scalar(tmp_b, tmp_b, 1.0, None, ALU.add).then_inc(gdec_step, 1)
                    dve.wait_ge(gdec_step, 2)
                    for b in range(NB):
                        nc.vector.scalar_tensor_tensor(out=gdec[:, b, :], in0=tmp_a[:, b, :], scalar=-1.0, in1=expa,
                                                       op0=ALU.mult, op1=ALU.mult).then_inc(gdec_step, 1)
                    nc.vector.reciprocal(beta, tmp_b).then_inc(gdec_step, 1)
                if s == 7:
                    dve.wait_ge(cum_exp, 1)
                    dve.wait_ge(gdec_step, 5)
                    nc.vector.tensor_tensor(bsuf, beta, esuf, ALU.mult).then_inc(tiny_done, 1)
                    nc.vector.tensor_scalar(necol, ecol, -1.0, None, ALU.mult).then_inc(tiny_done, 1)

            def conv(p, j):
                dve.wait_ge(evicted, 4 * p + j + 2)
                if p == 0 and j == 0:
                    dve.wait_ge(consts_ready, 1)
                    dve.wait_ge(vec_done, 2)
                if p:
                    dve.wait_ge(silu_done, 3 * (p - 1) + j + 1)
                tile0 = {0: 8, 1: 0, 2: 16}[j] + 2 * p
                for tap in range(TAPS):
                    for h in range(2):
                        c = 24 * tap + tile0 + h
                        src = convin[:, 2 * j + h, tap:tap + T]
                        dst = convd[:, 2 * j + h, :]
                        if tap == 0:
                            ins = nc.vector.tensor_scalar(dst, src, conv_w[:, c:c + 1], None, ALU.mult)
                        else:
                            dve.wait_ge(conv_step, 24 * p + 8 * j + 2 * tap - 1 + h)
                            ins = nc.vector.scalar_tensor_tensor(out=dst, in0=src, scalar=conv_w[:, c:c + 1], in1=dst,
                                                                 op0=ALU.mult, op1=ALU.add)
                        ins.then_inc(conv_step, 1)

            def square(p, j):
                dve.wait_ge(silu_done, 3 * p + j + 1)
                if p:
                    dve.wait_ge(kq_normed, 2 * p)
                nc.vector.tensor_tensor(sumsq[:, 2 * j:2 * j + 2], kqv[:, 2 * j:2 * j + 2], kqv[:, 2 * j:2 * j + 2],
                                        ALU.mult).then_inc(sq_done, 1)

            def decays(p):
                if p == 0:
                    dve.wait_ge(gdec_step, 5)
                    dve.wait_ge(consts_ready, 1)
                if p:
                    dve.wait_ge(bgam_done, 4 * p)
                for j in range(4):
                    h, b = divmod(j, 2)
                    nc.vector.tensor_scalar(gam[:, j, :], upto, gdec[:, b, 2 * p + h:2 * p + h + 1], None, ALU.mult)\
                        .then_inc(gu_done, 1)

            def gdn(p, s):
                n = p + 1
                if s in (1, 2):
                    j = s - 1
                    dve.wait_ge(rn_done, 2 * p + j + 1)
                    nc.vector.tensor_tensor(kqv[:, 2 * j:2 * j + 2], kqv[:, 2 * j:2 * j + 2], sumsq[:, 2 * j:2 * j + 2],
                                            ALU.mult).then_inc(kq_normed, 1)
                if s == 2:
                    dve.wait_ge(gam_done, n)
                    for j in range(4):
                        h, b = divmod(j, 2)
                        nc.vector.scalar_tensor_tensor(out=bgam[:, j, :], in0=gam[:, j, :],
                                                       scalar=beta[:, b, 2 * p + h:2 * p + h + 1], in1=upto,
                                                       op0=ALU.mult, op1=ALU.mult).then_inc(bgam_done, 1)
                if s == 3:
                    dve.wait_ge(bgam_done, 4 * n)
                    dve.wait_ge(kk_ps, n)
                    nc.vector.tensor_tensor(nmat, psm[0][:, :].rearrange("p (j t) -> p j t", j=4), bgam, ALU.mult)\
                        .then_inc(nmat_done, 1)
                    dve.wait_ge(nmat_done, n)
                    if p == 0:
                        dve.wait_ge(mask_ready, 1)
                    nc.vector.tensor_tensor(wup, nmat, mask[:, 0:1, :].to_broadcast([P, 4, P]), ALU.mult).then_inc(w_done, 1)
                    dve.wait_ge(w_done, 8 * p + 1)
                    nc.vector.tensor_tensor(wup, ident[:, :].unsqueeze(1).to_broadcast([P, 4, P]), wup, ALU.subtract)\
                        .then_inc(w_done, 1)
                if s == 4:
                    dve.wait_ge(qk_ps, n)
                    nc.vector.tensor_tensor(attn, psm[1][:, :].rearrange("p (j t) -> p j t", j=4), bgam, ALU.mult)\
                        .then_inc(attn_done, 1)
                    dve.wait_ge(ecum_done, n)
                    dve.wait_ge(kq_normed, 2 * n)
                    nc.vector.tensor_tensor(qdec, kqv[:, 2:4, P:T], ecum, ALU.mult).then_inc(qdec_done, 1)
                if 6 <= s < 18 and s % 2:
                    lev = (s - 5) // 2
                    if lev < 6:
                        dve.wait_ge(yd_ps, 5 * p + lev)
                        nc.vector.tensor_tensor(ylow, ylow, psm[5][:, :].rearrange("p (j t) -> p j t", j=4), ALU.subtract)\
                            .then_inc(y_done, 1)
                    dve.wait_ge(wd_ps, 6 * p + lev)
                    nc.vector.tensor_tensor(wup, wup, psm[4][:, :].rearrange("p (j t) -> p j t", j=4), ALU.subtract)\
                        .then_inc(w_done, 1)
                if s == 18:
                    dve.wait_ge(z0_done, n)
                    if p == 0:
                        dve.wait_ge(tiny_done, 2)
                    for h in range(2):
                        nc.vector.tensor_scalar(z0d[:, h, :], z0[:, h, :], bsuf[:, 0, 2 * p + h:2 * p + h + 1], None,
                                                ALU.mult).then_inc(z0d_done, 1)
                if s == 20:
                    dve.wait_ge(ks_ps, n)
                    for h in range(2):
                        nc.vector.scalar_tensor_tensor(out=vnew[:, h, :], in0=psm[2][:, h * P:(h + 1) * P],
                                                       scalar=necol[:, 1, 2 * p + h:2 * p + h + 1], in1=vtok[:, 2 * h + 1, :],
                                                       op0=ALU.mult, op1=ALU.add).then_inc(vnew_done, 1)
                if s == 23:
                    dve.wait_ge(orms_done, n)
                    if p:
                        dve.wait_ge(mix_lo, p)
                    nc.vector.tensor_tensor(omix, psm[4][:, :].rearrange("p (h t) -> p h t", h=2), orms, ALU.mult)\
                        .then_inc(on_done, 1)
                if s == 24:
                    dve.wait_ge(on_done, n)
                    dve.wait_ge(evicted, 4 * p + 5)
                    nc.vector.scalar_tensor_tensor(out=omix, in0=omix, scalar=gdn_w, in1=gz, op0=ALU.mult, op1=ALU.mult)\
                        .then_inc(omix_done, 1)
                if s == 25:
                    dve.wait_ge(mix_hi, n)
                    k = slice(8 + 2 * p, 10 + 2 * p)
                    nc.vector.tensor_tensor(mlo[:, k, :], omix, mhi[:, k, :].bitcast(F32), ALU.subtract).then_inc(mix_lo, 1)

            def gla(g, s):
                for hb in range(4):
                    h, b = divmod(hb, 2)
                    head, n = 2 * g + h, 4 * g + hb
                    s0 = 1 + 6 * hb
                    if s == s0 + 1:
                        dve.wait_ge(gexp_done, 2 * n + 2)
                        if n >= 2:
                            dve.wait_ge(score_ps, n - 1 + (1 if b == 0 else 0))
                        nc.vector.tensor_tensor(gkd[:, b], gexp, gk[:, g, h:h + 1, b * P:(b + 1) * P].to_broadcast([P, 8, P]),
                                                ALU.mult).then_inc(gkd_done, 1)
                        nc.vector.tensor_tensor(gqd[:, b], gexp, gq[:, g, h:h + 1, b * P:(b + 1) * P].to_broadcast([P, 8, P]),
                                                ALU.mult).then_inc(gqd_done, 1)
                    if s == s0 + 4:
                        dve.wait_ge(score_ps, n + 1)
                        if n:
                            dve.wait_ge(gattn_done, n)
                        for k in range(2):
                            nc.vector.tensor_tensor(gprod[:, 4 * k:4 * k + 4], psm[2 + k][:, :].rearrange("p (l t) -> p l t", l=4),
                                                    mask[:, 4 * k:4 * k + 4], ALU.mult).then_inc(prod_done, 1)
                        dve.wait_ge(prod_done, 2 * n + 2)
                        if head >= 1:
                            dve.wait_ge(o_ps, 4 + max(0, head - 1))
                        nc.vector.tensor_reduce(gattn[:, h, 2 * b, :], gprod.rearrange("p l t -> p t l"), AX_X, ALU.add)\
                            .then_inc(gattn_done, 1)
                    if s == s0 + 8 and b:
                        dve.wait_ge(orms_done, 5 + head)
                        o = orms.rearrange("p a t -> p (a t)")[:, 0:T]
                        for a in range(2):
                            ins = nc.vector.scalar_tensor_tensor(out=gon[:, head, a * T:(a + 1) * T], in0=psm[5][:, a * T:(a + 1) * T],
                                                                 scalar=gla_w[:, a:a + 1], in1=o, op0=ALU.mult, op1=ALU.mult)
                            if a:
                                ins.then_inc(on_done, 1)

            def gate(head, part):
                if part == 0:
                    dve.wait_ge(evicted, 24 + head + 2)
                    dve.wait_ge(on_done, 5 + head)
                    dve.wait_ge(mix_lo, 4 + head)
                    nc.vector.tensor_tensor(omix, gon[:, head, :].rearrange("p (a t) -> p a t", a=2), gz, ALU.mult)\
                        .then_inc(omix_done, 1)
                else:
                    dve.wait_ge(mix_hi, 5 + head)
                    k = slice(2 * head, 2 * head + 2)
                    nc.vector.tensor_tensor(mlo[:, k, :], omix, mhi[:, k, :].bitcast(F32), ALU.subtract).then_inc(mix_lo, 1)

            for ph in range(7):
                for s in range(PHASE_STEPS):
                    u = 1 + 16 * ph + s // 2
                    if s % 2 == 0:
                        split_lo(u + AHEAD)
                    if ph == 0:
                        setup(s)
                    if ph < 4 and s in (8, 16, 24):
                        conv(ph, s // 8 - 1)
                    if ph < 4 and s in (27, 28):
                        square(ph, s - 27)
                    if ph < 4 and s == 30:
                        decays(ph)
                    if 1 <= ph <= 4:
                        gdn(ph - 1, s)
                    if ph >= 5:
                        gla(ph - 5, s)
                    if ph == 6 and s in (9, 17, 25):
                        gate(s // 8 - 1, 0)
                    if ph == 6 and s in (11, 19, 27):
                        gate(s // 8 - 1, 1)

            def add_chunk(c, first_bank, units):
                dve.wait_ge(unit_used, units)
                for b in range(NB):
                    ps = bank[first_bank + b]
                    nc.vector.tensor_tensor(resid[:, b, 512 * c:512 * (c + 1)], resid[:, b, 512 * c:512 * (c + 1)],
                                            ps[:, :], ALU.add).then_inc(res_add, 1)

            for c in range(4):
                for q in range(OUT_UNITS):
                    split_lo(U_OUT + OUT_UNITS * c + q + AHEAD)
                    if c == 0 and q == 0:
                        gate(3, 0)
                    if c == 0 and q == 1:
                        gate(3, 1)
                        dve.wait_ge(x_again, 32)
                    if c and q == 0:
                        add_chunk(c - 1, 2 * ((c - 1) % 2), U_OUT + OUT_UNITS * c)
                    if c and q == 3:
                        for n in range(2):
                            split_hT(8 + 2 * (c - 1) + n)

            def rms_total():
                nc.vector.tensor_reduce(stat[:, 16:18], stat[:, 8:16].rearrange("p (b c) -> p b c", b=2), AX_X, ALU.add)\
                    .then_inc(ss_done, 1)

            def gate_scale(n):
                two = fgate.rearrange("p (a t) -> p a t", a=2)
                nc.vector.tensor_tensor(two, psd[0][:, :].rearrange("p (a t) -> p a t", a=2),
                                        rb[:, :].unsqueeze(1).to_broadcast([P, 2, T]), ALU.mult).then_inc(g_scaled, 1)

            def up_and_product(n, lo_out, hi_in):
                dve.wait_ge(unit_used, n * GU_UNITS + (U_GU + GU_UNITS))
                nc.vector.tensor_tensor(fup.rearrange("p (a t) -> p a t", a=2), psd[1][:, :].rearrange("p (a t) -> p a t", a=2),
                                        rb[:, :].unsqueeze(1).to_broadcast([P, 2, T]), ALU.mult).then_inc(u_scaled, 1)
                dve.wait_ge(u_scaled, n + 1)
                dve.wait_ge(g_silu, n + 1)
                nc.vector.tensor_tensor(fprod, fup, fgate, ALU.mult).then_inc(f_done, 1)
                dve.wait_ge(f_hi, n + 1)
                nc.vector.tensor_tensor(lo_out, fprod, hi_in, ALU.subtract).then_inc(f_lo, 1)

            split_lo(U_GU + 2)
            add_chunk(3, 2, U_GU)
            for n in range(2):
                split_hT(14 + n)
            dve.wait_ge(ssq_done, 8)
            rms_total()
            dve.wait_ge(r_done, 1)
            for b in range(NB):
                nc.vector.tensor_scalar(rb_col[b], ones[:, :], stat[:, 20 + b:21 + b], None, ALU.mult).then_inc(rcol_done, 1)
            for q in range(1, GU_UNITS):
                split_lo(U_GU + q + AHEAD)
                if q == 4:
                    dve.wait_ge(unit_used, U_GU + BLK_UNITS)
                    dve.wait_ge(rb_done, 1)
                    gate_scale(0)
            up_and_product(0, flo_t[:, 0:512], fhi_t[:, 0:512].bitcast(F32))
            with dve.Fori(1, PAIRS) as i:
                for q in range(GU_UNITS):
                    split_lo(U_GU + q + AHEAD, i * GU_UNITS + (U_GU + q + AHEAD))
                    if q == 4:
                        dve.wait_ge(unit_used, i * GU_UNITS + (U_GU + BLK_UNITS))
                        gate_scale(i)
                up_and_product(i, flo_t[:, bass.ds(i * 512, 512)], fhi_t[:, bass.ds(i * 512, 512)].bitcast(F32))

            for c in range(4):
                for q in range(DOWN_UNITS):
                    u = U_DOWN + DOWN_UNITS * c + q + AHEAD
                    if u < U_END:
                        split_lo(u)
                add_chunk(c, 2 - 2 * (c % 2), U_DOWN + DOWN_UNITS * (c + 1))
            dve.wait_ge(ssq_done, 16)
            rms_total()
            dve.wait_ge(r_done, 2)
            dve.wait_ge(fw_in, 16)
            for n in range(4):
                b, h = divmod(n, 2)
                v = resid[:, b, 1024 * h:1024 * (h + 1)]
                nc.vector.scalar_tensor_tensor(out=v, in0=v, scalar=stat[:, 20 + b:21 + b],
                                               in1=final_w[:, 1024 * h:1024 * (h + 1)], op0=ALU.mult, op1=ALU.mult)\
                    .then_inc(y_ready, 1)

        @block.tensor
        def _(pe):
            def mm(o, w, m, start=True, stop=True):
                return nc.tensor.matmul(o, w, m, start=start, stop=stop, skip_group_check=True)

            def three(o, wh, wl, xh, xl, start, stop):
                mm(o, wh, xh, start, False)
                mm(o, wh, xl, False, False)
                return mm(o, wl, xh, False, stop)

            pe.wait_ge(cst_ready, 1)
            pe.wait_ge(vec_in_sem, 80)
            nc.tensor.transpose(psd[0][:, 0:128], vec_in[:, 0, :], ident[:, :])
            nc.tensor.transpose(psd[0][:, 128:131], vec_in[0:3, 1, :], ident[0:3, 0:3]).then_inc(vec_ps, 1)

            def turn(n, ps):
                for k in range(2):
                    kt = 2 * (n % 8) + k
                    for b in range(NB):
                        ins = nc.tensor.transpose(ps[:, k * T + b * P:k * T + (b + 1) * P],
                                                  resid[:, b, kt * P:(kt + 1) * P], ident[:, :])
                ins.then_inc(hT_ps, 1)

            pe.wait_ge(x_scaled, 2)
            for n in range(8):
                if n >= 6:
                    pe.wait_ge(hT_staged, 2 * (n - 6) + 2)
                turn(n, psm[n % 6])

            pe.wait_ge(lo_done, 1)
            for k in range(KT):
                if k % 2 == 0:
                    pe.wait_ge(hT_lo, k // 2 + 1)
                ins = three(psd[1][0:64, 0:T], ring(whi, 0, KT)[:, k, :], ring(wlo, 0, KT)[:, k, :], hhi[:, k, :],
                            hlo[:, k, :], k == 0, k == KT - 1)
            ins.then_inc(unit_used, 1)

            def dense(ps, u, k0, half, tokens_on_partitions=False, signal=True):
                wh, wl = ring(whi, u, 4), ring(wlo, u, 4)
                for k in (2 * half, 2 * half + 1):
                    kt = k0 + k
                    for a in range(2):
                        o = ps[:, a * T:(a + 1) * T]
                        start, stop = kt == 0 and a == 0, kt == KT - 1
                        at = slice(a * P, (a + 1) * P)
                        if tokens_on_partitions:
                            mm(o, hhi[:, kt, at], wh[:, k, :], start, False)
                            mm(o, hhi[:, kt, at], wl[:, k, :], False, False)
                            ins = mm(o, hlo[:, kt, at], wh[:, k, :], False, stop)
                        else:
                            ins = three(o, wh[:, k, at], wl[:, k, at], hhi[:, kt, :], hlo[:, kt, :], start, stop)
                if half:
                    ins.then_inc(unit_used, 1)

            def setup(s):
                if s == 1:
                    pe.wait_ge(evicted, 1)
                    pe.wait_ge(hT_staged, 16)
                    for b in range(NB):
                        ins = nc.tensor.transpose(psm[0][:, 16 * b:16 * b + 16], lowrank[32:48, b * P:(b + 1) * P],
                                                  ident[32:48, 32:48])
                    ins.then_inc(ab_ps, 1)
                    pe.wait_ge(gate_in, 32)
                    for b in range(NB):
                        mm(psm[1 + b][:, :], lowrank[0:RANK, b * P:(b + 1) * P], w2_sb, True, False)
                        mm(psm[1 + b][:, :], ones[0:1, :], gb_sb, False, True).then_inc(logit_ps, 1)
                if s == 6:
                    pe.wait_ge(gdec_step, 5)
                    pe.wait_ge(consts_ready, 1)
                    mm(psm[3][:, 0:16], upto, gdec.rearrange("p b h -> p (b h)"))
                    mm(psm[3][:, 16:32], after, gdec.rearrange("p b h -> p (b h)")).then_inc(cum_ps, 1)

            def gdn(p, s):
                n = p + 1
                if s == 0:
                    if p:
                        pe.wait_ge(z0_done, p)
                        pe.wait_ge(s_done, p)
                    for j in range(2):
                        pe.wait_ge(sq_done, 2 * p + j + 1)
                        mm(psm[j][:, :], ones[:, :], sumsq[:, 2 * j:2 * j + 2].rearrange("p h t -> p (h t)")).then_inc(nsum_ps, 1)
                if s == 1:
                    pe.wait_ge(gu_done, 4 * n)
                    if p:
                        pe.wait_ge(on_done, p)
                        pe.wait_ge(vnew_done, 2 * p)
                    mm(psm[4][:, :], after, gam.rearrange("p j t -> p (j t)")).then_inc(decay_ps, 1)
                    mm(psm[5][:, 0:T].rearrange("p (h t) -> p h t", h=2), ones[:, :],
                       gam.rearrange("p (h b) t -> p h b t", b=2)[:, :, 1, :]).then_inc(cumb_ps, 1)
                    for j in range(4):
                        h, b = divmod(j, 2)
                        ins = nc.tensor.transpose(psm[2][:, j * P:(j + 1) * P], kqv[:, 4 + h, b * P:(b + 1) * P], ident[:, :])
                    ins.then_inc(vT_ps, 1)
                if s == 3:
                    pe.wait_ge(kq_normed, 2 * p + 1)
                    for j in range(4):
                        h, b = divmod(j, 2)
                        k = kqv[:, h, b * P:(b + 1) * P]
                        ins = nc.tensor.transpose(psm[3][:, j * P:(j + 1) * P], k, ident[:, :])
                    ins.then_inc(kT_ps, 1)
                    for j in range(4):
                        h, b = divmod(j, 2)
                        k = kqv[:, h, b * P:(b + 1) * P]
                        ins = mm(psm[0][:, j * P:(j + 1) * P], k, k)
                    ins.then_inc(kk_ps, 1)
                if s == 4:
                    pe.wait_ge(kq_normed, 2 * n)
                    for j in range(4):
                        h, b = divmod(j, 2)
                        at = slice(b * P, (b + 1) * P)
                        ins = mm(psm[1][:, j * P:(j + 1) * P], kqv[:, h, at], kqv[:, 2 + h, at])
                    ins.then_inc(qk_ps, 1)
                if s == 5:
                    pe.wait_ge(w_done, 8 * p + 2)
                    pe.wait_ge(vtok_done, n)
                    for j in range(4):
                        ins = nc.tensor.transpose(psm[2][:, j * P:(j + 1) * P], wup[:, j, :], ident[:, :])
                    ins.then_inc(wT_ps, 1)
                if 6 <= s < 18:
                    lev = (s - 4) // 2
                    if s % 2 == 0:
                        pe.wait_ge(nmask_done, 6 * p + lev)
                        pe.wait_ge(y_done, 6 * p + lev)
                        pe.wait_ge(ktok_done, n)
                        for j in range(4):
                            ins = mm(psm[3][:, j * P:(j + 1) * P], nmask[:, lev % 2, j, :], ylow[:, j, :])
                        ins.then_inc(t1_ps, 1)
                    else:
                        pe.wait_ge(t1_done, 6 * p + lev)
                        pe.wait_ge(w_done, 8 * p + 1 + lev)
                        if lev == 1:
                            pe.wait_ge(ecum_done, n)
                        if lev < 6:
                            for j in range(4):
                                ins = mm(psm[5][:, j * P:(j + 1) * P], wup[:, j, :], t1[:, j, :])
                            ins.then_inc(yd_ps, 1)
                        for j in range(4):
                            ins = mm(psm[4][:, j * P:(j + 1) * P], t1[:, j, :], wup[:, j, :])
                        ins.then_inc(wd_ps, 1)
                if s == 18:
                    pe.wait_ge(w_done, 8 * n)
                    for h in range(2):
                        ins = mm(psm[0][:, h * P:(h + 1) * P], wup[:, 2 * h, :], vtok[:, 2 * h, :])
                    ins.then_inc(z0_ps, 1)
                if s == 19:
                    pe.wait_ge(z0d_done, 2 * n)
                    pe.wait_ge(attn_done, n)
                    for h in range(2):
                        ins = mm(psm[1][:, h * P:(h + 1) * P], ktok[:, 2 * h, :], z0d[:, h, :])
                    ins.then_inc(s_ps, 1)
                if s == 20:
                    pe.wait_ge(s_done, n)
                    for h in range(2):
                        ins = mm(psm[2][:, h * P:(h + 1) * P], kqv[:, h, P:T], state[:, h, :])
                    ins.then_inc(ks_ps, 1)
                if s == 21:
                    pe.wait_ge(vnew_done, 2 * n)
                    pe.wait_ge(t1_done, 6 * n)
                    for h in range(2):
                        ins = mm(psm[3][:, h * P:(h + 1) * P], wup[:, 2 * h + 1, :], vnew[:, h, :])
                    ins.then_inc(z1_ps, 1)
                if s == 22:
                    pe.wait_ge(z1_done, n)
                    pe.wait_ge(qdec_done, n)
                    for h in range(2):
                        o = psm[4][:, h * T:(h + 1) * T]
                        mm(o[:, 0:P], z0[:, h, :], attn[:, 2 * h, :])
                        mm(o[:, P:T], z1[:, h, :], attn[:, 2 * h + 1, :], True, False)
                        ins = mm(o[:, P:T], state[:, h, :], qdec[:, h, :], False, True)
                    ins.then_inc(o_ps, 1)
                if s == 23:
                    pe.wait_ge(osq_done, n)
                    mm(psm[5][:, :], ones[:, :], orms.rearrange("p a t -> p (a t)")).then_inc(osum_ps, 1)

            def gla(g, s):
                for hb in range(4):
                    h, b = divmod(hb, 2)
                    head, n = 2 * g + h, 4 * g + hb
                    s0 = 1 + 6 * hb
                    if s == s0:
                        if n == 0:
                            pe.wait_ge(mask_ready, 1)
                            pe.wait_ge(loga_done, 2)
                            pe.wait_ge(s_done, 4)
                        for k in range(2):
                            if n:
                                pe.wait_ge(gexp_done, 2 * n - 1 + k)
                            mm(psm[k][:, :], loga[:, b, head * P:(head + 1) * P],
                               msum[:, b + 4 * k:b + 4 * k + 4, :].rearrange("p l t -> p (l t)")).then_inc(gsum_ps, 1)
                    if s == s0 + 3:
                        pe.wait_ge(gkd_done, n + 1)
                        pe.wait_ge(gqd_done, n + 1)
                        if n == 0:
                            pe.wait_ge(z1_done, 4)
                        else:
                            pe.wait_ge(prod_done, 2 * n)
                        for lev in range(7):
                            i = lev + 1 - b
                            mm(psm[2 + lev // 4][:, (lev % 4) * P:(lev % 4 + 1) * P], gkd[:, b, i, :], gqd[:, b, i, :])
                        at = slice(b * P, (b + 1) * P)
                        ins = mm(psm[3][:, 3 * P:], gk[:, g, h, at], gq[:, g, h, at])
                        if b:
                            pe.wait_ge(on_done, 4 + head)
                            ins = mm(psm[4][:, 0:P], gkd[:, 0, 0, :], gqd[:, 1, 7, :])
                        ins.then_inc(score_ps, 1)
                    if s == s0 + 6 and b:
                        pe.wait_ge(gattn_done, n + 1)
                        pe.wait_ge(cross_done, head + 1)
                        pe.wait_ge(evicted, 16 + 4 * g + 2 + h + 2)
                        for a in range(2):
                            o = psm[5][:, a * T:(a + 1) * T]
                            c = slice(a * P, (a + 1) * P)
                            mm(o, gv[:, head, 0, c], gattn[:, h, 0:2, :].rearrange("p i t -> p (i t)"), a == 0, False)
                            ins = mm(o[:, P:T], gv[:, head, 1, c], gattn[:, h, 2, :], False, True)
                        ins.then_inc(o_ps, 1)
                    if s == s0 + 7 and b:
                        pe.wait_ge(osq_done, 5 + head)
                        mm(psm[4][:, T:2 * T], ones[:, :], orms[:, 0, :], True, False)
                        mm(psm[4][:, T:2 * T], ones[:, :], orms[:, 1, :], False, True).then_inc(osum_ps, 1)

            for ph in range(7):
                for s in range(PHASE_STEPS):
                    blk, half = 4 * ph + s // 8, s % 2
                    u = 1 + 16 * ph + s // 2
                    if s % 8 == 0 and blk:
                        pe.wait_ge(evicted, blk)
                    if half == 0:
                        pe.wait_ge(lo_done, u + 1)
                    dense(psd[blk % 2], u, 4 * (s // 2 % 4), half, 16 <= blk < 24 and blk % 4 >= 2)
                    if ph == 0:
                        setup(s)
                    if 1 <= ph <= 4:
                        gdn(ph - 1, s)
                    if ph >= 5:
                        gla(ph - 5, s)

            def dense_rows(first_bank, u, act_hi, act_lo, tiles, first, last):
                wh, wl = ring(whi, u, 2), ring(wlo, u, 2)
                for k in range(2):
                    kt = tiles[k]
                    for b in range(NB):
                        at = slice(b * P, (b + 1) * P)
                        o = bank[first_bank + b][:, :]
                        mm(o, act_hi[:, kt, at], wh[:, k, :], first and k == 0, False)
                        mm(o, act_hi[:, kt, at], wl[:, k, :], False, False)
                        ins = mm(o, act_lo[:, kt, at], wh[:, k, :], False, last and k == 1)
                ins.then_inc(unit_used, 1)

            for c in range(4):
                for q in range(OUT_UNITS):
                    u = U_OUT + OUT_UNITS * c + q
                    if q == 0 and c == 0:
                        pe.wait_ge(evicted, NBLK + 1)
                    if q == 0 and c == 1:
                        pe.wait_ge(on_done, 8)
                    if q == 0 and c >= 2:
                        pe.wait_ge(res_add, 2 * (c - 1))
                    pe.wait_ge(lo_done, u + 1)
                    if c == 0:
                        kt = OUT_ORDER[2 * q]
                        pe.wait_ge(mix_lo, kt // 2 - 3 if kt >= 8 else 5 + kt // 2)
                    dense_rows(2 * (c % 2), u, mhi, mlo, OUT_ORDER[2 * q:2 * q + 2], q == 0, q == OUT_UNITS - 1)
                    if c and q == 2:
                        pe.wait_ge(res_add, 2 * c)
                        for n in range(2):
                            if c == 3:
                                pe.wait_ge(hT_staged, 2 * (8 + n) + 2)
                            turn(8 + 2 * (c - 1) + n, psm[2 * ((c - 1) % 2) + n])

            def gate_or_up(ps, u, q):
                for half in range(2):
                    dense(ps, u, 4 * (q % BLK_UNITS), half)

            for q in range(GU_UNITS):
                u = U_GU + q
                pe.wait_ge(lo_done, u + 1)
                if q == 0:
                    pe.wait_ge(res_add, 6)
                if q < 4:
                    pe.wait_ge(hT_lo, 8 + 2 * (q + 1))
                gate_or_up(psd[q // BLK_UNITS], u, q)
                if q == 1:
                    pe.wait_ge(res_add, 8)
                    for n in range(2):
                        pe.wait_ge(hT_staged, 2 * (10 + n) + 2)
                        turn(14 + n, psm[2 + n])
                if q == 3:
                    pe.wait_ge(rcol_done, 2)
                    for b in range(NB):
                        ins = mm(psm[0][:, b * P:(b + 1) * P], rb_col[b], ident[:, :])
                    ins.then_inc(rb_ps, 1)
            with pe.Fori(1, PAIRS) as i:
                for q in range(GU_UNITS):
                    if q == 0:
                        pe.wait_ge(g_scaled, i)
                    if q == 4:
                        pe.wait_ge(u_scaled, i)
                    pe.wait_ge(lo_done, i * GU_UNITS + (U_GU + q + 1))
                    gate_or_up(psd[q // BLK_UNITS], U_GU + q, q)

            for c in range(4):
                for q in range(DOWN_UNITS):
                    u = U_DOWN + DOWN_UNITS * c + q
                    if q == 0 and c == 1:
                        pe.wait_ge(u_scaled, PAIRS)
                    if q == 0 and c >= 2:
                        pe.wait_ge(res_add, 8 + 2 * (c - 1))
                    pe.wait_ge(lo_done, u + 1)
                    if c == 0:
                        pe.wait_ge(f_lo, q + 1)
                    dense_rows(2 - 2 * (c % 2), u, fhi, flo, (2 * q, 2 * q + 1), q == 0, q == DOWN_UNITS - 1)


_INS = ["x", "attn_norm_w", "w_in", "gla_gate_w2", "gla_gate_b", "gla_norm_w", "gdn_conv_w", "gdn_a_log",
        "gdn_dt_bias", "gdn_norm_w", "w_out", "ffn_norm_w", "w_gate", "w_up", "w_down", "final_norm_w"]


def kernel(**inputs):
    import numpy as _np
    import concourse.bacc as _bacc
    from concourse import mybir as _mybir
    from concourse.bass_utils import run_bass_kernel_spmd as _run

    nc = _bacc.Bacc("TRN2", target_bir_lowering=False, num_devices=1)
    arrays, args = {}, []
    for name in _INS:
        a = _np.ascontiguousarray(inputs[name])
        arrays[f"in_{name}_dram"] = a
        args.append(nc.dram_tensor(f"in_{name}_dram", a.shape, _mybir.dt.from_np(a.dtype), kind="ExternalInput").ap())
    args.append(nc.dram_tensor("out_0_dram", (1, T, D), _mybir.dt.float32, kind="ExternalOutput").ap())
    hybrid_block(nc, *args)
    r = _run(nc, [arrays], core_ids=[0])
    return r.results[0]["out_0_dram"]
```

```python
from contextlib import ExitStack

import concourse.bass as bass
from concourse import mybir

F32 = mybir.dt.float32
F32R = mybir.dt.float32r
ALU = mybir.AluOpType
ACT = mybir.ActivationFunctionType
AX_X = mybir.AxisListType.X

P = 128
T = 256
NB = T // P
D = 2048
KT = D // P
DFF = 5632
FT = DFF // P
EPS = 1e-6
DK = 128
GLA_HEADS, GDN_HEADS, RANK = 4, 8, 16
TAU = 16.0
TAPS = 4
BASE = 16
LOG_BASE = 4
LEVELS = 7 - LOG_BASE
BLOCKS = P // BASE
LOWER = BASE // 2

A_Q, A_K, A_V, A_LR, A_GATE = 0, 512, 1024, 2048, 2064
B_Q, B_K, B_V, B_A, B_Z = 3088, 4112, 5136, 6160, 6176

COLS = 256
UNIT = 1024
RING = 4
AHEAD = 2
PHASE_STEPS = 32
CONV_STEPS = (12, 16, 24)
POOL_STEPS = (4, 6, 8, 10)

IN_BLOCKS = [c for p in range(4) for c in (B_K + COLS * p, B_Q + COLS * p, B_V + COLS * p, B_Z + COLS * p)]
IN_BLOCKS += [c for g in range(2) for c in (A_Q + COLS * g, A_K + COLS * g, A_V + 512 * g, A_V + 512 * g + COLS)]
IN_BLOCKS += [A_GATE + COLS * h for h in range(GLA_HEADS)]
NBLK = len(IN_BLOCKS)
BLK_UNITS = KT * COLS // UNIT
NARROW = BLK_UNITS
U_OUT = 1 + NBLK * BLK_UNITS
OUT_UNITS = KT * 512 // UNIT
U_GU = U_OUT + 4 * OUT_UNITS
PAIRS = DFF // COLS
GU_UNITS = 2 * BLK_UNITS
U_DOWN = U_GU + PAIRS * GU_UNITS
DOWN_UNITS = FT * 512 // UNIT
U_END = U_DOWN + 4 * DOWN_UNITS


def unit_of(ph, s):
    return 16 * ph + s // 2 + (0 if ph == 0 and s < 8 else 1)


def used_after(b):
    return BLK_UNITS if b == 0 else 1 + BLK_UNITS * (b + 1)


def evicted_after(b):
    return 1 if b == 0 else b + 2


OUT_ORDER = list(range(8, KT)) + list(range(8))


def hybrid_block(nc, x, attn_norm_w, w_in, gla_gate_w2, gla_gate_b, gla_norm_w, gdn_conv_w, gdn_a_log,
                 gdn_dt_bias, gdn_norm_w, w_out, ffn_norm_w, w_gate, w_up, w_down, final_norm_w, out):
    x_tok = x.rearrange("a (b p) d -> p (a b) d", p=P)
    out_tok = out.rearrange("a (b p) d -> p (a b) d", p=P)

    with ExitStack() as ctx:
        def sb(name, words, dt=F32, stack=ctx):
            return stack.enter_context(nc.sbuf_tensor(name, [P, words], dt))

        def sem(name):
            return ctx.enter_context(nc.semaphore(name))

        def cut(t, at, *shape):
            n = 1
            for s in shape:
                n *= s
            v = t[:, at:at + n]
            if len(shape) == 2:
                return v.rearrange("p (a b) -> p a b", a=shape[0])
            if len(shape) == 3:
                return v.rearrange("p (a b c) -> p a b c", a=shape[0], b=shape[1])
            return v

        raw = sb("raw", RING * UNIT)
        whi = sb("whi", RING * UNIT, F32R)
        wlo = sb("wlo", RING * UNIT, F32R)
        hhi_t = sb("hhi", KT * T, F32R)
        hlo_t = sb("hlo", KT * T, F32R)
        big = sb("big", NB * D)
        ident = sb("ident", P)
        ones = sb("ones", P)
        vec_t = sb("vecT", 132)
        cst = sb("cst", 4)
        rb = sb("rb", T)
        stat = sb("stat", 32)
        hhi, hlo = cut(hhi_t, 0, KT, T), cut(hlo_t, 0, KT, T)
        resid = cut(big, 0, NB, D)
        conv_w = vec_t[:, 0:96]
        attn_w, ffn_w = vec_t[:, 96:112], vec_t[:, 112:128]
        gla_w, gdn_w = vec_t[:, 128:130], vec_t[:, 130:131]
        eps_c, dk_eps_c, one_c = cst[:, 0:1], cst[:, 1:2], cst[:, 2:3]

        mix_scope = ExitStack()
        mhi_t = sb("mixhi", KT * T, F32R, mix_scope)
        mlo_t = sb("mixlo", KT * T, F32R, mix_scope)
        mhi, mlo = cut(mhi_t, 0, KT, T), cut(mlo_t, 0, KT, T)
        consts = sb("consts", 8 * P, stack=mix_scope)
        mask = cut(consts, 0, 8, P)
        msum_t = sb("msum", 9 * P, F32R, mix_scope)
        msum = cut(msum_t, 0, 9, P)
        after, upto = msum[:, 0, :].bitcast(F32), msum[:, 8, :].bitcast(F32)
        kqv = cut(big, 0, 6, T)
        convd = cut(big, 6 * T, 6, T)
        sumsq = cut(big, 12 * T, 4, T)
        gkd = big[:, 0:2048].rearrange("p (b l t) -> p b l t", b=2, l=8)
        gqd = big[:, 2048:4096].rearrange("p (b l t) -> p b l t", b=2, l=8)
        work = sb("work", 2048, stack=mix_scope)
        convin = cut(work, 0, 6, T + TAPS - 1)
        gexp, gprod = cut(work, 0, 8, P), cut(work, 1024, 8, P)
        gdn_a = sb("gdn_a", 2048, stack=mix_scope)
        vtok, ktok = cut(gdn_a, 0, 4, P), cut(gdn_a, 512, 4, P)
        wup, ylow = cut(gdn_a, 1024, 4, P), cut(gdn_a, 1536, 4, P)
        gon = gdn_a[:, 0:2048].rearrange("p (h n) -> p h n", h=4)
        gdn_b = sb("gdn_b", 1024, stack=mix_scope)
        nmask = gdn_b[:, 0:1024].rearrange("p (b j t) -> p b j t", b=2, j=4)
        gattn = gdn_b[:, 0:768].rearrange("p (h i t) -> p h i t", h=2, i=3)
        gdn_c = sb("gdn_c", 5 * 512, stack=mix_scope)
        gam, bgam = cut(gdn_c, 0, 4, P), cut(gdn_c, 512, 4, P)
        attn, nmat, t1 = cut(gdn_c, 1024, 4, P), cut(gdn_c, 1536, 4, P), cut(gdn_c, 2048, 4, P)
        gates, gates2 = gdn_c[:, 0:512], gdn_c[:, 512:1024]
        lowrank = gdn_c[:, 1024:1280]
        w2_sb, gb_sb = gdn_c[0:RANK, 1536:2048], gdn_c[0:1, 2048:2560]
        stage = cut(gdn_c, 0, 2, 512)
        gdn_d = sb("gdn_d", 7 * 256 + 3 * 512, stack=mix_scope)
        z0, z1, z0d = cut(gdn_d, 0, 2, P), cut(gdn_d, 256, 2, P), cut(gdn_d, 512, 2, P)
        state, vnew = cut(gdn_d, 768, 2, P), cut(gdn_d, 1024, 2, P)
        qdec, ecum = cut(gdn_d, 1280, 2, P), cut(gdn_d, 1536, 2, P)
        gz, orms, omix = cut(gdn_d, 1792, 2, T), cut(gdn_d, 2304, 2, T), cut(gdn_d, 2816, 2, T)
        vec_in = gdn_d[:, 0:256].rearrange("p (a b) -> p a b", a=2)
        gq_t = sb("gq", 1024, stack=mix_scope)
        gk_t = sb("gk", 1024, stack=mix_scope)
        gv_t = sb("gv", 2048, stack=mix_scope)
        loga_hi_t = sb("loga_hi", 1024, F32R, mix_scope)
        loga_lo_t = sb("loga_lo", 1024, F32R, mix_scope)
        gq, gk = cut(gq_t, 0, 2, 2, T), cut(gk_t, 0, 2, 2, T)
        gv = gv_t[:, :].rearrange("p (h b v) -> p h b v", h=4, b=2)
        loga_hi, loga_lo = cut(loga_hi_t, 0, NB, 512), cut(loga_lo_t, 0, NB, 512)
        loga = cut(gdn_d, 0, NB, 512)
        msum_in = cut(gdn_d, 1024, 9, P)
        tiny = sb("tiny", 12 * 16, stack=mix_scope)
        ab, gdec, beta, ecol, esuf = (cut(tiny, 32 * 0, 2, 16), cut(tiny, 32, 2, 8), cut(tiny, 48, 2, 8),
                                      cut(tiny, 64, 2, 8), cut(tiny, 80, 2, 8))
        base_t = sb("base", P + BASE, stack=mix_scope)
        block_neg = base_t[:, 0:P]
        eye_neg = base_t[:, P:P + BASE]
        base_n, base_w = cut(gdn_a, 1536, 4, BASE), cut(gdn_a, 1536 + 4 * BASE, 4, BASE)
        sel = [cut(big, 12 * T, LOWER, 4, BASE), cut(big, 12 * T + 2 * BASE * BASE, LOWER, 4, LOWER)]
        bsuf, necol, tmp_a, tmp_b = cut(tiny, 96, 2, 8), cut(tiny, 112, 2, 8), cut(tiny, 128, 2, 8), cut(tiny, 144, 2, 8)
        alog_b, dtb_b, expa = tiny[:, 160:168], tiny[:, 168:176], tiny[:, 176:184]
        mix_scope.close()

        fhi_t = sb("ffhi", FT * T, F32R)
        flo_t = sb("fflo", FT * T, F32R)
        fhi, flo = cut(fhi_t, 0, FT, T), cut(flo_t, 0, FT, T)
        ffn_tmp = sb("ffn_tmp", 3 * 512)
        fgate, fup = ffn_tmp[:, 0:512], ffn_tmp[:, 512:1024]
        fprod = ffn_tmp[:, 1024:1536]
        final_w = sb("final_w", D)
        rb_col = [final_w[:, b * P:(b + 1) * P] for b in range(NB)]

        psd = [ctx.enter_context(nc.psum_tensor(f"psd{i}", [P, 512], F32)) for i in range(2)]
        psm = [ctx.enter_context(nc.psum_tensor(f"psm{i}", [P, 512], F32)) for i in range(6)]
        bank = psd + psm[4:6]

        raw_in = [sem(f"raw_in{i}") for i in range(RING)]
        hi_done, lo_done, unit_used = sem("hi_done"), sem("lo_done"), sem("unit_used")
        x_in = [sem(f"x_in{i}") for i in range(2 * NB)]
        vec_in_sem, gate_in, tiny_in = sem("vec_in"), sem("gate_in"), sem("tiny_in")
        pool_seq, pad_ready, cst_ready, msum_built, consts_ready = (sem("pool_seq"), sem("pad_ready"), sem("cst_ready"),
                                                                    sem("msum_built"), sem("consts_ready"))
        mask_ready = sem("mask_ready")
        ms_act, ms_dve, ms_total, ms_ln = sem("ms_act"), sem("ms_dve"), sem("ms_total"), sem("ms_ln")
        rstd_done, x_scaled0, x_scaled1 = sem("rstd_done"), sem("x_scaled0"), sem("x_scaled1")
        vec_ps, vec_done = sem("vec_ps"), sem("vec_done")
        hT_ps, hT_staged, hT_hi, hT_lo = sem("hT_ps"), sem("hT_staged"), sem("hT_hi"), sem("hT_lo")
        evicted = sem("evicted")
        ab_ps, logit_ps, ab_done, abs_done = sem("ab_ps"), sem("logit_ps"), sem("ab_done"), sem("abs_done")
        lnexp, loga_done, loga_split, gdec_step, act_tiny = sem("lnexp"), sem("loga_done"), sem("loga_split"), sem("gdec_step"), sem("act_tiny")
        cum_ps, cum_exp, tiny_done = sem("cum_ps"), sem("cum_exp"), sem("tiny_done")
        conv_step, silu_done, sq_done = sem("conv_step"), sem("silu_done"), sem("sq_done")
        nsum_ps, ln_done, rn_done, kq_normed = sem("nsum_ps"), sem("ln_done"), sem("rn_done"), sem("kq_normed")
        gu_done, decay_ps, cumb_ps, gam_done, ecum_done = (sem("gu_done"), sem("decay_ps"), sem("cumb_ps"),
                                                           sem("gam_done"), sem("ecum_done"))
        bgam_done, vT_ps, kT_ps, kk_ps, qk_ps = sem("bgam_done"), sem("vT_ps"), sem("kT_ps"), sem("kk_ps"), sem("qk_ps")
        vtok_done, ktok_done, nmat_done, attn_done, qdec_done = (sem("vtok_done"), sem("ktok_done"), sem("nmat_done"),
                                                                 sem("attn_done"), sem("qdec_done"))
        neg_ready, eye_step, base_n_done, sel_done, rows_ps, base_step = (
            sem("neg_ready"), sem("eye_step"), sem("base_n_done"), sem("sel_done"), sem("rows_ps"), sem("base_step"))
        nmask_done, w_done, wT_ps, y_done = sem("nmask_done"), sem("w_done"), sem("wT_ps"), sem("y_done")
        t1_ps, t1_done, wd_ps, yd_ps = sem("t1_ps"), sem("t1_done"), sem("wd_ps"), sem("yd_ps")
        z0_ps, z0_done, z0d_done, s_ps, s_done = sem("z0_ps"), sem("z0_done"), sem("z0d_done"), sem("s_ps"), sem("s_done")
        ks_ps, vnew_done, z1_ps, z1_done = sem("ks_ps"), sem("vnew_done"), sem("z1_ps"), sem("z1_done")
        o_ps, osq_done, osum_ps, oln_done, orms_done, on_done = (sem("o_ps"), sem("osq_done"), sem("osum_ps"),
                                                                 sem("oln_done"), sem("orms_done"), sem("on_done"))
        omix_done, mix_hi, mix_lo = sem("omix_done"), sem("mix_hi"), sem("mix_lo")
        gsum_ps, gexp_done, gkd_done, gqd_done = sem("gsum_ps"), sem("gexp_done"), sem("gkd_done"), sem("gqd_done")
        score_ps, prod_done, gattn_done, cross_done = sem("score_ps"), sem("prod_done"), sem("gattn_done"), sem("cross_done")
        x_again, res_add, ssq_done, ss_done, r_ln, r_done = (sem("x_again"), sem("res_add"), sem("ssq_done"),
                                                             sem("ss_done"), sem("r_ln"), sem("r_done"))
        rcol_done, rb_ps, rb_done = sem("rcol_done"), sem("rb_ps"), sem("rb_done")
        g_scaled, g_silu, u_scaled, f_done, f_hi, f_lo = (sem("g_scaled"), sem("g_silu"), sem("u_scaled"),
                                                          sem("f_done"), sem("f_hi"), sem("f_lo"))
        fw_in, y_ready, stored = sem("fw_in"), sem("y_ready"), sem("stored")

        block = ctx.enter_context(nc.Block())

        def slot(u):
            return u % RING

        def ring(t, u, k):
            s = slot(u) * UNIT
            return t[:, s:s + UNIT].rearrange("p (k c) -> p k c", k=k)

        @block.sync
        def _(sp):
            def load(u, src, n=None):
                n = u if n is None else n
                sp.wait_ge(lo_done, n - RING + 1)
                sp.dma_start(ring(raw, u, src.shape[1]), src).then_inc(raw_in[slot(u)], 16)

            def rows(w, k0, nk, c0, nc_):
                return w[k0 * P:(k0 + nk) * P, bass.ds(c0, nc_)].rearrange("(k p) c -> p k c", p=P)

            for n in range(2 * NB):
                b, h = divmod(n, 2)
                at = slice(h * D // 2, (h + 1) * D // 2)
                sp.dma_start(resid[:, b, at], x_tok[:, b, at]).then_inc(x_in[n], 16)
            for u in range(RING):
                sp.dma_start(ring(raw, u, 4), rows(w_in, 4 * u, 4, IN_BLOCKS[0], COLS)).then_inc(raw_in[u], 16)
            sp.wait_ge(lo_done, 1)
            small = ring(raw, NARROW, KT)
            sp.dma_start(small[:, :, 0:RANK], rows(w_in, 0, KT, A_LR, RANK)).then_inc(raw_in[0], 16)
            sp.dma_start(small[:, :, 32:48], rows(w_in, 0, KT, B_A, 16)).then_inc(raw_in[0], 16)
            for u in range(NARROW + 1, U_OUT):
                b, q = divmod(u - 1, BLK_UNITS)
                load(u, rows(w_in, 4 * q, 4, IN_BLOCKS[b], COLS))
            sp.wait_ge(score_ps, 8)
            for b in range(NB):
                sp.dma_start(resid[:, b, :], x_tok[:, b, :]).then_inc(x_again, 16)
            for u in range(U_OUT, U_GU):
                c, q = divmod(u - U_OUT, OUT_UNITS)
                load(u, rows(w_out, OUT_ORDER[2 * q], 2, 512 * c, 512))
            with sp.Fori(0, PAIRS) as i:
                for q in range(GU_UNITS):
                    w = w_gate if q < BLK_UNITS else w_up
                    load(U_GU + q, rows(w, 4 * (q % BLK_UNITS), 4, i * COLS, COLS), i * GU_UNITS + (U_GU + q))
            sp.dma_start(final_w[:, :], final_norm_w.partition_broadcast(P)).then_inc(fw_in, 16)
            with sp.Fori(0, 2) as cc:
                for u in range(2 * DOWN_UNITS):
                    c, q = divmod(u, DOWN_UNITS)
                    load(U_DOWN + u, rows(w_down, 2 * q, 2, cc * 1024 + 512 * c, 512),
                         cc * (2 * DOWN_UNITS) + (U_DOWN + u))
            for n in range(4):
                sp.wait_ge(y_ready, n + 1)
                b, h = divmod(n, 2)
                sp.dma_start(out_tok[:, b, 1024 * h:1024 * (h + 1)],
                             resid[:, b, 1024 * h:1024 * (h + 1)]).then_inc(stored, 16)
            sp.wait_ge(stored, 64)

        @block.gpsimd
        def _(pool):
            made = [0]

            def then(ins):
                made[0] += 1
                ins.then_inc(pool_seq, 1)
                pool.wait_ge(pool_seq, made[0])

            def keep(view, op, base, pattern, cm, fill=0.0):
                then(nc.gpsimd.affine_select(out=view, in_=view, compare_op=op, fill=fill, base=base,
                                             pattern=pattern, channel_multiplier=cm))

            then(nc.gpsimd.memset(ident[:, :], 0.0))
            keep(ident[:, :], ALU.not_equal, 0, [[-1, P]], 1, 1.0)
            then(nc.gpsimd.memset(cst[:, 0:1], EPS))
            then(nc.gpsimd.memset(cst[:, 1:2], DK * EPS))
            nc.gpsimd.memset(ones[:, :], 1.0).then_inc(cst_ready, 1)
            nc.gpsimd.memset(convin[:, :, 0:TAPS - 1], 0.0).then_inc(pad_ready, 1)
            pool.wait_ge(vec_ps, 1)
            then(nc.gpsimd.memset(msum_in[:, :, :], 1.0))
            keep(msum_in[:, 0, :], ALU.is_ge, -1, [[-1, P]], 1)
            keep(msum_in[:, 8, :], ALU.is_ge, 0, [[1, P]], -1)
            for lev in range(7):
                b = 1 << lev
                n = P // (2 * b)
                v = msum_in[:, 1 + lev, :].rearrange("p (n o c) -> p n o c", o=2, c=b)
                keep(v[:, :, 0, :], ALU.is_ge, -1, [[-2 * b, n], [-1, b]], 1)
                keep(v[:, :, 0, :], ALU.is_ge, b - 1, [[2 * b, n], [0, b]], -1)
                keep(v[:, :, 1, :], ALU.is_ge, -b, [[-2 * b, n], [0, b]], 1)
                keep(v[:, :, 1, :], ALU.is_ge, b, [[2 * b, n], [1, b]], -1)
            nc.gpsimd.tensor_copy(mask[:, 7, :], ident[:, :]).then_inc(msum_built, 1)
            then(nc.gpsimd.memset(mask[:, 0:7, :], 0.0))
            for lev in range(7):
                b = 1 << lev
                n = P // (2 * b)
                m = mask[:, lev, :].rearrange("p (n o c) -> p n o c", o=2, c=b)[:, :, 1, :]
                then(nc.gpsimd.memset(m, 1.0))
                keep(m, ALU.is_ge, 0, [[-2 * b, n], [0, b]], 1)
                keep(m, ALU.is_ge, b - 1, [[2 * b, n], [0, b]], -1)
            then(nc.gpsimd.memset(block_neg, -1.0))
            v = block_neg.rearrange("p (n c) -> p n c", c=BASE)
            keep(v, ALU.is_ge, 0, [[-BASE, BLOCKS], [0, BASE]], 1)
            keep(v, ALU.is_ge, BASE - 1, [[BASE, BLOCKS], [0, BASE]], -1)
            nc.gpsimd.memset(cst[:, 2:3], 1.0).then_inc(mask_ready, 1)
            def gla_q(n):
                head, b = divmod(n, 2)
                g, h = divmod(head, 2)
                pool.wait_ge(gexp_done, 2 * n + 2)
                if n >= 2:
                    pool.wait_ge(score_ps, n - b)
                nc.gpsimd.tensor_tensor(gqd[:, b], gexp, gq[:, g, h:h + 1, b * P:(b + 1) * P].to_broadcast([P, 8, P]),
                                        ALU.mult).then_inc(gqd_done, 1)

            def split_lo(u):
                pool.wait_ge(hi_done, u + 1)
                pool.wait_ge(lo_done, u)
                at = slice(slot(u) * UNIT, (slot(u) + 1) * UNIT)
                nc.gpsimd.tensor_tensor(wlo[:, at], raw[:, at], whi[:, at].bitcast(F32), ALU.subtract).then_inc(lo_done, 1)

            for p in range(4):
                for i in range(LEVELS):
                    n, lev = LEVELS * p + i, LOG_BASE + i
                    for s in POOL_STEPS[2 * i:2 * i + 2]:
                        split_lo(unit_of(p + 1, s) + AHEAD)
                    pool.wait_ge(nmat_done, p + 1)
                    if n >= 2:
                        pool.wait_ge(t1_ps, n - 1)
                    nc.gpsimd.tensor_tensor(nmask[:, n % 2], nmat, mask[:, lev:lev + 1, :].to_broadcast([P, 4, P]),
                                            ALU.mult).then_inc(nmask_done, 1)
            for n in range(2 * GLA_HEADS):
                gla_q(n)

        @block.scalar
        def _(act):
            def split_hi(u, n=None):
                n = u if n is None else n
                if isinstance(n, int):
                    act.wait_ge(raw_in[slot(u)], 16 * (n // RING + 1) + (16 if slot(u) == 0 and n else 0))
                    if n >= RING:
                        act.wait_ge(unit_used, n - RING + 1)
                nc.scalar.activation(whi[:, slot(u) * UNIT:(slot(u) + 1) * UNIT],
                                     raw[:, slot(u) * UNIT:(slot(u) + 1) * UNIT], ACT.Copy).then_inc(hi_done, 1)

            def split_hi_at(u, rounds, units):
                act.wait_ge(raw_in[slot(u)], rounds * 16 + (16 * (u // RING + 1) + (16 if slot(u) == 0 else 0)))
                act.wait_ge(unit_used, units + (u - RING + 1))
                split_hi(u, units)

            def lnexp_tables():
                nc.scalar.preload_act_table_set("natural_log_exp_and_others")

            def copy(o, i, **kw):
                return nc.scalar.activation(o, i, ACT.Copy, **kw)

            def rsqrt(o, i, tmp, scale, bias, ln_sem, n, done):
                nc.scalar.activation(tmp, i, ACT.Ln, bias=bias, scale=scale).then_inc(ln_sem, 1)
                act.wait_ge(ln_sem, n)
                nc.scalar.activation(o, tmp, ACT.Exp, scale=-0.5).then_inc(done, 1)

            act.dma_start(vec_in[0:96, 0, :], gdn_conv_w.rearrange("j (t p) -> (j t) p", p=P)).then_inc(vec_in_sem, 16)
            act.dma_start(vec_in[96:112, 0, :], attn_norm_w.rearrange("(t p) -> t p", p=P)).then_inc(vec_in_sem, 16)
            act.dma_start(vec_in[112:128, 0, :], ffn_norm_w.rearrange("(t p) -> t p", p=P)).then_inc(vec_in_sem, 16)
            act.dma_start(vec_in[0:2, 1, :], gla_norm_w.rearrange("(t p) -> t p", p=P)).then_inc(vec_in_sem, 16)
            act.dma_start(vec_in[2:3, 1, :], gdn_norm_w.rearrange("(t p) -> t p", p=P)).then_inc(vec_in_sem, 16)
            act.dma_start(w2_sb, gla_gate_w2).then_inc(gate_in, 16)
            act.dma_start(gb_sb, gla_gate_b.rearrange("(a n) -> a n", a=1)).then_inc(gate_in, 16)
            act.dma_start(alog_b, gdn_a_log.partition_broadcast(P)).then_inc(tiny_in, 16)
            act.dma_start(dtb_b, gdn_dt_bias.partition_broadcast(P)).then_inc(tiny_in, 16)
            def rms_x(b):
                act.wait_ge(x_in[2 * b], 16)
                nc.scalar.activation(gv_t[:, 0:D // 2], resid[:, b, 0:D // 2], ACT.Square,
                                     accum_out=stat[:, 2 * b:2 * b + 1]).then_inc(ms_act, 1)
                act.wait_ge(ms_total, b + 1)
                act.wait_ge(cst_ready, 1)
                rsqrt(stat[:, 6 + b:7 + b], stat[:, 4 + b:5 + b], stat[:, 24 + b:25 + b], 1.0 / D, eps_c, ms_ln, b + 1,
                      rstd_done)
                act.wait_ge(rstd_done, b + 1)
                copy(resid[:, b, D // 2:], resid[:, b, D // 2:], scale=stat[:, 6 + b:7 + b]).then_inc(x_scaled1, 1)

            def stage_hT(n, g, w, ps):
                act.wait_ge(hT_ps, n + 1)
                if n >= 2:
                    act.wait_ge(hT_lo, n - 1)
                for k in range(4):
                    copy(stage[:, n % 2, k * P:(k + 1) * P], ps[:, k * P:(k + 1) * P],
                         scale=w[:, 4 * g + k:4 * g + k + 1]).then_inc(hT_staged, 1)

            lnexp_tables()
            rms_x(0)
            act.wait_ge(vec_ps, 1)
            copy(vec_t[:, 0:128], psd[0][:, 0:128]).then_inc(vec_done, 1)
            copy(vec_t[:, 128:131], psd[0][:, 128:131]).then_inc(vec_done, 1)
            act.wait_ge(vec_done, 2)

            for n in range(2):
                stage_hT(n, n, attn_w, psm[n])
            rms_x(1)
            for n in range(2, 8):
                if n in (4, 5):
                    split_hi(n - 4)
                stage_hT(n, n % 4, attn_w, psm[n % 6])

            def evict(b):
                act.wait_ge(unit_used, used_after(b) if b >= 0 else NARROW + 1)
                ps = psd[b % 2] if b >= 0 else psm[5]
                two = ps[:, :].rearrange("p (h t) -> p h t", h=2)
                if b < 0:
                    copy(lowrank[0:64, :], ps[0:64, 0:T]).then_inc(evicted, 1)
                elif b < 16 and b % 4 < 3:
                    p, j = divmod(b, 4)
                    if p:
                        act.wait_ge(conv_step, 24 * (p - 1) + 8 * (j + 1))
                    copy(convin[:, 2 * j:2 * j + 2, TAPS - 1:], two).then_inc(evicted, 1)
                elif b < 16:
                    if b // 4:
                        act.wait_ge(omix_done, b // 4)
                    nc.scalar.activation(gz, two, ACT.Silu).then_inc(evicted, 1)
                elif b < 24:
                    g, j = divmod(b - 16, 4)
                    if j == 0:
                        copy(gq[:, g], two, scale=DK ** -0.5).then_inc(evicted, 1)
                    elif j == 1:
                        copy(gk[:, g], two).then_inc(evicted, 1)
                    else:
                        copy(gv[:, 2 * g + j - 2], two).then_inc(evicted, 1)
                else:
                    act.wait_ge(omix_done, 4 + b - 24)
                    nc.scalar.activation(gz, two, ACT.Silu).then_inc(evicted, 1)

            def setup(s):
                if s == 11:
                    lnexp_tables()
                    act.wait_ge(tiny_in, 32)
                    nc.scalar.activation(expa, alog_b, ACT.Exp).then_inc(act_tiny, 1)
                    act.wait_ge(ab_done, 2)
                    nc.scalar.activation(tmp_a, ab[:, :, 0:8], ACT.Abs).then_inc(act_tiny, 1)
                    act.wait_ge(act_tiny, 2)
                    nc.scalar.activation(tmp_a, tmp_a, ACT.Exp, scale=-1.0).then_inc(act_tiny, 1)
                    nc.scalar.activation(tmp_b, ab[:, :, 8:16], ACT.Exp, scale=-1.0).then_inc(act_tiny, 1)
                    act.wait_ge(act_tiny, 4)
                    nc.scalar.activation(tmp_a, tmp_a, ACT.Ln, bias=ones[:, 0:1]).then_inc(act_tiny, 1)
                if s in (12, 13):
                    b = s - 12
                    act.wait_ge(logit_ps, b + 1)
                    if b:
                        act.wait_ge(loga_done, b)
                    nc.scalar.activation(gates, psm[1 + b][:, :], ACT.Abs).then_inc(lnexp, 1)
                    act.wait_ge(lnexp, 3 * b + 1)
                    nc.scalar.activation(gates2, gates, ACT.Exp, scale=-1.0).then_inc(lnexp, 1)
                    act.wait_ge(lnexp, 3 * b + 2)
                    nc.scalar.activation(gates, gates2, ACT.Ln, bias=ones[:, 0:1]).then_inc(lnexp, 1)
                if s == 16:
                    act.wait_ge(cum_ps, 1)
                    nc.scalar.activation(tiny[:, 64:96], psm[3][:, 0:32], ACT.Exp).then_inc(cum_exp, 1)

            def silu(p, s):
                j = s - 26
                act.wait_ge(conv_step, 24 * p + 8 * (j + 1))
                if p:
                    act.wait_ge(ks_ps, p)
                nc.scalar.activation(kqv[:, 2 * j:2 * j + 2, :], convd[:, 2 * j:2 * j + 2, :], ACT.Silu).then_inc(silu_done, 1)

            def out_norm(n, ps, sum_ps, width, dv, s, s0):
                if s == s0:
                    act.wait_ge(o_ps, n + 1)
                    if n:
                        act.wait_ge(on_done, n)
                    nc.scalar.activation(orms, ps, ACT.Square).then_inc(osq_done, 1)
                if s == s0 + 1:
                    act.wait_ge(osum_ps, n + 1)
                    o = orms.rearrange("p a t -> p (a t)")[:, 0:width]
                    rsqrt(o, sum_ps, o, 1.0 / dv, eps_c, oln_done, n + 1, orms_done)

            def gdn(p, s):
                n = p + 1
                if s == 1:
                    lnexp_tables()
                    act.wait_ge(nsum_ps, 2 * p + 1)
                    rsqrt(sumsq[:, 0:2], psm[0][:, :].rearrange("p (h t) -> p h t", h=2), sumsq[:, 0:2], 1.0, eps_c,
                          ln_done, 2 * p + 1, rn_done)
                    act.wait_ge(nsum_ps, 2 * p + 2)
                    rsqrt(sumsq[:, 2:4], psm[1][:, :].rearrange("p (h t) -> p h t", h=2), sumsq[:, 2:4], float(DK),
                          dk_eps_c, ln_done, 2 * p + 2, rn_done)
                if s == 2:
                    act.wait_ge(decay_ps, n)
                    act.wait_ge(cumb_ps, n)
                    nc.scalar.activation(gam, psm[4][:, :].rearrange("p (j t) -> p j t", j=4), ACT.Exp).then_inc(gam_done, 1)
                    nc.scalar.activation(ecum, psm[5][:, 0:T].rearrange("p (h t) -> p h t", h=2), ACT.Exp).then_inc(ecum_done, 1)
                if s == 3:
                    act.wait_ge(vT_ps, n)
                    copy(vtok, psm[2][:, :].rearrange("p (j t) -> p j t", j=4)).then_inc(vtok_done, 1)
                    act.wait_ge(kT_ps, n)
                    copy(ktok, psm[3][:, :].rearrange("p (j t) -> p j t", j=4)).then_inc(ktok_done, 1)
                if s == 13:
                    act.wait_ge(wT_ps, n)
                    copy(ylow, psm[2][:, :].rearrange("p (j t) -> p j t", j=4)).then_inc(y_done, 1)
                if 14 <= s < 20 and s % 2 == 0:
                    act.wait_ge(t1_ps, LEVELS * p + (s - 12) // 2)
                    copy(t1, psm[3][:, :].rearrange("p (j t) -> p j t", j=4)).then_inc(t1_done, 1)
                if s == 20:
                    act.wait_ge(z0_ps, n)
                    copy(z0, psm[0][:, 0:T].rearrange("p (h t) -> p h t", h=2)).then_inc(z0_done, 1)
                if s == 21:
                    act.wait_ge(s_ps, n)
                    copy(state, psm[1][:, 0:T].rearrange("p (h t) -> p h t", h=2)).then_inc(s_done, 1)
                if s == 23:
                    act.wait_ge(z1_ps, n)
                    copy(z1, psm[3][:, 0:T].rearrange("p (h t) -> p h t", h=2)).then_inc(z1_done, 1)
                out_norm(p, psm[4][:, :].rearrange("p (h t) -> p h t", h=2), psm[5][:, :], 512, DK, s, 24)
                if s == 26:
                    act.wait_ge(omix_done, n)
                    copy(mhi[:, 8 + 2 * p:10 + 2 * p, :], omix).then_inc(mix_hi, 1)

            def gla(g, s):
                for hb in range(4):
                    h, b = divmod(hb, 2)
                    head, n = 2 * g + h, 4 * g + hb
                    s0 = 1 + 6 * hb
                    if s == s0:
                        if hb == 0:
                            lnexp_tables()
                        for k in range(2):
                            act.wait_ge(gsum_ps, 2 * n + k + 1)
                            if n and k == 0:
                                act.wait_ge(gkd_done, n)
                                act.wait_ge(gqd_done, n)
                            nc.scalar.activation(gexp[:, 4 * k:4 * k + 4, :], psm[k][:, :].rearrange("p (l t) -> p l t", l=4),
                                                 ACT.Exp, scale=1.0 / TAU).then_inc(gexp_done, 1)
                    if s == s0 + 5 and b:
                        act.wait_ge(score_ps, n + 1)
                        copy(gattn[:, h, 1, :], psm[4][:, 0:P]).then_inc(cross_done, 1)
                    if b:
                        out_norm(4 + head, psm[5][:, :].rearrange("p (a t) -> p a t", a=2), psm[4][:, T:2 * T], T, 2 * DK,
                                 s, s0 + 7)

            def gate_hi(head):
                act.wait_ge(omix_done, 5 + head)
                copy(mhi[:, 2 * head:2 * head + 2, :], omix).then_inc(mix_hi, 1)

            for ph in range(7):
                for s in range(PHASE_STEPS):
                    if ph == 0 and s == 8:
                        split_hi(NARROW + AHEAD)
                        evict(0)
                    if s % 2 == 0:
                        split_hi(unit_of(ph, s) + AHEAD)
                        if s % 8 == 0 and (ph or s):
                            evict(4 * ph + s // 8 - 1 if ph or s > 8 else -1)
                    if ph == 0:
                        setup(s)
                    if ph < 4 and 26 <= s < 29:
                        silu(ph, s)
                    if 1 <= ph <= 4:
                        gdn(ph - 1, s)
                    if ph >= 5:
                        gla(ph - 5, s)
                    if ph == 6 and s in (10, 18, 26):
                        gate_hi(s // 8 - 1)

            evict(27)
            lnexp_tables()

            def chunk_tail(c):
                for b in range(NB):
                    act.wait_ge(res_add, 2 * c + b + 1)
                    if 2 * c + b:
                        act.wait_ge(ssq_done, 2 * c + b)
                    nc.scalar.activation(gz.rearrange("p a t -> p (a t)"), resid[:, b, 512 * c:512 * (c + 1)], ACT.Square,
                                         accum_out=stat[:, 8 + 4 * b + c:9 + 4 * b + c]).then_inc(ssq_done, 1)

            for c in range(4):
                for q in range(OUT_UNITS):
                    split_hi(U_OUT + OUT_UNITS * c + q + AHEAD)
                    if c == 0 and q == 1:
                        gate_hi(3)
                    if c and q == 2:
                        chunk_tail(c - 1)
                    if c and q == 3:
                        for b in range(NB):
                            stage_hT(8 + 2 * (c - 1) + b, c - 1, ffn_w, psm[2 * ((c - 1) % 2) + b])

            def gate_silu(n):
                act.wait_ge(g_scaled, n)
                nc.scalar.activation(fgate, fgate, ACT.Silu).then_inc(g_silu, 1)

            split_hi(U_GU + 2)
            chunk_tail(3)
            split_hi(U_GU + 3)
            for b in range(NB):
                stage_hT(14 + b, 3, ffn_w, psm[2 + b])
            split_hi(U_GU + 4)
            act.wait_ge(ss_done, 1)
            nc.scalar.activation(stat[:, 18:20], stat[:, 16:18], ACT.Ln, bias=eps_c, scale=1.0 / D).then_inc(r_ln, 1)
            act.wait_ge(r_ln, 1)
            nc.scalar.activation(stat[:, 20:22], stat[:, 18:20], ACT.Exp, scale=-0.5).then_inc(r_done, 1)
            act.wait_ge(rb_ps, 1)
            copy(rb[:, :], psm[0][:, 0:T]).then_inc(rb_done, 1)
            for q in range(3, GU_UNITS):
                split_hi(U_GU + q + AHEAD)
                if q == 4:
                    gate_silu(1)
            act.wait_ge(f_done, 1)
            copy(fhi[:, 0:2, :], fprod.rearrange("p (a t) -> p a t", a=2)).then_inc(f_hi, 1)
            with act.Fori(1, PAIRS) as i:
                for q in range(GU_UNITS):
                    split_hi_at(U_GU + q + AHEAD, i * (GU_UNITS // RING), i * GU_UNITS)
                    if q == 4:
                        gate_silu(i + 1)
                act.wait_ge(f_done, i + 1)
                copy(fhi_t[:, bass.ds(i * 512, 512)], fprod).then_inc(f_hi, 1)

            lnexp_tables()

            def down_tail(c):
                for b in range(NB):
                    act.wait_ge(res_add, 8 + 2 * c + b + 1)
                    act.wait_ge(ssq_done, 8 + 2 * c + b)
                    nc.scalar.activation(fgate, resid[:, b, 512 * c:512 * (c + 1)], ACT.Square,
                                         accum_out=stat[:, 8 + 4 * b + c:9 + 4 * b + c]).then_inc(ssq_done, 1)

            for c in range(4):
                for q in range(DOWN_UNITS):
                    u = U_DOWN + DOWN_UNITS * c + q + AHEAD
                    if u < U_END:
                        split_hi(u)
                down_tail(c)
            act.wait_ge(ss_done, 2)
            nc.scalar.activation(stat[:, 18:20], stat[:, 16:18], ACT.Ln, bias=eps_c, scale=1.0 / D).then_inc(r_ln, 1)
            act.wait_ge(r_ln, 2)
            nc.scalar.activation(stat[:, 20:22], stat[:, 18:20], ACT.Exp, scale=-0.5).then_inc(r_done, 1)

        @block.vector
        def _(dve):
            def split_lo(u, n=None):
                n = u if n is None else n
                dve.wait_ge(hi_done, n + 1)
                at = slice(slot(u) * UNIT, (slot(u) + 1) * UNIT)
                nc.vector.tensor_tensor(wlo[:, at], raw[:, at], whi[:, at].bitcast(F32), ALU.subtract).then_inc(lo_done, 1)

            def rms_x(b):
                dve.wait_ge(x_in[2 * b + 1], 16)
                v = resid[:, b, D // 2:]
                nc.vector.tensor_tensor_reduce(gq_t[:, 0:D // 2], v, v, 1.0, 0.0, ALU.mult, ALU.add,
                                               stat[:, 2 * b + 1:2 * b + 2]).then_inc(ms_dve, 1)
                dve.wait_ge(ms_act, b + 1)
                dve.wait_ge(ms_dve, b + 1)
                nc.vector.tensor_tensor(stat[:, 4 + b:5 + b], stat[:, 2 * b:2 * b + 1], stat[:, 2 * b + 1:2 * b + 2],
                                        ALU.add).then_inc(ms_total, 1)
                dve.wait_ge(rstd_done, b + 1)
                nc.vector.tensor_scalar(resid[:, b, 0:D // 2], resid[:, b, 0:D // 2], stat[:, 6 + b:7 + b], None, ALU.mult)\
                    .then_inc(x_scaled0, 1)

            def split_hT(n):
                b, g = divmod(n, 4) if n < 8 else ((n - 8) % 2, (n - 8) // 2)
                k, at = slice(4 * g, 4 * g + 4), slice(b * P, (b + 1) * P)
                s = stage[:, n % 2, :].rearrange("p (k t) -> p k t", k=4)
                dve.wait_ge(hT_staged, 4 * n + 4)
                nc.vector.tensor_copy(hhi[:, k, at], s).then_inc(hT_hi, 1)
                dve.wait_ge(hT_hi, n + 1)
                nc.vector.tensor_tensor(hlo[:, k, at], s, hhi[:, k, at].bitcast(F32), ALU.subtract).then_inc(hT_lo, 1)

            rms_x(0)
            split_hT(0)
            rms_x(1)
            for n in range(1, 8):
                if n in (4, 5):
                    split_lo(n - 4)
                split_hT(n)

            def setup(s):
                if s == 10:
                    dve.wait_ge(ab_ps, 1)
                    nc.vector.tensor_copy(ab, psm[0][:, 0:32].rearrange("p (b c) -> p b c", b=2)).then_inc(ab_done, 1)
                    dve.wait_ge(ab_done, 1)
                    dve.wait_ge(tiny_in, 32)
                    for b in range(NB):
                        ins = nc.vector.tensor_tensor(ab[:, b, 0:8], ab[:, b, 0:8], dtb_b, ALU.add)
                        if b:
                            ins.then_inc(ab_done, 1)
                if s in (12, 13):
                    b = s - 12
                    dve.wait_ge(lnexp, 3 * b + 3)
                    nc.vector.scalar_tensor_tensor(out=loga[:, b, :], in0=psm[1 + b][:, :], scalar=0.0, in1=gates,
                                                   op0=ALU.min, op1=ALU.subtract).then_inc(loga_done, 1)
                if s == 12:
                    dve.wait_ge(act_tiny, 5)
                    nc.vector.scalar_tensor_tensor(out=tmp_a, in0=ab[:, :, 0:8], scalar=0.0, in1=tmp_a,
                                                   op0=ALU.max, op1=ALU.add).then_inc(gdec_step, 1)
                    nc.vector.tensor_scalar(tmp_b, tmp_b, 1.0, None, ALU.add).then_inc(gdec_step, 1)
                    dve.wait_ge(gdec_step, 2)
                    for b in range(NB):
                        nc.vector.scalar_tensor_tensor(out=gdec[:, b, :], in0=tmp_a[:, b, :], scalar=-1.0, in1=expa,
                                                       op0=ALU.mult, op1=ALU.mult).then_inc(gdec_step, 1)
                    nc.vector.reciprocal(beta, tmp_b).then_inc(gdec_step, 1)
                if s == 14:
                    dve.wait_ge(msum_built, 1)
                    nc.vector.tensor_copy(msum, msum_in).then_inc(consts_ready, 1)
                if s == 16:
                    dve.wait_ge(loga_done, 2)
                    nc.vector.tensor_copy(loga_hi, loga).then_inc(loga_split, 1)
                    dve.wait_ge(loga_split, 1)
                    nc.vector.tensor_tensor(loga_lo, loga, loga_hi.bitcast(F32), ALU.subtract).then_inc(loga_split, 1)
                if s == 17:
                    dve.wait_ge(cum_exp, 1)
                    dve.wait_ge(gdec_step, 5)
                    nc.vector.tensor_tensor(bsuf, beta, esuf, ALU.mult).then_inc(tiny_done, 1)
                    nc.vector.tensor_scalar(necol, ecol, -1.0, None, ALU.mult).then_inc(tiny_done, 1)
                if s == 24:
                    dve.wait_ge(mask_ready, 1)
                    nc.vector.tensor_tensor(t1[:, 0, :], ident[:, :], block_neg, ALU.mult).then_inc(eye_step, 1)
                    dve.wait_ge(eye_step, 1)
                    nc.vector.tensor_reduce(eye_neg, t1[:, 0, :].rearrange("p (n c) -> p c n", n=BLOCKS), AX_X, ALU.add)\
                        .then_inc(eye_step, 1)

            def conv(p, j):
                dve.wait_ge(evicted, evicted_after(4 * p + j))
                if p == 0 and j == 0:
                    dve.wait_ge(pad_ready, 1)
                    dve.wait_ge(vec_done, 2)
                if p:
                    dve.wait_ge(silu_done, 3 * (p - 1) + j + 1)
                tile0 = {0: 8, 1: 0, 2: 16}[j] + 2 * p
                for tap in range(TAPS):
                    for h in range(2):
                        c = 24 * tap + tile0 + h
                        src = convin[:, 2 * j + h, tap:tap + T]
                        dst = convd[:, 2 * j + h, :]
                        if tap == 0:
                            ins = nc.vector.tensor_scalar(dst, src, conv_w[:, c:c + 1], None, ALU.mult)
                        else:
                            dve.wait_ge(conv_step, 24 * p + 8 * j + 2 * tap - 1 + h)
                            ins = nc.vector.scalar_tensor_tensor(out=dst, in0=src, scalar=conv_w[:, c:c + 1], in1=dst,
                                                                 op0=ALU.mult, op1=ALU.add)
                        ins.then_inc(conv_step, 1)

            def square(p, j):
                dve.wait_ge(silu_done, 3 * p + j + 1)
                if p:
                    dve.wait_ge(kq_normed, 2 * p)
                nc.vector.tensor_tensor(sumsq[:, 2 * j:2 * j + 2], kqv[:, 2 * j:2 * j + 2], kqv[:, 2 * j:2 * j + 2],
                                        ALU.mult).then_inc(sq_done, 1)

            def decays(p):
                if p == 0:
                    dve.wait_ge(gdec_step, 5)
                    dve.wait_ge(consts_ready, 1)
                if p:
                    dve.wait_ge(bgam_done, 4 * p)
                for j in range(4):
                    h, b = divmod(j, 2)
                    nc.vector.tensor_scalar(gam[:, j, :], upto, gdec[:, b, 2 * p + h:2 * p + h + 1], None, ALU.mult)\
                        .then_inc(gu_done, 1)

            base_steps = 2 + 4 * (BASE - 1)

            def gdn(p, s):
                n = p + 1
                if s in (1, 2):
                    j = s - 1
                    dve.wait_ge(rn_done, 2 * p + j + 1)
                    nc.vector.tensor_tensor(kqv[:, 2 * j:2 * j + 2], kqv[:, 2 * j:2 * j + 2], sumsq[:, 2 * j:2 * j + 2],
                                            ALU.mult).then_inc(kq_normed, 1)
                if s == 2:
                    dve.wait_ge(gam_done, n)
                    for j in range(4):
                        h, b = divmod(j, 2)
                        nc.vector.scalar_tensor_tensor(out=bgam[:, j, :], in0=gam[:, j, :],
                                                       scalar=beta[:, b, 2 * p + h:2 * p + h + 1], in1=upto,
                                                       op0=ALU.mult, op1=ALU.mult).then_inc(bgam_done, 1)
                if s == 3:
                    dve.wait_ge(bgam_done, 4 * n)
                    dve.wait_ge(kk_ps, n)
                    nc.vector.tensor_tensor(nmat, psm[0][:, :].rearrange("p (j t) -> p j t", j=4), bgam, ALU.mult)\
                        .then_inc(nmat_done, 1)
                    dve.wait_ge(nmat_done, n)
                    nc.vector.tensor_tensor(t1, nmat, block_neg.unsqueeze(1).to_broadcast([P, 4, P]), ALU.mult)\
                        .then_inc(base_step, 1)
                    dve.wait_ge(base_step, base_steps * p + 1)
                    nc.vector.tensor_reduce(base_n, t1.rearrange("p j (n c) -> p j c n", n=BLOCKS), AX_X, ALU.add)\
                        .then_inc(base_n_done, 1)
                    if p == 0:
                        dve.wait_ge(eye_step, 2)
                    nc.vector.tensor_copy(base_w, eye_neg.unsqueeze(1).to_broadcast([P, 4, BASE])).then_inc(base_step, 1)
                if s == 3:
                    dve.wait_ge(base_n_done, n)
                    for i in range(2):
                        cols = slice(LOWER * i, BASE)
                        nc.vector.tensor_tensor(sel[i], base_n[:, :, cols].unsqueeze(1).to_broadcast([P, LOWER, 4, BASE - LOWER * i]),
                                                eye_neg[:, LOWER * i:LOWER * (i + 1)].unsqueeze(2).unsqueeze(3)
                                                .to_broadcast([P, LOWER, 4, BASE - LOWER * i]), ALU.mult).then_inc(sel_done, 1)
                if 5 <= s < 12:
                    for r in range((s - 5) * 15 // 7, (s - 4) * 15 // 7):
                        i = r // LOWER
                        if r % LOWER == 0:
                            dve.wait_ge(rows_ps, 2 * p + i + 1)
                        row = psm[4 + i][:, 0:LOWER * 4 * (BASE - LOWER * i)].rearrange("p (s j t) -> p s j t", s=LOWER, j=4)
                        for j in range(4):
                            dve.wait_ge(base_step, base_steps * p + (4 * r + j - 1 if r else 2))
                            nc.vector.scalar_tensor_tensor(out=base_w[:, j, r + 1:], in0=row[:, r % LOWER, j, r + 1 - LOWER * i:],
                                                           scalar=base_w[:, j, r:r + 1], in1=base_w[:, j, r + 1:],
                                                           op0=ALU.mult, op1=ALU.add).then_inc(base_step, 1)
                if s == 11:
                    dve.wait_ge(base_step, base_steps * n)
                    nc.vector.tensor_tensor(wup.rearrange("p j (n c) -> p j n c", n=BLOCKS),
                                            base_w.unsqueeze(2).to_broadcast([P, 4, BLOCKS, BASE]),
                                            block_neg.rearrange("p (n c) -> p n c", n=BLOCKS).unsqueeze(1)
                                            .to_broadcast([P, 4, BLOCKS, BASE]), ALU.mult).then_inc(w_done, 1)
                if s == 12:
                    dve.wait_ge(qk_ps, n)
                    nc.vector.tensor_tensor(attn, psm[1][:, :].rearrange("p (j t) -> p j t", j=4), bgam, ALU.mult)\
                        .then_inc(attn_done, 1)
                    dve.wait_ge(ecum_done, n)
                    dve.wait_ge(kq_normed, 2 * n)
                    nc.vector.tensor_tensor(qdec, kqv[:, 2:4, P:T], ecum, ALU.mult).then_inc(qdec_done, 1)
                if 14 <= s < 20 and s % 2:
                    i = (s - 14) // 2
                    if i < LEVELS - 1:
                        dve.wait_ge(yd_ps, (LEVELS - 1) * p + i + 1)
                        nc.vector.tensor_tensor(ylow, ylow, psm[5][:, :].rearrange("p (j t) -> p j t", j=4), ALU.subtract)\
                            .then_inc(y_done, 1)
                    dve.wait_ge(wd_ps, LEVELS * p + i + 1)
                    nc.vector.tensor_tensor(wup, wup, psm[4][:, :].rearrange("p (j t) -> p j t", j=4), ALU.subtract)\
                        .then_inc(w_done, 1)
                if s == 20:
                    dve.wait_ge(z0_done, n)
                    if p == 0:
                        dve.wait_ge(tiny_done, 2)
                    for h in range(2):
                        nc.vector.tensor_scalar(z0d[:, h, :], z0[:, h, :], bsuf[:, 0, 2 * p + h:2 * p + h + 1], None,
                                                ALU.mult).then_inc(z0d_done, 1)
                if s == 22:
                    dve.wait_ge(ks_ps, n)
                    for h in range(2):
                        nc.vector.scalar_tensor_tensor(out=vnew[:, h, :], in0=psm[2][:, h * P:(h + 1) * P],
                                                       scalar=necol[:, 1, 2 * p + h:2 * p + h + 1], in1=vtok[:, 2 * h + 1, :],
                                                       op0=ALU.mult, op1=ALU.add).then_inc(vnew_done, 1)
                if s == 25:
                    dve.wait_ge(orms_done, n)
                    if p:
                        dve.wait_ge(mix_lo, p)
                    nc.vector.tensor_tensor(omix, psm[4][:, :].rearrange("p (h t) -> p h t", h=2), orms, ALU.mult)\
                        .then_inc(on_done, 1)
                if s == 26:
                    dve.wait_ge(on_done, n)
                    dve.wait_ge(evicted, evicted_after(4 * p + 3))
                    nc.vector.scalar_tensor_tensor(out=omix, in0=omix, scalar=gdn_w, in1=gz, op0=ALU.mult, op1=ALU.mult)\
                        .then_inc(omix_done, 1)
                if s == 27:
                    dve.wait_ge(mix_hi, n)
                    k = slice(8 + 2 * p, 10 + 2 * p)
                    nc.vector.tensor_tensor(mlo[:, k, :], omix, mhi[:, k, :].bitcast(F32), ALU.subtract).then_inc(mix_lo, 1)

            def gla(g, s):
                for hb in range(4):
                    h, b = divmod(hb, 2)
                    head, n = 2 * g + h, 4 * g + hb
                    s0 = 1 + 6 * hb
                    if s == s0 + 1:
                        dve.wait_ge(gexp_done, 2 * n + 2)
                        if n >= 2:
                            dve.wait_ge(score_ps, n - b)
                        nc.vector.tensor_tensor(gkd[:, b], gexp, gk[:, g, h:h + 1, b * P:(b + 1) * P].to_broadcast([P, 8, P]),
                                                ALU.mult).then_inc(gkd_done, 1)
                    if s == s0 + 5:
                        dve.wait_ge(score_ps, n + 1)
                        if n:
                            dve.wait_ge(gattn_done, n)
                        for k in range(2):
                            nc.vector.tensor_tensor(gprod[:, 4 * k:4 * k + 4], psm[2 + k][:, :].rearrange("p (l t) -> p l t", l=4),
                                                    mask[:, 4 * k:4 * k + 4], ALU.mult).then_inc(prod_done, 1)
                        dve.wait_ge(prod_done, 2 * n + 2)
                        if head >= 1:
                            dve.wait_ge(o_ps, 4 + max(0, head - 1))
                        nc.vector.tensor_reduce(gattn[:, h, 2 * b, :], gprod.rearrange("p l t -> p t l"), AX_X, ALU.add)\
                            .then_inc(gattn_done, 1)
                    if s == s0 + 9 and b:
                        dve.wait_ge(orms_done, 5 + head)
                        o = orms.rearrange("p a t -> p (a t)")[:, 0:T]
                        for a in range(2):
                            ins = nc.vector.scalar_tensor_tensor(out=gon[:, head, a * T:(a + 1) * T], in0=psm[5][:, a * T:(a + 1) * T],
                                                                 scalar=gla_w[:, a:a + 1], in1=o, op0=ALU.mult, op1=ALU.mult)
                            if a:
                                ins.then_inc(on_done, 1)

            def gate(head, part):
                if part == 0:
                    dve.wait_ge(evicted, evicted_after(24 + head))
                    dve.wait_ge(on_done, 5 + head)
                    dve.wait_ge(mix_lo, 4 + head)
                    nc.vector.tensor_tensor(omix, gon[:, head, :].rearrange("p (a t) -> p a t", a=2), gz, ALU.mult)\
                        .then_inc(omix_done, 1)
                else:
                    dve.wait_ge(mix_hi, 5 + head)
                    k = slice(2 * head, 2 * head + 2)
                    nc.vector.tensor_tensor(mlo[:, k, :], omix, mhi[:, k, :].bitcast(F32), ALU.subtract).then_inc(mix_lo, 1)

            for ph in range(7):
                for s in range(PHASE_STEPS):
                    if ph == 0 and s == 8:
                        split_lo(NARROW + AHEAD)
                    if s % 2 == 0 and not (1 <= ph <= 4 and s in POOL_STEPS):
                        if 1 <= ph <= 4 and s == POOL_STEPS[-1] + 2:
                            dve.wait_ge(lo_done, unit_of(ph, s) + AHEAD)
                        split_lo(unit_of(ph, s) + AHEAD)
                    if ph == 0:
                        setup(s)
                    if ph < 4 and s in CONV_STEPS:
                        conv(ph, CONV_STEPS.index(s))
                    if ph < 4 and s in (27, 28):
                        square(ph, s - 27)
                    if ph < 4 and s == 30:
                        decays(ph)
                    if 1 <= ph <= 4:
                        gdn(ph - 1, s)
                    if ph >= 5:
                        gla(ph - 5, s)
                    if ph == 6 and s in (9, 17, 25):
                        gate(s // 8 - 1, 0)
                    if ph == 6 and s in (11, 19, 27):
                        gate(s // 8 - 1, 1)

            def add_chunk(c, first_bank, units):
                dve.wait_ge(unit_used, units)
                for b in range(NB):
                    ps = bank[first_bank + b]
                    nc.vector.tensor_tensor(resid[:, b, 512 * c:512 * (c + 1)], resid[:, b, 512 * c:512 * (c + 1)],
                                            ps[:, :], ALU.add).then_inc(res_add, 1)

            for c in range(4):
                for q in range(OUT_UNITS):
                    split_lo(U_OUT + OUT_UNITS * c + q + AHEAD)
                    if c == 0 and q == 0:
                        gate(3, 0)
                    if c == 0 and q == 1:
                        gate(3, 1)
                        dve.wait_ge(x_again, 32)
                    if c and q == 0:
                        add_chunk(c - 1, 2 * ((c - 1) % 2), U_OUT + OUT_UNITS * c)
                    if c and q == 3:
                        for b in range(NB):
                            split_hT(8 + 2 * (c - 1) + b)

            def rms_total():
                nc.vector.tensor_reduce(stat[:, 16:18], stat[:, 8:16].rearrange("p (b c) -> p b c", b=2), AX_X, ALU.add)\
                    .then_inc(ss_done, 1)

            def gate_scale(n):
                two = fgate.rearrange("p (a t) -> p a t", a=2)
                nc.vector.tensor_tensor(two, psd[0][:, :].rearrange("p (a t) -> p a t", a=2),
                                        rb[:, :].unsqueeze(1).to_broadcast([P, 2, T]), ALU.mult).then_inc(g_scaled, 1)

            def up_and_product(n, lo_out, hi_in):
                dve.wait_ge(unit_used, n * GU_UNITS + (U_GU + GU_UNITS))
                nc.vector.tensor_tensor(fup.rearrange("p (a t) -> p a t", a=2), psd[1][:, :].rearrange("p (a t) -> p a t", a=2),
                                        rb[:, :].unsqueeze(1).to_broadcast([P, 2, T]), ALU.mult).then_inc(u_scaled, 1)
                dve.wait_ge(u_scaled, n + 1)
                dve.wait_ge(g_silu, n + 1)
                nc.vector.tensor_tensor(fprod, fup, fgate, ALU.mult).then_inc(f_done, 1)
                dve.wait_ge(f_hi, n + 1)
                nc.vector.tensor_tensor(lo_out, fprod, hi_in, ALU.subtract).then_inc(f_lo, 1)

            split_lo(U_GU + 2)
            add_chunk(3, 2, U_GU)
            split_lo(U_GU + 3)
            for b in range(NB):
                split_hT(14 + b)
            split_lo(U_GU + 4)
            dve.wait_ge(ssq_done, 8)
            rms_total()
            dve.wait_ge(r_done, 1)
            for b in range(NB):
                nc.vector.tensor_scalar(rb_col[b], ones[:, :], stat[:, 20 + b:21 + b], None, ALU.mult).then_inc(rcol_done, 1)
            for q in range(3, GU_UNITS):
                split_lo(U_GU + q + AHEAD)
                if q == 4:
                    dve.wait_ge(unit_used, U_GU + BLK_UNITS)
                    dve.wait_ge(rb_done, 1)
                    gate_scale(0)
            up_and_product(0, flo_t[:, 0:512], fhi_t[:, 0:512].bitcast(F32))
            with dve.Fori(1, PAIRS) as i:
                for q in range(GU_UNITS):
                    split_lo(U_GU + q + AHEAD, i * GU_UNITS + (U_GU + q + AHEAD))
                    if q == 4:
                        dve.wait_ge(unit_used, i * GU_UNITS + (U_GU + BLK_UNITS))
                        gate_scale(i)
                up_and_product(i, flo_t[:, bass.ds(i * 512, 512)], fhi_t[:, bass.ds(i * 512, 512)].bitcast(F32))

            for c in range(4):
                for q in range(DOWN_UNITS):
                    u = U_DOWN + DOWN_UNITS * c + q + AHEAD
                    if u < U_END:
                        split_lo(u)
                add_chunk(c, 2 - 2 * (c % 2), U_DOWN + DOWN_UNITS * (c + 1))
            dve.wait_ge(ssq_done, 16)
            rms_total()
            dve.wait_ge(r_done, 2)
            dve.wait_ge(fw_in, 16)
            for n in range(4):
                b, h = divmod(n, 2)
                v = resid[:, b, 1024 * h:1024 * (h + 1)]
                nc.vector.scalar_tensor_tensor(out=v, in0=v, scalar=stat[:, 20 + b:21 + b],
                                               in1=final_w[:, 1024 * h:1024 * (h + 1)], op0=ALU.mult, op1=ALU.mult)\
                    .then_inc(y_ready, 1)

        @block.tensor
        def _(pe):
            def mm(o, w, m, start=True, stop=True):
                return nc.tensor.matmul(o, w, m, start=start, stop=stop, skip_group_check=True)

            def three(o, wh, wl, xh, xl, start, stop):
                mm(o, wh, xh, start, False)
                mm(o, wh, xl, False, False)
                return mm(o, wl, xh, False, stop)

            pe.wait_ge(cst_ready, 1)
            pe.wait_ge(vec_in_sem, 80)
            nc.tensor.transpose(psd[0][:, 0:128], vec_in[:, 0, :], ident[:, :])
            nc.tensor.transpose(psd[0][:, 128:131], vec_in[0:3, 1, :], ident[0:3, 0:3]).then_inc(vec_ps, 1)

            def turn(b, g, ps):
                for k in range(4):
                    ins = nc.tensor.transpose(ps[:, k * P:(k + 1) * P], resid[:, b, (4 * g + k) * P:(4 * g + k + 1) * P],
                                              ident[:, :])
                ins.then_inc(hT_ps, 1)

            for n in range(8):
                b, g = divmod(n, 4)
                pe.wait_ge(x_scaled0 if g < 2 else x_scaled1, b + 1)
                if n >= 6:
                    pe.wait_ge(hT_staged, 4 * (n - 6) + 4)
                turn(b, g, psm[n % 6])

            def dense(ps, u, k0, half, tokens_on_partitions=False, signal=True):
                wh, wl = ring(whi, u, 4), ring(wlo, u, 4)
                for k in (2 * half, 2 * half + 1):
                    kt = k0 + k
                    for a in range(2):
                        o = ps[:, a * T:(a + 1) * T]
                        start, stop = kt == 0 and a == 0, kt == KT - 1
                        at = slice(a * P, (a + 1) * P)
                        if tokens_on_partitions:
                            mm(o, hhi[:, kt, at], wh[:, k, :], start, False)
                            mm(o, hhi[:, kt, at], wl[:, k, :], False, False)
                            ins = mm(o, hlo[:, kt, at], wh[:, k, :], False, stop)
                        else:
                            ins = three(o, wh[:, k, at], wl[:, k, at], hhi[:, kt, :], hlo[:, kt, :], start, stop)
                if half:
                    ins.then_inc(unit_used, 1)

            def setup(s):
                if s == 9:
                    pe.wait_ge(evicted, 2)
                    for b in range(NB):
                        ins = nc.tensor.transpose(psm[0][:, 16 * b:16 * b + 16], lowrank[32:48, b * P:(b + 1) * P],
                                                  ident[32:48, 32:48])
                    ins.then_inc(ab_ps, 1)
                    pe.wait_ge(gate_in, 32)
                    for b in range(NB):
                        mm(psm[1 + b][:, :], lowrank[0:RANK, b * P:(b + 1) * P], w2_sb, True, False)
                        mm(psm[1 + b][:, :], ones[0:1, :], gb_sb, False, True).then_inc(logit_ps, 1)
                if s == 15:
                    pe.wait_ge(gdec_step, 5)
                    pe.wait_ge(consts_ready, 1)
                    mm(psm[3][:, 0:16], upto, gdec.rearrange("p b h -> p (b h)"))
                    mm(psm[3][:, 16:32], after, gdec.rearrange("p b h -> p (b h)")).then_inc(cum_ps, 1)

            def gdn(p, s):
                n = p + 1
                if s == 0:
                    if p:
                        pe.wait_ge(z0_done, p)
                        pe.wait_ge(s_done, p)
                    for j in range(2):
                        pe.wait_ge(sq_done, 2 * p + j + 1)
                        mm(psm[j][:, :], ones[:, :], sumsq[:, 2 * j:2 * j + 2].rearrange("p h t -> p (h t)")).then_inc(nsum_ps, 1)
                if s == 1:
                    pe.wait_ge(gu_done, 4 * n)
                    if p:
                        pe.wait_ge(on_done, p)
                        pe.wait_ge(vnew_done, 2 * p)
                    mm(psm[4][:, :], after, gam.rearrange("p j t -> p (j t)")).then_inc(decay_ps, 1)
                    mm(psm[5][:, 0:T].rearrange("p (h t) -> p h t", h=2), ones[:, :],
                       gam.rearrange("p (h b) t -> p h b t", b=2)[:, :, 1, :]).then_inc(cumb_ps, 1)
                    for j in range(4):
                        h, b = divmod(j, 2)
                        ins = nc.tensor.transpose(psm[2][:, j * P:(j + 1) * P], kqv[:, 4 + h, b * P:(b + 1) * P], ident[:, :])
                    ins.then_inc(vT_ps, 1)
                if s == 3:
                    pe.wait_ge(kq_normed, 2 * p + 1)
                    for j in range(4):
                        h, b = divmod(j, 2)
                        k = kqv[:, h, b * P:(b + 1) * P]
                        ins = nc.tensor.transpose(psm[3][:, j * P:(j + 1) * P], k, ident[:, :])
                    ins.then_inc(kT_ps, 1)
                    for j in range(4):
                        h, b = divmod(j, 2)
                        k = kqv[:, h, b * P:(b + 1) * P]
                        ins = mm(psm[0][:, j * P:(j + 1) * P], k, k)
                    ins.then_inc(kk_ps, 1)
                if s == 4:
                    pe.wait_ge(kq_normed, 2 * n)
                    for j in range(4):
                        h, b = divmod(j, 2)
                        at = slice(b * P, (b + 1) * P)
                        ins = mm(psm[1][:, j * P:(j + 1) * P], kqv[:, h, at], kqv[:, 2 + h, at])
                    ins.then_inc(qk_ps, 1)
                if s == 5:
                    pe.wait_ge(ecum_done, n)
                    for i in range(2):
                        pe.wait_ge(sel_done, 2 * p + i + 1)
                        mm(psm[4 + i][:, 0:LOWER * 4 * (BASE - LOWER * i)], block_neg,
                           sel[i].rearrange("p s j t -> p (s j t)")).then_inc(rows_ps, 1)
                if s == 13:
                    pe.wait_ge(w_done, (1 + LEVELS) * p + 1)
                    pe.wait_ge(vtok_done, n)
                    for j in range(4):
                        ins = nc.tensor.transpose(psm[2][:, j * P:(j + 1) * P], wup[:, j, :], ident[:, :])
                    ins.then_inc(wT_ps, 1)
                if 14 <= s < 20:
                    i = (s - 14) // 2
                    if s % 2 == 0:
                        pe.wait_ge(nmask_done, LEVELS * p + i + 1)
                        pe.wait_ge(y_done, LEVELS * p + i + 1)
                        pe.wait_ge(ktok_done, n)
                        for j in range(4):
                            ins = mm(psm[3][:, j * P:(j + 1) * P], nmask[:, (LEVELS * p + i) % 2, j, :], ylow[:, j, :])
                        ins.then_inc(t1_ps, 1)
                    else:
                        pe.wait_ge(t1_done, LEVELS * p + i + 1)
                        pe.wait_ge(w_done, (1 + LEVELS) * p + 1 + i)
                        if i < LEVELS - 1:
                            for j in range(4):
                                ins = mm(psm[5][:, j * P:(j + 1) * P], wup[:, j, :], t1[:, j, :])
                            ins.then_inc(yd_ps, 1)
                        for j in range(4):
                            ins = mm(psm[4][:, j * P:(j + 1) * P], t1[:, j, :], wup[:, j, :])
                        ins.then_inc(wd_ps, 1)
                if s == 20:
                    pe.wait_ge(w_done, (1 + LEVELS) * n)
                    for h in range(2):
                        ins = mm(psm[0][:, h * P:(h + 1) * P], wup[:, 2 * h, :], vtok[:, 2 * h, :])
                    ins.then_inc(z0_ps, 1)
                if s == 21:
                    pe.wait_ge(z0d_done, 2 * n)
                    pe.wait_ge(attn_done, n)
                    for h in range(2):
                        ins = mm(psm[1][:, h * P:(h + 1) * P], ktok[:, 2 * h, :], z0d[:, h, :])
                    ins.then_inc(s_ps, 1)
                if s == 22:
                    pe.wait_ge(s_done, n)
                    for h in range(2):
                        ins = mm(psm[2][:, h * P:(h + 1) * P], kqv[:, h, P:T], state[:, h, :])
                    ins.then_inc(ks_ps, 1)
                if s == 23:
                    pe.wait_ge(vnew_done, 2 * n)
                    pe.wait_ge(t1_done, LEVELS * n)
                    for h in range(2):
                        ins = mm(psm[3][:, h * P:(h + 1) * P], wup[:, 2 * h + 1, :], vnew[:, h, :])
                    ins.then_inc(z1_ps, 1)
                if s == 24:
                    pe.wait_ge(z1_done, n)
                    pe.wait_ge(qdec_done, n)
                    for h in range(2):
                        o = psm[4][:, h * T:(h + 1) * T]
                        mm(o[:, 0:P], z0[:, h, :], attn[:, 2 * h, :])
                        mm(o[:, P:T], z1[:, h, :], attn[:, 2 * h + 1, :], True, False)
                        ins = mm(o[:, P:T], state[:, h, :], qdec[:, h, :], False, True)
                    ins.then_inc(o_ps, 1)
                if s == 25:
                    pe.wait_ge(osq_done, n)
                    mm(psm[5][:, :], ones[:, :], orms.rearrange("p a t -> p (a t)")).then_inc(osum_ps, 1)

            def gla(g, s):
                for hb in range(4):
                    h, b = divmod(hb, 2)
                    head, n = 2 * g + h, 4 * g + hb
                    s0 = 1 + 6 * hb
                    if s == s0:
                        if n == 0:
                            pe.wait_ge(mask_ready, 1)
                            pe.wait_ge(loga_split, 2)
                            pe.wait_ge(s_done, 4)
                        for k in range(2):
                            if n:
                                pe.wait_ge(gexp_done, 2 * n - 1 + k)
                            sums = msum[:, b + 4 * k:b + 4 * k + 4, :].rearrange("p l t -> p (l t)")
                            mm(psm[k][:, :], loga_hi[:, b, head * P:(head + 1) * P], sums, True, False)
                            mm(psm[k][:, :], loga_lo[:, b, head * P:(head + 1) * P], sums, False, True).then_inc(gsum_ps, 1)
                    if s == s0 + 4:
                        pe.wait_ge(gkd_done, n + 1)
                        pe.wait_ge(gqd_done, n + 1)
                        if n == 0:
                            pe.wait_ge(z1_done, 4)
                        else:
                            pe.wait_ge(prod_done, 2 * n)
                        for lev in range(7):
                            i = lev + 1 - b
                            mm(psm[2 + lev // 4][:, (lev % 4) * P:(lev % 4 + 1) * P], gkd[:, b, i, :], gqd[:, b, i, :])
                        at = slice(b * P, (b + 1) * P)
                        ins = mm(psm[3][:, 3 * P:], gk[:, g, h, at], gq[:, g, h, at])
                        if b:
                            pe.wait_ge(on_done, 4 + head)
                            ins = mm(psm[4][:, 0:P], gkd[:, 0, 0, :], gqd[:, 1, 7, :])
                        ins.then_inc(score_ps, 1)
                    if s == s0 + 7 and b:
                        pe.wait_ge(gattn_done, n + 1)
                        pe.wait_ge(cross_done, head + 1)
                        pe.wait_ge(evicted, evicted_after(16 + 4 * g + 2 + h))
                        for a in range(2):
                            o = psm[5][:, a * T:(a + 1) * T]
                            c = slice(a * P, (a + 1) * P)
                            mm(o, gv[:, head, 0, c], gattn[:, h, 0:2, :].rearrange("p i t -> p (i t)"), a == 0, False)
                            ins = mm(o[:, P:T], gv[:, head, 1, c], gattn[:, h, 2, :], False, True)
                        ins.then_inc(o_ps, 1)
                    if s == s0 + 8 and b:
                        pe.wait_ge(osq_done, 5 + head)
                        mm(psm[4][:, T:2 * T], ones[:, :], orms[:, 0, :], True, False)
                        mm(psm[4][:, T:2 * T], ones[:, :], orms[:, 1, :], False, True).then_inc(osum_ps, 1)

            for ph in range(7):
                for s in range(PHASE_STEPS):
                    blk, half = 4 * ph + s // 8, s % 2
                    u = unit_of(ph, s)
                    if blk == 1 and s == 8:
                        pe.wait_ge(lo_done, NARROW + 1)
                        for k in range(KT):
                            ins = three(psm[5][0:64, 0:T], ring(whi, NARROW, KT)[:, k, :], ring(wlo, NARROW, KT)[:, k, :],
                                        hhi[:, k, :], hlo[:, k, :], k == 0, k == KT - 1)
                        ins.then_inc(unit_used, 1)
                    if s % 8 == 0 and blk >= 2:
                        pe.wait_ge(evicted, evicted_after(blk - 2))
                    if half == 0:
                        pe.wait_ge(lo_done, u + 1)
                        if blk == 0:
                            pe.wait_ge(hT_lo, 5 + u)
                    dense(psd[blk % 2], u, 4 * (s // 2 % 4), half, 16 <= blk < 24 and blk % 4 >= 2)
                    if ph == 0:
                        setup(s)
                    if 1 <= ph <= 4:
                        gdn(ph - 1, s)
                    if ph >= 5:
                        gla(ph - 5, s)

            def dense_rows(first_bank, u, act_hi, act_lo, tiles, first, last):
                wh, wl = ring(whi, u, 2), ring(wlo, u, 2)
                for k in range(2):
                    kt = tiles[k]
                    for b in range(NB):
                        at = slice(b * P, (b + 1) * P)
                        o = bank[first_bank + b][:, :]
                        mm(o, act_hi[:, kt, at], wh[:, k, :], first and k == 0, False)
                        mm(o, act_hi[:, kt, at], wl[:, k, :], False, False)
                        ins = mm(o, act_lo[:, kt, at], wh[:, k, :], False, last and k == 1)
                ins.then_inc(unit_used, 1)

            for c in range(4):
                for q in range(OUT_UNITS):
                    u = U_OUT + OUT_UNITS * c + q
                    if q == 0 and c == 0:
                        pe.wait_ge(evicted, NBLK + 1)
                    if q == 0 and c == 1:
                        pe.wait_ge(on_done, 8)
                    if q == 0 and c >= 2:
                        pe.wait_ge(res_add, 2 * (c - 1))
                    pe.wait_ge(lo_done, u + 1)
                    if c == 0:
                        kt = OUT_ORDER[2 * q]
                        pe.wait_ge(mix_lo, kt // 2 - 3 if kt >= 8 else 5 + kt // 2)
                    dense_rows(2 * (c % 2), u, mhi, mlo, OUT_ORDER[2 * q:2 * q + 2], q == 0, q == OUT_UNITS - 1)
                    if c and q == 2:
                        pe.wait_ge(res_add, 2 * c)
                        for b in range(NB):
                            if c == 3:
                                pe.wait_ge(hT_staged, 4 * (8 + b) + 4)
                            turn(b, c - 1, psm[2 * ((c - 1) % 2) + b])

            def gate_or_up(ps, u, q):
                for half in range(2):
                    dense(ps, u, 4 * (q % BLK_UNITS), half)

            for q in range(GU_UNITS):
                u = U_GU + q
                pe.wait_ge(lo_done, u + 1)
                if q == 0:
                    pe.wait_ge(res_add, 6)
                if q < 4:
                    pe.wait_ge(hT_lo, 8 + 2 * (q + 1))
                gate_or_up(psd[q // BLK_UNITS], u, q)
                if q == 1:
                    pe.wait_ge(res_add, 8)
                    for b in range(NB):
                        pe.wait_ge(hT_staged, 4 * (10 + b) + 4)
                        turn(b, 3, psm[2 + b])
                if q == 3:
                    pe.wait_ge(rcol_done, 2)
                    for b in range(NB):
                        ins = mm(psm[0][:, b * P:(b + 1) * P], rb_col[b], ident[:, :])
                    ins.then_inc(rb_ps, 1)
            with pe.Fori(1, PAIRS) as i:
                for q in range(GU_UNITS):
                    if q == 0:
                        pe.wait_ge(g_scaled, i)
                    if q == 4:
                        pe.wait_ge(u_scaled, i)
                    pe.wait_ge(lo_done, i * GU_UNITS + (U_GU + q + 1))
                    gate_or_up(psd[q // BLK_UNITS], U_GU + q, q)

            for c in range(4):
                for q in range(DOWN_UNITS):
                    u = U_DOWN + DOWN_UNITS * c + q
                    if q == 0 and c == 1:
                        pe.wait_ge(u_scaled, PAIRS)
                    if q == 0 and c >= 2:
                        pe.wait_ge(res_add, 8 + 2 * (c - 1))
                    pe.wait_ge(lo_done, u + 1)
                    if c == 0:
                        pe.wait_ge(f_lo, q + 1)
                    dense_rows(2 - 2 * (c % 2), u, fhi, flo, (2 * q, 2 * q + 1), q == 0, q == DOWN_UNITS - 1)


_INS = ["x", "attn_norm_w", "w_in", "gla_gate_w2", "gla_gate_b", "gla_norm_w", "gdn_conv_w", "gdn_a_log",
        "gdn_dt_bias", "gdn_norm_w", "w_out", "ffn_norm_w", "w_gate", "w_up", "w_down", "final_norm_w"]


def kernel(**inputs):
    import numpy as _np
    import concourse.bacc as _bacc
    from concourse import mybir as _mybir
    from concourse.bass_utils import run_bass_kernel_spmd as _run

    nc = _bacc.Bacc("TRN2", target_bir_lowering=False, num_devices=1)
    arrays, args = {}, []
    for name in _INS:
        a = _np.ascontiguousarray(inputs[name])
        arrays[f"in_{name}_dram"] = a
        args.append(nc.dram_tensor(f"in_{name}_dram", a.shape, _mybir.dt.from_np(a.dtype), kind="ExternalInput").ap())
    args.append(nc.dram_tensor("out_0_dram", (1, T, D), _mybir.dt.float32, kind="ExternalOutput").ap())
    hybrid_block(nc, *args)
    r = _run(nc, [arrays], core_ids=[0])
    return r.results[0]["out_0_dram"]
```

```python
from contextlib import ExitStack

import concourse.bass as bass
from concourse import mybir

F32 = mybir.dt.float32
F32R = mybir.dt.float32r
ALU = mybir.AluOpType
ACT = mybir.ActivationFunctionType
AX_X = mybir.AxisListType.X

P = 128
T = 256
NB = T // P
D = 2048
KT = D // P
DFF = 5632
FT = DFF // P
EPS = 1e-6
DK = 128
GLA_HEADS, GDN_HEADS, RANK = 4, 8, 16
TAU = 16.0
TAPS = 4
BASE = 16
LOG_BASE = 4
LEVELS = 7 - LOG_BASE
BLOCKS = P // BASE
LOWER = BASE // 2

A_Q, A_K, A_V, A_LR, A_GATE = 0, 512, 1024, 2048, 2064
B_Q, B_K, B_V, B_A, B_Z = 3088, 4112, 5136, 6160, 6176

COLS = 256
UNIT = 1024
RING = 4
AHEAD = 2
PHASE_STEPS = 32
POOL_STEPS = (4, 6, 8, 10)

IN_BLOCKS = [c for p in range(4) for c in (B_K + COLS * p, B_Q + COLS * p, B_V + COLS * p, B_Z + COLS * p)]
IN_BLOCKS += [c for g in range(2) for c in (A_Q + COLS * g, A_K + COLS * g, A_V + 512 * g, A_V + 512 * g + COLS)]
IN_BLOCKS += [A_GATE + COLS * h for h in range(GLA_HEADS)]
NBLK = len(IN_BLOCKS)
BLK_UNITS = KT * COLS // UNIT
NARROW = BLK_UNITS
U_OUT = 1 + NBLK * BLK_UNITS
OUT_UNITS = KT * 512 // UNIT
U_GU = U_OUT + 4 * OUT_UNITS
PAIRS = DFF // COLS
GU_UNITS = 2 * BLK_UNITS
U_DOWN = U_GU + PAIRS * GU_UNITS
DOWN_UNITS = FT * 512 // UNIT
U_END = U_DOWN + 4 * DOWN_UNITS
LAST = RING
ACT_COLS = 640


def unit_of(ph, s):
    return 16 * ph + s // 2 + (0 if ph == 0 and s < 8 else 1)


def used_after(b):
    return BLK_UNITS if b == 0 else 1 + BLK_UNITS * (b + 1)


def evicted_after(b):
    return 1 if b == 0 else b + 2


def pairs_of(i):
    b = BASE << i
    return [(slice(e, e + b), slice(e + b, e + 2 * b)) for e in range(0, P, 2 * b)]


OUT_ORDER = list(range(8, KT)) + list(range(8))


def hybrid_block(nc, x, attn_norm_w, w_in, gla_gate_w2, gla_gate_b, gla_norm_w, gdn_conv_w, gdn_a_log,
                 gdn_dt_bias, gdn_norm_w, w_out, ffn_norm_w, w_gate, w_up, w_down, final_norm_w, out):
    x_tok = x.rearrange("a (b p) d -> p (a b) d", p=P)
    out_tok = out.rearrange("a (b p) d -> p (a b) d", p=P)

    with ExitStack() as ctx:
        def sb(name, words, dt=F32, stack=ctx):
            return stack.enter_context(nc.sbuf_tensor(name, [P, words], dt))

        def sem(name):
            return ctx.enter_context(nc.semaphore(name))

        def cut(t, at, *shape):
            n = 1
            for s in shape:
                n *= s
            v = t[:, at:at + n]
            if len(shape) == 2:
                return v.rearrange("p (a b) -> p a b", a=shape[0])
            if len(shape) == 3:
                return v.rearrange("p (a b c) -> p a b c", a=shape[0], b=shape[1])
            return v

        raw = sb("raw", RING * UNIT)
        whi = sb("whi", RING * UNIT, F32R)
        wlo = sb("wlo", RING * UNIT, F32R)
        hhi_t = sb("hhi", KT * T, F32R)
        hlo_t = sb("hlo", KT * T, F32R)
        big = sb("big", NB * D)
        ident = sb("ident", P)
        ones = sb("ones", P)
        vec_t = sb("vecT", 132)
        cst = sb("cst", 2)
        rb = sb("rb", T)
        stat = sb("stat", 32)
        hhi, hlo = cut(hhi_t, 0, KT, T), cut(hlo_t, 0, KT, T)
        resid = cut(big, 0, NB, D)
        conv_w = vec_t[:, 0:96]
        attn_w, ffn_w = vec_t[:, 96:112], vec_t[:, 112:128]
        gla_w, gdn_w = vec_t[:, 128:130], vec_t[:, 130:131]
        eps_c, dk_eps_c = cst[:, 0:1], cst[:, 1:2]

        mix_scope = ExitStack()
        mhi_t = sb("mixhi", KT * T, F32R, mix_scope)
        mlo_t = sb("mixlo", KT * T, F32R, mix_scope)
        mhi, mlo = cut(mhi_t, 0, KT, T), cut(mlo_t, 0, KT, T)
        consts = sb("consts", 8 * P, stack=mix_scope)
        mask = cut(consts, 0, 8, P)
        msum_t = sb("msum", 9 * P, F32R, mix_scope)
        msum = cut(msum_t, 0, 9, P)
        after, upto = msum[:, 0, :].bitcast(F32), msum[:, 8, :].bitcast(F32)
        kqv = cut(big, 0, 6, T)
        convd = cut(big, 6 * T, 6, T)
        sumsq = cut(big, 12 * T, 4, T)
        sq_hi, sq_lo = cut(mhi_t, 0, 4, T), cut(mlo_t, 0, 4, T)
        g_up_hi, g_up_lo = cut(mhi_t, 4 * T, 4, P), cut(mlo_t, 4 * T, 4, P)
        gkd = big[:, 0:2048].rearrange("p (b l t) -> p b l t", b=2, l=8)
        gqd = big[:, 2048:4096].rearrange("p (b l t) -> p b l t", b=2, l=8)
        work = sb("work", 2048, stack=mix_scope)
        convin = cut(work, 0, 6, T + TAPS - 1)
        gexp, gprod = cut(work, 0, 8, P), cut(work, 1024, 8, P)
        gdn_a = sb("gdn_a", 2048, stack=mix_scope)
        vtok, ktok = cut(gdn_a, 0, 4, P), cut(gdn_a, 512, 4, P)
        wup, ylow = cut(gdn_a, 1024, 4, P), cut(gdn_a, 1536, 4, P)
        gon = gdn_a[:, 0:2048].rearrange("p (h n) -> p h n", h=4)
        gdn_b = sb("gdn_b", 768, stack=mix_scope)
        nmask = cut(gdn_b, 0, 4, P)
        gattn = gdn_b[:, 0:768].rearrange("p (h i t) -> p h i t", h=2, i=3)
        gdn_c = sb("gdn_c", 5 * 512, stack=mix_scope)
        gam, bgam = cut(gdn_c, 0, 4, P), cut(gdn_c, 512, 4, P)
        attn, nmat, t1 = cut(gdn_c, 1024, 4, P), cut(gdn_c, 1536, 4, P), cut(gdn_c, 2048, 4, P)
        gates, gates2 = gdn_c[:, 0:512], gdn_c[:, 512:1024]
        lowrank = gdn_c[:, 1024:1280]
        w2_sb, gb_b = gdn_c[0:RANK, 1536:2048], gdn_c[:, 2048:2560]
        stage = cut(gdn_c, 0, 2, 512)
        gdn_d = sb("gdn_d", 7 * 256 + 3 * 512, stack=mix_scope)
        z0, z1, z0d = cut(gdn_d, 0, 2, P), cut(gdn_d, 256, 2, P), cut(gdn_d, 512, 2, P)
        state, vnew = cut(gdn_d, 768, 2, P), cut(gdn_d, 1024, 2, P)
        qdec, ecum = cut(gdn_d, 1280, 2, P), cut(gdn_d, 1536, 2, P)
        gz, orms, omix = cut(gdn_d, 1792, 2, T), cut(gdn_d, 2304, 2, T), cut(gdn_d, 2816, 2, T)
        vec_in = gdn_d[:, 0:256].rearrange("p (a b) -> p a b", a=2)
        gq_t = sb("gq", 1024, stack=mix_scope)
        gk_t = sb("gk", 1024, stack=mix_scope)
        gv_t = sb("gv", 2048, stack=mix_scope)
        loga_hi_t = sb("loga_hi", 1024, F32R, mix_scope)
        loga_lo_t = sb("loga_lo", 1024, F32R, mix_scope)
        gq, gk = cut(gq_t, 0, 2, 2, T), cut(gk_t, 0, 2, 2, T)
        gv = gv_t[:, :].rearrange("p (h b v) -> p h b v", h=4, b=2)
        loga_hi, loga_lo = cut(loga_hi_t, 0, NB, 512), cut(loga_lo_t, 0, NB, 512)
        loga = cut(gdn_d, 0, NB, 512)
        msum_in = cut(gdn_d, 1024, 9, P)
        tiny = sb("tiny", 216, stack=mix_scope)
        ab, gdec, beta, ecol, esuf = (cut(tiny, 32 * 0, 2, 16), cut(tiny, 32, 2, 8), cut(tiny, 48, 2, 8),
                                      cut(tiny, 64, 2, 8), cut(tiny, 80, 2, 8))
        g_hi, g_lo = cut(tiny, 184, 2, 8), cut(tiny, 200, 2, 8)
        ones_r = sb("ones_r", P, F32R, mix_scope)
        base_t = sb("base", P + BASE, stack=mix_scope)
        block_neg = base_t[:, 0:P]
        eye_neg = base_t[:, P:P + BASE]
        base_n, base_w = cut(gdn_a, 1536, 4, BASE), cut(gdn_a, 1536 + 4 * BASE, 4, BASE)
        sel = [cut(big, 12 * T, LOWER, 4, BASE), cut(big, 12 * T + 2 * BASE * BASE, LOWER, 4, LOWER)]
        bsuf, necol, tmp_a, tmp_b = cut(tiny, 96, 2, 8), cut(tiny, 112, 2, 8), cut(tiny, 128, 2, 8), cut(tiny, 144, 2, 8)
        alog_b, dtb_b, expa = tiny[:, 160:168], tiny[:, 168:176], tiny[:, 176:184]
        mix_scope.close()

        fhi_t = sb("ffhi", FT * T, F32R)
        flo_t = sb("fflo", FT * T, F32R)
        fhi, flo = cut(fhi_t, 0, FT, T), cut(flo_t, 0, FT, T)
        ffn_tmp = sb("ffn_tmp", 3 * 512)
        fgate, fup = ffn_tmp[:, 0:512], ffn_tmp[:, 512:1024]
        fprod = ffn_tmp[:, 1024:1536]
        final_w = sb("final_w", D)
        rb_col = [final_w[:, b * P:(b + 1) * P] for b in range(NB)]

        psd = [ctx.enter_context(nc.psum_tensor(f"psd{i}", [P, 512], F32)) for i in range(2)]
        psm = [ctx.enter_context(nc.psum_tensor(f"psm{i}", [P, 512], F32)) for i in range(6)]
        out_banks = [[psd[0], psm[3]], psm[4:6], psd, psm[4:6]]
        down_banks = [psm[4:6], psd, psm[4:6], psd]

        raw_in = [sem(f"raw_in{i}") for i in range(RING)]
        hi_done, lo_done, unit_used = sem("hi_done"), sem("lo_done"), sem("unit_used")
        x_in = [sem(f"x_in{i}") for i in range(2 * NB)]
        vec_in_sem, gate_in, tiny_in = sem("vec_in"), sem("gate_in"), sem("tiny_in")
        pool_seq, pad_ready, cst_ready, msum_built, consts_ready = (sem("pool_seq"), sem("pad_ready"), sem("cst_ready"),
                                                                    sem("msum_built"), sem("consts_ready"))
        mask_ready = sem("mask_ready")
        ms_act, ms_dve, ms_total, ms_ln = sem("ms_act"), sem("ms_dve"), sem("ms_total"), sem("ms_ln")
        rstd_done, x_scaled0, x_scaled1 = sem("rstd_done"), sem("x_scaled0"), sem("x_scaled1")
        vec_ps, vec_done = sem("vec_ps"), sem("vec_done")
        hT_ps, hT_staged, hT_hi, hT_lo = sem("hT_ps"), sem("hT_staged"), sem("hT_hi"), sem("hT_lo")
        evicted = sem("evicted")
        ab_ps, logit_ps, ab_done = sem("ab_ps"), sem("logit_ps"), sem("ab_done")
        lnexp, loga_done, loga_split, gdec_step, act_tiny = sem("lnexp"), sem("loga_done"), sem("loga_split"), sem("gdec_step"), sem("act_tiny")
        cum_ps, cum_exp, tiny_done = sem("cum_ps"), sem("cum_exp"), sem("tiny_done")
        ones_done, logit_done = sem("ones_done"), sem("logit_done")
        conv_step, silu_done, sq_done = sem("conv_step"), sem("silu_done"), sem("sq_done")
        sq_hi_done, sq_lo_done, sq_added = sem("sq_hi_done"), sem("sq_lo_done"), sem("sq_added")
        nsum_ps, ln_done, rn_done, kq_normed = sem("nsum_ps"), sem("ln_done"), sem("rn_done"), sem("kq_normed")
        gu_done, decay_ps, cumb_ps, gam_done, ecum_done = (sem("gu_done"), sem("decay_ps"), sem("cumb_ps"),
                                                           sem("gam_done"), sem("ecum_done"))
        bgam_done, vT_ps, kT_ps, kk_ps, qk_ps = sem("bgam_done"), sem("vT_ps"), sem("kT_ps"), sem("kk_ps"), sem("qk_ps")
        vtok_done, ktok_done, nmat_done, attn_done, qdec_done = (sem("vtok_done"), sem("ktok_done"), sem("nmat_done"),
                                                                 sem("attn_done"), sem("qdec_done"))
        eye_step, base_n_done, sel_done, rows_ps, base_step = (
            sem("eye_step"), sem("base_n_done"), sem("sel_done"), sem("rows_ps"), sem("base_step"))
        nmask_done, w_done, wT_ps, y_done = sem("nmask_done"), sem("w_done"), sem("wT_ps"), sem("y_done")
        t1_ps, t1_done, wd_ps, yd_ps = sem("t1_ps"), sem("t1_done"), sem("wd_ps"), sem("yd_ps")
        z0_ps, z0_done, z0d_done, s_ps, s_done = sem("z0_ps"), sem("z0_done"), sem("z0d_done"), sem("s_ps"), sem("s_done")
        ks_ps, vnew_done, z1_ps, z1_done = sem("ks_ps"), sem("vnew_done"), sem("z1_ps"), sem("z1_done")
        o_ps, osq_done, osum_ps, oln_done, orms_done, on_done = (sem("o_ps"), sem("osq_done"), sem("osum_ps"),
                                                                 sem("oln_done"), sem("orms_done"), sem("on_done"))
        omix_done, mix_hi, mix_lo = sem("omix_done"), sem("mix_hi"), sem("mix_lo")
        gsum_ps, gexp_done, gkd_done, gqd_done = sem("gsum_ps"), sem("gexp_done"), sem("gkd_done"), sem("gqd_done")
        score_ps, prod_done, gattn_done, cross_done = sem("score_ps"), sem("prod_done"), sem("gattn_done"), sem("cross_done")
        x_again, res_add, ssq_done, ss_done, r_ln, r_done = (sem("x_again"), sem("res_add"), sem("ssq_done"),
                                                             sem("ss_done"), sem("r_ln"), sem("r_done"))
        rcol_done, rb_ps, rb_done = sem("rcol_done"), sem("rb_ps"), sem("rb_done")
        g_scaled, g_silu, u_scaled, f_done, f_hi, f_lo = (sem("g_scaled"), sem("g_silu"), sem("u_scaled"),
                                                          sem("f_done"), sem("f_hi"), sem("f_lo"))
        fw_in, fw_scaled, partial, down_ps = sem("fw_in"), sem("fw_scaled"), sem("partial"), sem("down_ps")
        last_w, y_act, y_dve, stored = sem("last_w"), sem("y_act"), sem("y_dve"), sem("stored")

        block = ctx.enter_context(nc.Block())

        def slot(u):
            return u % RING

        def ring(t, u, k):
            s = slot(u) * UNIT
            return t[:, s:s + UNIT].rearrange("p (k c) -> p k c", k=k)

        @block.sync
        def _(sp):
            def load(u, src, n=None):
                n = u if n is None else n
                sp.wait_ge(lo_done, n - RING + 1)
                sp.dma_start(ring(raw, u, src.shape[1]), src).then_inc(raw_in[slot(u)], 16)

            def rows(w, k0, nk, c0, nc_):
                return w[k0 * P:(k0 + nk) * P, bass.ds(c0, nc_)].rearrange("(k p) c -> p k c", p=P)

            for b in range(NB):
                for h in range(2):
                    at = slice(h * D // 2, (h + 1) * D // 2)
                    sp.dma_start(resid[:, b, at], x_tok[:, b, at]).then_inc(x_in[2 * b + h], 16)
                if b == 0:
                    for dst, w in ((vec_in[0:96, 0, :], gdn_conv_w.rearrange("j (t p) -> (j t) p", p=P)),
                                   (vec_in[96:112, 0, :], attn_norm_w.rearrange("(t p) -> t p", p=P)),
                                   (vec_in[112:128, 0, :], ffn_norm_w.rearrange("(t p) -> t p", p=P)),
                                   (vec_in[0:2, 1, :], gla_norm_w.rearrange("(t p) -> t p", p=P)),
                                   (vec_in[2:3, 1, :], gdn_norm_w.rearrange("(t p) -> t p", p=P))):
                        sp.dma_start(dst, w).then_inc(vec_in_sem, 16)
            for u in range(RING):
                sp.dma_start(ring(raw, u, 4), rows(w_in, 4 * u, 4, IN_BLOCKS[0], COLS)).then_inc(raw_in[u], 16)
            sp.dma_start(w2_sb, gla_gate_w2).then_inc(gate_in, 16)
            sp.dma_start(gb_b, gla_gate_b.partition_broadcast(P)).then_inc(gate_in, 16)
            sp.dma_start(alog_b, gdn_a_log.partition_broadcast(P)).then_inc(tiny_in, 16)
            sp.dma_start(dtb_b, gdn_dt_bias.partition_broadcast(P)).then_inc(tiny_in, 16)
            sp.wait_ge(lo_done, 1)
            small = ring(raw, NARROW, KT)
            sp.dma_start(small[:, :, 0:RANK], rows(w_in, 0, KT, A_LR, RANK)).then_inc(raw_in[0], 16)
            sp.dma_start(small[:, :, 32:48], rows(w_in, 0, KT, B_A, 16)).then_inc(raw_in[0], 16)
            for u in range(NARROW + 1, U_OUT):
                b, q = divmod(u - 1, BLK_UNITS)
                load(u, rows(w_in, 4 * q, 4, IN_BLOCKS[b], COLS))
            sp.wait_ge(score_ps, 8)
            for b in range(NB):
                sp.dma_start(resid[:, b, :], x_tok[:, b, :]).then_inc(x_again, 16)
            for u in range(U_OUT, U_GU):
                c, q = divmod(u - U_OUT, OUT_UNITS)
                load(u, rows(w_out, OUT_ORDER[2 * q], 2, 512 * c, 512))
            with sp.Fori(0, PAIRS) as i:
                for q in range(GU_UNITS):
                    w = w_gate if q < BLK_UNITS else w_up
                    load(U_GU + q, rows(w, 4 * (q % BLK_UNITS), 4, i * COLS, COLS), i * GU_UNITS + (U_GU + q))
            sp.dma_start(final_w[:, :], final_norm_w.partition_broadcast(P)).then_inc(fw_in, 16)
            with sp.Fori(0, 2) as cc:
                for u in range(2 * DOWN_UNITS):
                    c, q = divmod(u, DOWN_UNITS)
                    load(U_DOWN + u, rows(w_down, 2 * q, 2, cc * 1024 + 512 * c, 512),
                         cc * (2 * DOWN_UNITS) + (U_DOWN + u))
            for b in range(NB):
                sp.wait_ge(y_dve, 2 * b + 1)
                sp.dma_start(out_tok[:, b, ACT_COLS:512 * 3], resid[:, b, ACT_COLS:512 * 3]).then_inc(stored, 16)
                sp.wait_ge(y_act, b + 1)
                sp.dma_start(out_tok[:, b, 0:ACT_COLS], resid[:, b, 0:ACT_COLS]).then_inc(stored, 16)
                sp.wait_ge(y_dve, 2 * b + 2)
                sp.dma_start(out_tok[:, b, 512 * 3:], resid[:, b, 512 * 3:]).then_inc(stored, 16)
            sp.wait_ge(stored, 16 * 3 * NB)

        @block.gpsimd
        def _(pool):
            made = [0]

            def then(ins):
                made[0] += 1
                ins.then_inc(pool_seq, 1)
                pool.wait_ge(pool_seq, made[0])

            def keep(view, op, base, pattern, cm, fill=0.0):
                then(nc.gpsimd.affine_select(out=view, in_=view, compare_op=op, fill=fill, base=base,
                                             pattern=pattern, channel_multiplier=cm))

            then(nc.gpsimd.memset(ident[:, :], 0.0))
            keep(ident[:, :], ALU.not_equal, 0, [[-1, P]], 1, 1.0)
            then(nc.gpsimd.memset(cst[:, 0:1], EPS))
            then(nc.gpsimd.memset(cst[:, 1:2], DK * EPS))
            nc.gpsimd.memset(ones[:, :], 1.0).then_inc(cst_ready, 1)
            nc.gpsimd.memset(convin[:, :, 0:TAPS - 1], 0.0).then_inc(pad_ready, 1)
            pool.wait_ge(vec_ps, 1)
            then(nc.gpsimd.memset(msum_in[:, :, :], 1.0))
            keep(msum_in[:, 0, :], ALU.is_ge, -1, [[-1, P]], 1)
            keep(msum_in[:, 8, :], ALU.is_ge, 0, [[1, P]], -1)
            for lev in range(7):
                b = 1 << lev
                n = P // (2 * b)
                v = msum_in[:, 1 + lev, :].rearrange("p (n o c) -> p n o c", o=2, c=b)
                keep(v[:, :, 0, :], ALU.is_ge, -1, [[-2 * b, n], [-1, b]], 1)
                keep(v[:, :, 0, :], ALU.is_ge, b - 1, [[2 * b, n], [0, b]], -1)
                keep(v[:, :, 1, :], ALU.is_ge, -b, [[-2 * b, n], [0, b]], 1)
                keep(v[:, :, 1, :], ALU.is_ge, b, [[2 * b, n], [1, b]], -1)
            nc.gpsimd.tensor_copy(mask[:, 7, :], ident[:, :]).then_inc(msum_built, 1)
            then(nc.gpsimd.memset(mask[:, 0:7, :], 0.0))
            for lev in range(7):
                b = 1 << lev
                n = P // (2 * b)
                m = mask[:, lev, :].rearrange("p (n o c) -> p n o c", o=2, c=b)[:, :, 1, :]
                then(nc.gpsimd.memset(m, 1.0))
                keep(m, ALU.is_ge, 0, [[-2 * b, n], [0, b]], 1)
                keep(m, ALU.is_ge, b - 1, [[2 * b, n], [0, b]], -1)
            then(nc.gpsimd.memset(block_neg, -1.0))
            v = block_neg.rearrange("p (n c) -> p n c", c=BASE)
            keep(v, ALU.is_ge, 0, [[-BASE, BLOCKS], [0, BASE]], 1)
            nc.gpsimd.affine_select(out=v, in_=v, compare_op=ALU.is_ge, fill=0.0, base=BASE - 1,
                                    pattern=[[BASE, BLOCKS], [0, BASE]], channel_multiplier=-1).then_inc(mask_ready, 1)

            def gla_q(n):
                head, b = divmod(n, 2)
                g, h = divmod(head, 2)
                pool.wait_ge(gexp_done, 2 * n + 2)
                if n >= 2:
                    pool.wait_ge(score_ps, n - b)
                nc.gpsimd.tensor_tensor(gqd[:, b], gexp, gq[:, g, h:h + 1, b * P:(b + 1) * P].to_broadcast([P, 8, P]),
                                        ALU.mult).then_inc(gqd_done, 1)

            def split_lo(u):
                pool.wait_ge(hi_done, u + 1)
                pool.wait_ge(lo_done, u)
                at = slice(slot(u) * UNIT, (slot(u) + 1) * UNIT)
                nc.gpsimd.tensor_tensor(wlo[:, at], raw[:, at], whi[:, at].bitcast(F32), ALU.subtract).then_inc(lo_done, 1)

            for p in range(4):
                for s in POOL_STEPS:
                    split_lo(unit_of(p + 1, s) + AHEAD)
                pool.wait_ge(nmat_done, p + 1)
                if p:
                    pool.wait_ge(t1_ps, LEVELS * (p - 1) + 1)
                nc.gpsimd.tensor_tensor(nmask, nmat, mask[:, LOG_BASE:LOG_BASE + 1, :].to_broadcast([P, 4, P]),
                                        ALU.mult).then_inc(nmask_done, 1)
            for n in range(2 * GLA_HEADS):
                gla_q(n)

        @block.scalar
        def _(act):
            def split_hi(u, n=None):
                n = u if n is None else n
                if isinstance(n, int):
                    act.wait_ge(raw_in[slot(u)], 16 * (n // RING + 1) + (16 if slot(u) == 0 and n else 0))
                    if n >= RING:
                        act.wait_ge(unit_used, n - RING + 1)
                nc.scalar.activation(whi[:, slot(u) * UNIT:(slot(u) + 1) * UNIT],
                                     raw[:, slot(u) * UNIT:(slot(u) + 1) * UNIT], ACT.Copy).then_inc(hi_done, 1)

            def split_hi_at(u, rounds, units):
                act.wait_ge(raw_in[slot(u)], rounds * 16 + (16 * (u // RING + 1) + (16 if slot(u) == 0 else 0)))
                act.wait_ge(unit_used, units + (u - RING + 1))
                split_hi(u, units)

            def lnexp_tables():
                nc.scalar.preload_act_table_set("natural_log_exp_and_others")

            def copy(o, i, **kw):
                return nc.scalar.activation(o, i, ACT.Copy, **kw)

            def rsqrt(o, i, tmp, scale, bias, ln_sem, n, done):
                nc.scalar.activation(tmp, i, ACT.Ln, bias=bias, scale=scale).then_inc(ln_sem, 1)
                act.wait_ge(ln_sem, n)
                nc.scalar.activation(o, tmp, ACT.Exp, scale=-0.5).then_inc(done, 1)

            def rms_x(b):
                act.wait_ge(x_in[2 * b], 16)
                nc.scalar.activation(gv_t[:, 0:D // 2], resid[:, b, 0:D // 2], ACT.Square,
                                     accum_out=stat[:, 2 * b:2 * b + 1]).then_inc(ms_act, 1)
                act.wait_ge(ms_total, b + 1)
                act.wait_ge(cst_ready, 1)
                rsqrt(stat[:, 6 + b:7 + b], stat[:, 4 + b:5 + b], stat[:, 24 + b:25 + b], 1.0 / D, eps_c, ms_ln, b + 1,
                      rstd_done)
                act.wait_ge(rstd_done, b + 1)
                copy(resid[:, b, D // 2:], resid[:, b, D // 2:], scale=stat[:, 6 + b:7 + b]).then_inc(x_scaled1, 1)

            def stage_hT(n, g, w, ps):
                act.wait_ge(hT_ps, n + 1)
                if n >= 2:
                    act.wait_ge(hT_lo, n - 1)
                for k in range(4):
                    copy(stage[:, n % 2, k * P:(k + 1) * P], ps[:, k * P:(k + 1) * P],
                         scale=w[:, 4 * g + k:4 * g + k + 1]).then_inc(hT_staged, 1)

            lnexp_tables()
            rms_x(0)
            act.wait_ge(vec_ps, 1)
            copy(vec_t[:, 0:128], psd[0][:, 0:128]).then_inc(vec_done, 1)
            copy(vec_t[:, 128:131], psd[0][:, 128:131]).then_inc(vec_done, 1)
            act.wait_ge(vec_done, 2)

            rms_x(1)
            for n in range(8):
                stage_hT(n, n // 2, attn_w, psm[n % 6])
                if n % 2:
                    split_hi(n // 2)

            def evict(b):
                act.wait_ge(unit_used, used_after(b) if b >= 0 else NARROW + 1)
                ps = psd[b % 2] if b >= 0 else psm[5]
                two = ps[:, :].rearrange("p (h t) -> p h t", h=2)
                if b < 0:
                    copy(lowrank[0:64, :], ps[0:64, 0:T]).then_inc(evicted, 1)
                elif b < 16 and b % 4 < 3:
                    p, j = divmod(b, 4)
                    if p:
                        act.wait_ge(conv_step, 24 * (p - 1) + 8 * (j + 1))
                    copy(convin[:, 2 * j:2 * j + 2, TAPS - 1:], two).then_inc(evicted, 1)
                elif b < 16:
                    if b // 4:
                        act.wait_ge(omix_done, b // 4)
                    nc.scalar.activation(gz, two, ACT.Silu).then_inc(evicted, 1)
                elif b < 24:
                    g, j = divmod(b - 16, 4)
                    if j == 0:
                        copy(gq[:, g], two, scale=DK ** -0.5).then_inc(evicted, 1)
                    elif j == 1:
                        copy(gk[:, g], two).then_inc(evicted, 1)
                    else:
                        copy(gv[:, 2 * g + j - 2], two).then_inc(evicted, 1)
                else:
                    act.wait_ge(omix_done, 4 + b - 24)
                    nc.scalar.activation(gz, two, ACT.Silu).then_inc(evicted, 1)
                    lnexp_tables()

            def setup(s):
                if s == 11:
                    lnexp_tables()
                    act.wait_ge(tiny_in, 32)
                    nc.scalar.activation(expa, alog_b, ACT.Exp).then_inc(act_tiny, 1)
                    act.wait_ge(ab_done, 2)
                    nc.scalar.activation(tmp_a, ab[:, :, 0:8], ACT.Abs).then_inc(act_tiny, 1)
                    act.wait_ge(act_tiny, 2)
                    nc.scalar.activation(tmp_a, tmp_a, ACT.Exp, scale=-1.0).then_inc(act_tiny, 1)
                    nc.scalar.activation(tmp_b, ab[:, :, 8:16], ACT.Exp, scale=-1.0).then_inc(act_tiny, 1)
                    act.wait_ge(act_tiny, 4)
                    nc.scalar.activation(tmp_a, tmp_a, ACT.Ln, bias=ones[:, 0:1]).then_inc(act_tiny, 1)
                if s in (12, 15):
                    b = s // 15
                    act.wait_ge(logit_done, b + 1)
                    if b:
                        act.wait_ge(loga_done, b)
                    nc.scalar.activation(gates, loga[:, b, :], ACT.Abs).then_inc(lnexp, 1)
                    act.wait_ge(lnexp, 3 * b + 1)
                    nc.scalar.activation(gates2, gates, ACT.Exp, scale=-1.0).then_inc(lnexp, 1)
                    act.wait_ge(lnexp, 3 * b + 2)
                    nc.scalar.activation(gates, gates2, ACT.Ln, bias=ones[:, 0:1]).then_inc(lnexp, 1)
                if s == 20:
                    act.wait_ge(cum_ps, 1)
                    nc.scalar.activation(tiny[:, 64:96], psm[3][:, 0:32], ACT.Exp).then_inc(cum_exp, 1)

            def silu(p, s):
                j = s - 26
                act.wait_ge(conv_step, 24 * p + 8 * (j + 1))
                if p:
                    act.wait_ge(ks_ps, p)
                nc.scalar.activation(kqv[:, 2 * j:2 * j + 2, :], convd[:, 2 * j:2 * j + 2, :], ACT.Silu).then_inc(silu_done, 1)

            def out_norm(n, ps, sum_ps, width, dv, s, s0, s1):
                if s == s0:
                    act.wait_ge(o_ps, n + 1)
                    if n:
                        act.wait_ge(on_done, n)
                    nc.scalar.activation(orms, ps, ACT.Square).then_inc(osq_done, 1)
                if s == s1:
                    act.wait_ge(osum_ps, n + 1)
                    o = orms.rearrange("p a t -> p (a t)")[:, 0:width]
                    rsqrt(o, sum_ps, o, 1.0 / dv, eps_c, oln_done, n + 1, orms_done)

            def gdn(p, s):
                n = p + 1
                if s == 1:
                    lnexp_tables()
                    act.wait_ge(nsum_ps, 2 * p + 1)
                    rsqrt(sumsq[:, 0:2], psm[0][:, :].rearrange("p (h t) -> p h t", h=2), sumsq[:, 0:2], 1.0, eps_c,
                          ln_done, 2 * p + 1, rn_done)
                    act.wait_ge(nsum_ps, 2 * p + 2)
                    rsqrt(sumsq[:, 2:4], psm[1][:, :].rearrange("p (h t) -> p h t", h=2), sumsq[:, 2:4], float(DK),
                          dk_eps_c, ln_done, 2 * p + 2, rn_done)
                if s == 2:
                    act.wait_ge(decay_ps, n)
                    act.wait_ge(cumb_ps, n)
                    nc.scalar.activation(gam, psm[4][:, :].rearrange("p (j t) -> p j t", j=4), ACT.Exp).then_inc(gam_done, 1)
                    nc.scalar.activation(ecum, psm[5][:, 0:T].rearrange("p (h t) -> p h t", h=2), ACT.Exp).then_inc(ecum_done, 1)
                if s == 3:
                    act.wait_ge(vT_ps, n)
                    copy(vtok, psm[2][:, :].rearrange("p (j t) -> p j t", j=4)).then_inc(vtok_done, 1)
                    act.wait_ge(kT_ps, n)
                    copy(ktok, psm[3][:, :].rearrange("p (j t) -> p j t", j=4)).then_inc(ktok_done, 1)
                if s == 13:
                    act.wait_ge(wT_ps, n)
                    copy(ylow, psm[2][:, :].rearrange("p (j t) -> p j t", j=4)).then_inc(y_done, 1)
                if 14 <= s < 20 and s % 2 == 0:
                    i = (s - 14) // 2
                    act.wait_ge(t1_ps, LEVELS * p + i + 1)
                    ps = psm[3][:, :].rearrange("p (j t) -> p j t", j=4)
                    if i == 0:
                        copy(t1, ps).then_inc(t1_done, 1)
                    else:
                        for even, odd in pairs_of(i):
                            ins = copy(t1[odd, :, even], ps[odd, :, even])
                        ins.then_inc(t1_done, 1)
                if s == 20:
                    act.wait_ge(z0_ps, n)
                    copy(z0, psm[0][:, 0:T].rearrange("p (h t) -> p h t", h=2)).then_inc(z0_done, 1)
                if s == 21:
                    act.wait_ge(s_ps, n)
                    copy(state, psm[1][:, 0:T].rearrange("p (h t) -> p h t", h=2)).then_inc(s_done, 1)
                if s == 23:
                    act.wait_ge(z1_ps, n)
                    copy(z1, psm[3][:, 0:T].rearrange("p (h t) -> p h t", h=2)).then_inc(z1_done, 1)
                out_norm(p, psm[4][:, :].rearrange("p (h t) -> p h t", h=2), psm[5][:, :], 512, DK, s, 24, 25)
                if s == 26:
                    act.wait_ge(omix_done, n)
                    copy(mhi[:, 8 + 2 * p:10 + 2 * p, :], omix).then_inc(mix_hi, 1)

            def gla(g, s):
                for hb in range(4):
                    h, b = divmod(hb, 2)
                    head, n = 2 * g + h, 4 * g + hb
                    s0 = 1 + 6 * hb
                    if s == s0:
                        if hb == 0:
                            lnexp_tables()
                        for k in range(2):
                            act.wait_ge(gsum_ps, 2 * n + k + 1)
                            if n and k == 0:
                                act.wait_ge(gkd_done, n)
                                act.wait_ge(gqd_done, n)
                            nc.scalar.activation(gexp[:, 4 * k:4 * k + 4, :], psm[k][:, :].rearrange("p (l t) -> p l t", l=4),
                                                 ACT.Exp, scale=1.0 / TAU).then_inc(gexp_done, 1)
                    if s == s0 + 5 and b:
                        act.wait_ge(score_ps, n + 1)
                        copy(gattn[:, h, 1, :], psm[4][:, 0:P]).then_inc(cross_done, 1)
                    if b:
                        out_norm(4 + head, psm[5][:, :].rearrange("p (a t) -> p a t", a=2), psm[4][:, T:2 * T], T, 2 * DK,
                                 s, s0 + 7, s0 + 9)

            def gate_hi(head):
                act.wait_ge(omix_done, 5 + head)
                copy(mhi[:, 2 * head:2 * head + 2, :], omix).then_inc(mix_hi, 1)

            for ph in range(7):
                for s in range(PHASE_STEPS):
                    if ph == 0 and s == 8:
                        split_hi(NARROW + AHEAD)
                        evict(0)
                    if s % 2 == 0:
                        if unit_of(ph, s) + AHEAD >= RING:
                            split_hi(unit_of(ph, s) + AHEAD)
                        if s % 8 == 0 and (ph or s):
                            evict(4 * ph + s // 8 - 1 if ph or s > 8 else -1)
                    if ph == 0:
                        setup(s)
                    if ph < 4 and 26 <= s < 29:
                        silu(ph, s)
                    if 1 <= ph <= 4:
                        gdn(ph - 1, s)
                    if ph >= 5:
                        gla(ph - 5, s)
                    if ph == 6 and s in (10, 18, 26):
                        gate_hi(s // 8 - 1)

            evict(27)

            def chunk_tail(c):
                for b in range(NB):
                    act.wait_ge(res_add, 2 * c + b + 1)
                    if 2 * c + b:
                        act.wait_ge(ssq_done, 2 * c + b)
                    nc.scalar.activation(gz.rearrange("p a t -> p (a t)"), resid[:, b, 512 * c:512 * (c + 1)], ACT.Square,
                                         accum_out=stat[:, 8 + 4 * b + c:9 + 4 * b + c]).then_inc(ssq_done, 1)

            for c in range(4):
                for q in range(OUT_UNITS):
                    split_hi(U_OUT + OUT_UNITS * c + q + AHEAD)
                    if c == 0 and q == 1:
                        gate_hi(3)
                    if c and q == 2:
                        chunk_tail(c - 1)
                    if c and q == 3:
                        for b in range(NB):
                            stage_hT(8 + 2 * (c - 1) + b, c - 1, ffn_w, psm[2 * ((c - 1) % 2) + b])

            def gate_silu(n):
                act.wait_ge(g_scaled, n)
                nc.scalar.activation(fgate, fgate, ACT.Silu).then_inc(g_silu, 1)

            split_hi(U_GU + 2)
            chunk_tail(3)
            split_hi(U_GU + 3)
            for b in range(NB):
                stage_hT(14 + b, 3, ffn_w, psm[2 + b])
            split_hi(U_GU + 4)
            act.wait_ge(ss_done, 1)
            nc.scalar.activation(stat[:, 18:20], stat[:, 16:18], ACT.Ln, bias=eps_c, scale=1.0 / D).then_inc(r_ln, 1)
            act.wait_ge(r_ln, 1)
            nc.scalar.activation(stat[:, 20:22], stat[:, 18:20], ACT.Exp, scale=-0.5).then_inc(r_done, 1)
            act.wait_ge(rb_ps, 1)
            copy(rb[:, :], psm[0][:, 0:T]).then_inc(rb_done, 1)
            for q in range(3, GU_UNITS):
                split_hi(U_GU + q + AHEAD)
                if q == 4:
                    gate_silu(1)
            act.wait_ge(f_done, 1)
            copy(fhi[:, 0:2, :], fprod.rearrange("p (a t) -> p a t", a=2)).then_inc(f_hi, 1)
            with act.Fori(1, PAIRS) as i:
                for q in range(GU_UNITS):
                    split_hi_at(U_GU + q + AHEAD, i * (GU_UNITS // RING), i * GU_UNITS)
                    if q == 4:
                        gate_silu(i + 1)
                act.wait_ge(f_done, i + 1)
                copy(fhi_t[:, bass.ds(i * 512, 512)], fprod).then_inc(f_hi, 1)

            def down_square(c, b):
                act.wait_ge(res_add, 8 + 2 * c + b + 1)
                act.wait_ge(ssq_done, 8 + 2 * c + b)
                nc.scalar.activation(fgate, resid[:, b, 512 * c:512 * (c + 1)], ACT.Square,
                                     accum_out=stat[:, 8 + 4 * b + c:9 + 4 * b + c]).then_inc(ssq_done, 1)

            for c in range(4):
                for q in range(DOWN_UNITS):
                    u = U_DOWN + DOWN_UNITS * c + q + AHEAD
                    if u < U_END:
                        split_hi(u)
                    if c == 0 and q == 3:
                        lnexp_tables()
                if c < 3:
                    for b in range(NB):
                        down_square(c, b)
            for b in range(NB):
                down_square(3, b)
                act.wait_ge(ssq_done, 8 + 6 + b + 1)
                act.wait_ge(partial, 2)
                nc.scalar.activation(stat[:, 18 + b:19 + b], stat[:, 11 + 4 * b:12 + 4 * b], ACT.Ln,
                                     bias=stat[:, 28 + b:29 + b], scale=1.0 / D).then_inc(r_ln, 1)
                act.wait_ge(r_ln, 2 + b)
                nc.scalar.activation(stat[:, 20 + b:21 + b], stat[:, 18 + b:19 + b], ACT.Exp, scale=-0.5).then_inc(r_done, 1)
                act.wait_ge(r_done, 2 + b)
                act.wait_ge(fw_scaled, 6)
                copy(resid[:, b, 0:ACT_COLS], resid[:, b, 0:ACT_COLS], scale=stat[:, 20 + b:21 + b]).then_inc(y_act, 1)

        @block.vector
        def _(dve):
            def split_lo(u, n=None):
                n = u if n is None else n
                dve.wait_ge(hi_done, n + 1)
                at = slice(slot(u) * UNIT, (slot(u) + 1) * UNIT)
                nc.vector.tensor_tensor(wlo[:, at], raw[:, at], whi[:, at].bitcast(F32), ALU.subtract).then_inc(lo_done, 1)

            def rms_x(b):
                dve.wait_ge(x_in[2 * b + 1], 16)
                v = resid[:, b, D // 2:]
                nc.vector.tensor_tensor_reduce(gq_t[:, 0:D // 2], v, v, 1.0, 0.0, ALU.mult, ALU.add,
                                               stat[:, 2 * b + 1:2 * b + 2]).then_inc(ms_dve, 1)
                dve.wait_ge(ms_act, b + 1)
                dve.wait_ge(ms_dve, b + 1)
                nc.vector.tensor_tensor(stat[:, 4 + b:5 + b], stat[:, 2 * b:2 * b + 1], stat[:, 2 * b + 1:2 * b + 2],
                                        ALU.add).then_inc(ms_total, 1)
                dve.wait_ge(rstd_done, b + 1)
                nc.vector.tensor_scalar(resid[:, b, 0:D // 2], resid[:, b, 0:D // 2], stat[:, 6 + b:7 + b], None, ALU.mult)\
                    .then_inc(x_scaled0, 1)

            def split_hT(n):
                b, g = n % 2, n % 8 // 2
                k, at = slice(4 * g, 4 * g + 4), slice(b * P, (b + 1) * P)
                s = stage[:, n % 2, :].rearrange("p (k t) -> p k t", k=4)
                dve.wait_ge(hT_staged, 4 * n + 4)
                nc.vector.tensor_copy(hhi[:, k, at], s).then_inc(hT_hi, 1)
                dve.wait_ge(hT_hi, n + 1)
                nc.vector.tensor_tensor(hlo[:, k, at], s, hhi[:, k, at].bitcast(F32), ALU.subtract).then_inc(hT_lo, 1)

            rms_x(0)
            rms_x(1)
            for n in range(8):
                split_hT(n)
                if n % 2:
                    split_lo(n // 2)

            def setup(s):
                if s == 10:
                    dve.wait_ge(ab_ps, 1)
                    nc.vector.tensor_copy(ab, psm[0][:, 0:32].rearrange("p (b c) -> p b c", b=2)).then_inc(ab_done, 1)
                    dve.wait_ge(ab_done, 1)
                    dve.wait_ge(tiny_in, 32)
                    for b in range(NB):
                        ins = nc.vector.tensor_tensor(ab[:, b, 0:8], ab[:, b, 0:8], dtb_b, ALU.add)
                        if b:
                            ins.then_inc(ab_done, 1)
                if s == 11:
                    dve.wait_ge(gate_in, 32)
                    for b in range(NB):
                        dve.wait_ge(logit_ps, b + 1)
                        nc.vector.tensor_tensor(loga[:, b, :], psm[1 + b][:, :], gb_b, ALU.add).then_inc(logit_done, 1)
                if s in (12, 15):
                    b = s // 15
                    dve.wait_ge(lnexp, 3 * b + 3)
                    nc.vector.scalar_tensor_tensor(out=loga[:, b, :], in0=loga[:, b, :], scalar=0.0, in1=gates,
                                                   op0=ALU.min, op1=ALU.subtract).then_inc(loga_done, 1)
                if s == 12:
                    dve.wait_ge(act_tiny, 5)
                    nc.vector.scalar_tensor_tensor(out=tmp_a, in0=ab[:, :, 0:8], scalar=0.0, in1=tmp_a,
                                                   op0=ALU.max, op1=ALU.add).then_inc(gdec_step, 1)
                    nc.vector.tensor_scalar(tmp_b, tmp_b, 1.0, None, ALU.add).then_inc(gdec_step, 1)
                    dve.wait_ge(gdec_step, 2)
                    for b in range(NB):
                        nc.vector.scalar_tensor_tensor(out=gdec[:, b, :], in0=tmp_a[:, b, :], scalar=-1.0, in1=expa,
                                                       op0=ALU.mult, op1=ALU.mult).then_inc(gdec_step, 1)
                    nc.vector.reciprocal(beta, tmp_b).then_inc(gdec_step, 1)
                if s == 14:
                    dve.wait_ge(msum_built, 1)
                    nc.vector.tensor_copy(msum, msum_in).then_inc(consts_ready, 1)
                    nc.vector.tensor_copy(ones_r[:, :], ones[:, :]).then_inc(ones_done, 1)
                if s == 17:
                    dve.wait_ge(gdec_step, 5)
                    nc.vector.tensor_copy(g_hi.bitcast(F32R), gdec).then_inc(gdec_step, 1)
                    dve.wait_ge(gdec_step, 6)
                    nc.vector.tensor_tensor(g_lo.bitcast(F32R), gdec, g_hi, ALU.subtract).then_inc(gdec_step, 1)
                if s == 18:
                    dve.wait_ge(loga_done, 2)
                    nc.vector.tensor_copy(loga_hi, loga).then_inc(loga_split, 1)
                    dve.wait_ge(loga_split, 1)
                    nc.vector.tensor_tensor(loga_lo, loga, loga_hi.bitcast(F32), ALU.subtract).then_inc(loga_split, 1)
                if s == 21:
                    dve.wait_ge(cum_exp, 1)
                    dve.wait_ge(gdec_step, 5)
                    nc.vector.tensor_tensor(bsuf, beta, esuf, ALU.mult).then_inc(tiny_done, 1)
                    nc.vector.tensor_scalar(necol, ecol, -1.0, None, ALU.mult).then_inc(tiny_done, 1)
                if s == 24:
                    dve.wait_ge(mask_ready, 1)
                    nc.vector.tensor_tensor(t1[:, 0, :], ident[:, :], block_neg, ALU.mult).then_inc(eye_step, 1)
                    dve.wait_ge(eye_step, 1)
                    nc.vector.tensor_reduce(eye_neg, t1[:, 0, :].rearrange("p (n c) -> p c n", n=BLOCKS), AX_X, ALU.add)\
                        .then_inc(eye_step, 1)

            def conv(p, j, taps=range(TAPS)):
                dve.wait_ge(evicted, evicted_after(4 * p + j))
                if p == 0 and j == 0:
                    dve.wait_ge(pad_ready, 1)
                    dve.wait_ge(vec_done, 2)
                if p:
                    dve.wait_ge(silu_done, 3 * (p - 1) + j + 1)
                tile0 = {0: 8, 1: 0, 2: 16}[j] + 2 * p
                for tap in taps:
                    for h in range(2):
                        c = 24 * tap + tile0 + h
                        src = convin[:, 2 * j + h, tap:tap + T]
                        dst = convd[:, 2 * j + h, :]
                        if tap == 0:
                            ins = nc.vector.tensor_scalar(dst, src, conv_w[:, c:c + 1], None, ALU.mult)
                        else:
                            dve.wait_ge(conv_step, 24 * p + 8 * j + 2 * tap - 1 + h)
                            ins = nc.vector.scalar_tensor_tensor(out=dst, in0=src, scalar=conv_w[:, c:c + 1], in1=dst,
                                                                 op0=ALU.mult, op1=ALU.add)
                        ins.then_inc(conv_step, 1)

            def square(p, j, part):
                k = slice(2 * j, 2 * j + 2)
                if part == 0:
                    dve.wait_ge(silu_done, 3 * p + j + 1)
                    if p:
                        dve.wait_ge(kq_normed, 2 * p)
                    nc.vector.tensor_tensor(sumsq[:, k], kqv[:, k], kqv[:, k], ALU.mult).then_inc(sq_done, 1)
                if part == 1:
                    dve.wait_ge(sq_done, 2 * p + j + 1)
                    nc.vector.tensor_copy(sq_hi[:, k], sumsq[:, k]).then_inc(sq_hi_done, 1)
                if part == 2:
                    dve.wait_ge(sq_hi_done, 2 * p + j + 1)
                    nc.vector.tensor_tensor(sq_lo[:, k], sumsq[:, k], sq_hi[:, k].bitcast(F32), ALU.subtract)\
                        .then_inc(sq_lo_done, 1)

            def decays(p, part):
                if p == 0:
                    dve.wait_ge(gdec_step, 7)
                    dve.wait_ge(consts_ready, 1)
                for j in range(4):
                    h, b = divmod(j, 2)
                    g = (g_hi, g_lo)[part][:, b, 2 * p + h:2 * p + h + 1]
                    nc.vector.tensor_scalar((g_up_hi, g_up_lo)[part][:, j, :], upto, g, None, ALU.mult).then_inc(gu_done, 1)

            base_steps = 2 + 4 * (BASE - 1)

            def gdn(p, s):
                n = p + 1
                if s in (1, 2):
                    j = s - 1
                    dve.wait_ge(rn_done, 2 * p + j + 1)
                    nc.vector.tensor_tensor(kqv[:, 2 * j:2 * j + 2], kqv[:, 2 * j:2 * j + 2], sumsq[:, 2 * j:2 * j + 2],
                                            ALU.mult).then_inc(kq_normed, 1)
                if s == 2:
                    dve.wait_ge(gam_done, n)
                    for j in range(4):
                        h, b = divmod(j, 2)
                        nc.vector.scalar_tensor_tensor(out=bgam[:, j, :], in0=gam[:, j, :],
                                                       scalar=beta[:, b, 2 * p + h:2 * p + h + 1], in1=upto,
                                                       op0=ALU.mult, op1=ALU.mult).then_inc(bgam_done, 1)
                if s == 3:
                    dve.wait_ge(bgam_done, 4 * n)
                    dve.wait_ge(kk_ps, n)
                    nc.vector.tensor_tensor(nmat, psm[0][:, :].rearrange("p (j t) -> p j t", j=4), bgam, ALU.mult)\
                        .then_inc(nmat_done, 1)
                    dve.wait_ge(nmat_done, n)
                    nc.vector.tensor_tensor(t1, nmat, block_neg.unsqueeze(1).to_broadcast([P, 4, P]), ALU.mult)\
                        .then_inc(base_step, 1)
                    dve.wait_ge(base_step, base_steps * p + 1)
                    nc.vector.tensor_reduce(base_n, t1.rearrange("p j (n c) -> p j c n", n=BLOCKS), AX_X, ALU.add)\
                        .then_inc(base_n_done, 1)
                    if p == 0:
                        dve.wait_ge(eye_step, 2)
                    nc.vector.tensor_copy(base_w, eye_neg.unsqueeze(1).to_broadcast([P, 4, BASE])).then_inc(base_step, 1)
                if s == 3:
                    dve.wait_ge(base_n_done, n)
                    for i in range(2):
                        cols = slice(LOWER * i, BASE)
                        nc.vector.tensor_tensor(sel[i], base_n[:, :, cols].unsqueeze(1).to_broadcast([P, LOWER, 4, BASE - LOWER * i]),
                                                eye_neg[:, LOWER * i:LOWER * (i + 1)].unsqueeze(2).unsqueeze(3)
                                                .to_broadcast([P, LOWER, 4, BASE - LOWER * i]), ALU.mult).then_inc(sel_done, 1)
                if 5 <= s < 12:
                    for r in range((s - 5) * 15 // 7, (s - 4) * 15 // 7):
                        i = r // LOWER
                        if r % LOWER == 0:
                            dve.wait_ge(rows_ps, 2 * p + i + 1)
                        row = psm[4 + i][:, 0:LOWER * 4 * (BASE - LOWER * i)].rearrange("p (s j t) -> p s j t", s=LOWER, j=4)
                        for j in range(4):
                            dve.wait_ge(base_step, base_steps * p + (4 * r + j - 1 if r else 2))
                            nc.vector.scalar_tensor_tensor(out=base_w[:, j, r + 1:], in0=row[:, r % LOWER, j, r + 1 - LOWER * i:],
                                                           scalar=base_w[:, j, r:r + 1], in1=base_w[:, j, r + 1:],
                                                           op0=ALU.mult, op1=ALU.add).then_inc(base_step, 1)
                if s == 11:
                    dve.wait_ge(base_step, base_steps * n)
                    nc.vector.tensor_tensor(wup.rearrange("p j (n c) -> p j n c", n=BLOCKS),
                                            base_w.unsqueeze(2).to_broadcast([P, 4, BLOCKS, BASE]),
                                            block_neg.rearrange("p (n c) -> p n c", n=BLOCKS).unsqueeze(1)
                                            .to_broadcast([P, 4, BLOCKS, BASE]), ALU.mult).then_inc(w_done, 1)
                if s == 12:
                    dve.wait_ge(qk_ps, n)
                    nc.vector.tensor_tensor(attn, psm[1][:, :].rearrange("p (j t) -> p j t", j=4), bgam, ALU.mult)\
                        .then_inc(attn_done, 1)
                    dve.wait_ge(ecum_done, n)
                    dve.wait_ge(kq_normed, 2 * n)
                    nc.vector.tensor_tensor(qdec, kqv[:, 2:4, P:T], ecum, ALU.mult).then_inc(qdec_done, 1)
                if 14 <= s < 20 and s % 2:
                    i = (s - 14) // 2
                    if i < LEVELS - 1:
                        dve.wait_ge(yd_ps, (LEVELS - 1) * p + i + 1)
                        ps = psm[5][:, :].rearrange("p (j t) -> p j t", j=4)
                        for even, odd in [(slice(0, P), slice(0, P))] if i == 0 else pairs_of(i):
                            ins = nc.vector.tensor_tensor(ylow[odd, :, even], ylow[odd, :, even], ps[odd, :, even], ALU.subtract)
                        ins.then_inc(y_done, 1)
                    dve.wait_ge(wd_ps, LEVELS * p + i + 1)
                    ps = psm[4][:, :].rearrange("p (j t) -> p j t", j=4)
                    for even, odd in [(slice(0, P), slice(0, P))] if i == 0 else pairs_of(i):
                        ins = nc.vector.tensor_tensor(wup[even, :, odd], wup[even, :, odd], ps[even, :, odd], ALU.subtract)
                    ins.then_inc(w_done, 1)
                if s == 20:
                    dve.wait_ge(z0_done, n)
                    if p == 0:
                        dve.wait_ge(tiny_done, 2)
                    for h in range(2):
                        nc.vector.tensor_scalar(z0d[:, h, :], z0[:, h, :], bsuf[:, 0, 2 * p + h:2 * p + h + 1], None,
                                                ALU.mult).then_inc(z0d_done, 1)
                if s == 22:
                    dve.wait_ge(ks_ps, n)
                    for h in range(2):
                        nc.vector.scalar_tensor_tensor(out=vnew[:, h, :], in0=psm[2][:, h * P:(h + 1) * P],
                                                       scalar=necol[:, 1, 2 * p + h:2 * p + h + 1], in1=vtok[:, 2 * h + 1, :],
                                                       op0=ALU.mult, op1=ALU.add).then_inc(vnew_done, 1)
                if s == 25:
                    dve.wait_ge(orms_done, n)
                    if p:
                        dve.wait_ge(mix_lo, p)
                    nc.vector.tensor_tensor(omix, psm[4][:, :].rearrange("p (h t) -> p h t", h=2), orms, ALU.mult)\
                        .then_inc(on_done, 1)
                if s == 26:
                    dve.wait_ge(on_done, n)
                    dve.wait_ge(evicted, evicted_after(4 * p + 3))
                    nc.vector.scalar_tensor_tensor(out=omix, in0=omix, scalar=gdn_w, in1=gz, op0=ALU.mult, op1=ALU.mult)\
                        .then_inc(omix_done, 1)
                if s == 27:
                    dve.wait_ge(mix_hi, n)
                    k = slice(8 + 2 * p, 10 + 2 * p)
                    nc.vector.tensor_tensor(mlo[:, k, :], omix, mhi[:, k, :].bitcast(F32), ALU.subtract).then_inc(mix_lo, 1)

            def gla(g, s):
                for hb in range(4):
                    h, b = divmod(hb, 2)
                    head, n = 2 * g + h, 4 * g + hb
                    s0 = 1 + 6 * hb
                    if s == s0 + 1:
                        dve.wait_ge(gexp_done, 2 * n + 2)
                        if n >= 2:
                            dve.wait_ge(score_ps, n - b)
                        nc.vector.tensor_tensor(gkd[:, b], gexp, gk[:, g, h:h + 1, b * P:(b + 1) * P].to_broadcast([P, 8, P]),
                                                ALU.mult).then_inc(gkd_done, 1)
                    if s == s0 + 5:
                        dve.wait_ge(score_ps, n + 1)
                        if n:
                            dve.wait_ge(gattn_done, n)
                        for k in range(2):
                            nc.vector.tensor_tensor(gprod[:, 4 * k:4 * k + 4], psm[2 + k][:, :].rearrange("p (l t) -> p l t", l=4),
                                                    mask[:, 4 * k:4 * k + 4], ALU.mult).then_inc(prod_done, 1)
                        dve.wait_ge(prod_done, 2 * n + 2)
                        if head >= 1:
                            dve.wait_ge(o_ps, 4 + max(0, head - 1))
                        nc.vector.tensor_reduce(gattn[:, h, 2 * b, :], gprod.rearrange("p l t -> p t l"), AX_X, ALU.add)\
                            .then_inc(gattn_done, 1)
                    if s == s0 + 7 and b:
                        dve.wait_ge(osq_done, 5 + head)
                        nc.vector.tensor_tensor(orms[:, 0, :], orms[:, 0, :], orms[:, 1, :], ALU.add).then_inc(sq_added, 1)
                    if s == s0 + 10 and b:
                        dve.wait_ge(orms_done, 5 + head)
                        o = orms.rearrange("p a t -> p (a t)")[:, 0:T]
                        for a in range(2):
                            ins = nc.vector.scalar_tensor_tensor(out=gon[:, head, a * T:(a + 1) * T], in0=psm[5][:, a * T:(a + 1) * T],
                                                                 scalar=gla_w[:, a:a + 1], in1=o, op0=ALU.mult, op1=ALU.mult)
                            if a:
                                ins.then_inc(on_done, 1)

            def gate(head, part):
                if part == 0:
                    dve.wait_ge(evicted, evicted_after(24 + head))
                    dve.wait_ge(on_done, 5 + head)
                    dve.wait_ge(mix_lo, 4 + head)
                    nc.vector.tensor_tensor(omix, gon[:, head, :].rearrange("p (a t) -> p a t", a=2), gz, ALU.mult)\
                        .then_inc(omix_done, 1)
                else:
                    dve.wait_ge(mix_hi, 5 + head)
                    k = slice(2 * head, 2 * head + 2)
                    nc.vector.tensor_tensor(mlo[:, k, :], omix, mhi[:, k, :].bitcast(F32), ALU.subtract).then_inc(mix_lo, 1)

            for ph in range(7):
                for s in range(PHASE_STEPS):
                    if ph == 0 and s == 8:
                        split_lo(NARROW + AHEAD)
                    if s % 2 == 0 and unit_of(ph, s) + AHEAD >= RING and not (1 <= ph <= 4 and s in POOL_STEPS):
                        if 1 <= ph <= 4 and s == POOL_STEPS[-1] + 2:
                            dve.wait_ge(lo_done, unit_of(ph, s) + AHEAD)
                        split_lo(unit_of(ph, s) + AHEAD)
                    if ph == 0:
                        setup(s)
                    if ph < 4 and s in (12, 24):
                        conv(ph, 2 * (s // 24))
                    if ph < 4 and s in (16, 18):
                        conv(ph, 1, range(s - 16, s - 14))
                    if ph < 4 and s == 27:
                        square(ph, 0, 0)
                        square(ph, 0, 1)
                    if ph < 4 and s == 28:
                        square(ph, 1, 0)
                        square(ph, 0, 2)
                        square(ph, 1, 1)
                        square(ph, 1, 2)
                    if ph < 4 and s in (21, 23):
                        decays(ph, s // 2 - 10)
                    if 1 <= ph <= 4:
                        gdn(ph - 1, s)
                    if ph >= 5:
                        gla(ph - 5, s)
                    if ph == 6 and s in (9, 17, 25):
                        gate(s // 8 - 1, 0)
                    if ph == 6 and s in (11, 19, 27):
                        gate(s // 8 - 1, 1)

            def add_chunk(c, banks, units):
                dve.wait_ge(unit_used, units)
                for b in range(NB):
                    ps = banks[b]
                    nc.vector.tensor_tensor(resid[:, b, 512 * c:512 * (c + 1)], resid[:, b, 512 * c:512 * (c + 1)],
                                            ps[:, :], ALU.add).then_inc(res_add, 1)

            for c in range(4):
                for q in range(OUT_UNITS):
                    split_lo(U_OUT + OUT_UNITS * c + q + AHEAD)
                    if c == 0 and q == 0:
                        gate(3, 0)
                    if c == 0 and q == 1:
                        gate(3, 1)
                        dve.wait_ge(x_again, 32)
                    if c and q == 0:
                        add_chunk(c - 1, out_banks[c - 1], U_OUT + OUT_UNITS * c)
                    if c and q == 3:
                        for b in range(NB):
                            split_hT(8 + 2 * (c - 1) + b)

            def rms_total():
                nc.vector.tensor_reduce(stat[:, 16:18], stat[:, 8:16].rearrange("p (b c) -> p b c", b=2), AX_X, ALU.add)\
                    .then_inc(ss_done, 1)

            def gate_scale(n):
                two = fgate.rearrange("p (a t) -> p a t", a=2)
                nc.vector.tensor_tensor(two, psd[0][:, :].rearrange("p (a t) -> p a t", a=2),
                                        rb[:, :].unsqueeze(1).to_broadcast([P, 2, T]), ALU.mult).then_inc(g_scaled, 1)

            def up_and_product(n, lo_out, hi_in):
                dve.wait_ge(unit_used, n * GU_UNITS + (U_GU + GU_UNITS))
                nc.vector.tensor_tensor(fup.rearrange("p (a t) -> p a t", a=2), psd[1][:, :].rearrange("p (a t) -> p a t", a=2),
                                        rb[:, :].unsqueeze(1).to_broadcast([P, 2, T]), ALU.mult).then_inc(u_scaled, 1)
                dve.wait_ge(u_scaled, n + 1)
                dve.wait_ge(g_silu, n + 1)
                nc.vector.tensor_tensor(fprod, fup, fgate, ALU.mult).then_inc(f_done, 1)
                dve.wait_ge(f_hi, n + 1)
                nc.vector.tensor_tensor(lo_out, fprod, hi_in, ALU.subtract).then_inc(f_lo, 1)

            split_lo(U_GU + 2)
            add_chunk(3, out_banks[3], U_GU)
            split_lo(U_GU + 3)
            for b in range(NB):
                split_hT(14 + b)
            split_lo(U_GU + 4)
            dve.wait_ge(ssq_done, 8)
            rms_total()
            dve.wait_ge(r_done, 1)
            for b in range(NB):
                nc.vector.tensor_scalar(rb_col[b], ones[:, :], stat[:, 20 + b:21 + b], None, ALU.mult).then_inc(rcol_done, 1)
            for q in range(3, GU_UNITS):
                split_lo(U_GU + q + AHEAD)
                if q == 4:
                    dve.wait_ge(unit_used, U_GU + BLK_UNITS)
                    dve.wait_ge(rb_done, 1)
                    gate_scale(0)
            up_and_product(0, flo_t[:, 0:512], fhi_t[:, 0:512].bitcast(F32))
            with dve.Fori(1, PAIRS) as i:
                for q in range(GU_UNITS):
                    split_lo(U_GU + q + AHEAD, i * GU_UNITS + (U_GU + q + AHEAD))
                    if q == 4:
                        dve.wait_ge(unit_used, i * GU_UNITS + (U_GU + BLK_UNITS))
                        gate_scale(i)
                up_and_product(i, flo_t[:, bass.ds(i * 512, 512)], fhi_t[:, bass.ds(i * 512, 512)].bitcast(F32))

            for c in range(4):
                for q in range(DOWN_UNITS):
                    u = U_DOWN + DOWN_UNITS * c + q + AHEAD
                    if u < U_END:
                        split_lo(u)
                    if c and q == 6:
                        dve.wait_ge(ssq_done, 8 + 2 * c)
                        dve.wait_ge(fw_in, 16)
                        cols = slice(512 * (c - 1), 512 * c)
                        for b in range(NB):
                            nc.vector.tensor_tensor(resid[:, b, cols], resid[:, b, cols], final_w[:, cols], ALU.mult)\
                                .then_inc(fw_scaled, 1)
                    if c == 3 and q == 7:
                        nc.vector.tensor_reduce(stat[:, 26:28], stat[:, 8:16].rearrange("p (b c) -> p b c", b=2)[:, :, 0:3],
                                                AX_X, ALU.add).then_inc(partial, 1)
                        dve.wait_ge(partial, 1)
                        nc.vector.tensor_scalar(stat[:, 28:30], stat[:, 26:28], 1.0 / D, EPS, ALU.mult, ALU.add)\
                            .then_inc(partial, 1)
                if c < 3:
                    add_chunk(c, down_banks[c], U_DOWN + DOWN_UNITS * (c + 1))
            cols = slice(512 * 3, D)
            for b in range(NB):
                last = (fup, fprod)[b]
                dve.wait_ge(down_ps, b + 1)
                nc.vector.tensor_tensor(resid[:, b, cols], resid[:, b, cols], down_banks[3][b][:, :], ALU.add).then_inc(res_add, 1)
                dve.wait_ge(res_add, 8 + 6 + b + 1)
                nc.vector.tensor_tensor(last, resid[:, b, cols], final_w[:, cols], ALU.mult).then_inc(last_w, 1)
                dve.wait_ge(r_done, 2 + b)
                rstd = stat[:, 20 + b:21 + b]
                dve.wait_ge(fw_scaled, 6)
                nc.vector.tensor_scalar(resid[:, b, ACT_COLS:512 * 3], resid[:, b, ACT_COLS:512 * 3], rstd, None, ALU.mult)\
                    .then_inc(y_dve, 1)
                dve.wait_ge(last_w, b + 1)
                nc.vector.tensor_scalar(resid[:, b, cols], last, rstd, None, ALU.mult).then_inc(y_dve, 1)

        @block.tensor
        def _(pe):
            def mm(o, w, m, start=True, stop=True):
                return nc.tensor.matmul(o, w, m, start=start, stop=stop, skip_group_check=True)

            def three(o, wh, wl, xh, xl, start, stop):
                mm(o, wh, xh, start, False)
                mm(o, wh, xl, False, False)
                return mm(o, wl, xh, False, stop)

            pe.wait_ge(cst_ready, 1)
            pe.wait_ge(vec_in_sem, 80)
            nc.tensor.transpose(psd[0][:, 0:128], vec_in[:, 0, :], ident[:, :])
            nc.tensor.transpose(psd[0][:, 128:131], vec_in[0:3, 1, :], ident[0:3, 0:3]).then_inc(vec_ps, 1)

            def turn(b, g, ps):
                for k in range(4):
                    ins = nc.tensor.transpose(ps[:, k * P:(k + 1) * P], resid[:, b, (4 * g + k) * P:(4 * g + k + 1) * P],
                                              ident[:, :])
                ins.then_inc(hT_ps, 1)

            for n in range(8):
                g, b = divmod(n, 2)
                pe.wait_ge(x_scaled0 if g < 2 else x_scaled1, b + 1)
                if n >= 6:
                    pe.wait_ge(hT_staged, 4 * (n - 6) + 4)
                turn(b, g, psm[n % 6])

            def dense(ps, u, k0, half, tokens_on_partitions=False):
                wh, wl = ring(whi, u, 4), ring(wlo, u, 4)
                for k in (2 * half, 2 * half + 1):
                    kt = k0 + k
                    for a in range(2):
                        o = ps[:, a * T:(a + 1) * T]
                        start, stop = kt == 0 and a == 0, kt == KT - 1
                        at = slice(a * P, (a + 1) * P)
                        if tokens_on_partitions:
                            mm(o, hhi[:, kt, at], wh[:, k, :], start, False)
                            mm(o, hhi[:, kt, at], wl[:, k, :], False, False)
                            ins = mm(o, hlo[:, kt, at], wh[:, k, :], False, stop)
                        else:
                            ins = three(o, wh[:, k, at], wl[:, k, at], hhi[:, kt, :], hlo[:, kt, :], start, stop)
                if half:
                    ins.then_inc(unit_used, 1)

            def setup(s):
                if s == 9:
                    pe.wait_ge(evicted, 2)
                    for b in range(NB):
                        ins = nc.tensor.transpose(psm[0][:, 16 * b:16 * b + 16], lowrank[32:48, b * P:(b + 1) * P],
                                                  ident[32:48, 32:48])
                    ins.then_inc(ab_ps, 1)
                    pe.wait_ge(gate_in, 32)
                    for b in range(NB):
                        mm(psm[1 + b][:, :], lowrank[0:RANK, b * P:(b + 1) * P], w2_sb).then_inc(logit_ps, 1)
                if s == 19:
                    pe.wait_ge(gdec_step, 5)
                    pe.wait_ge(consts_ready, 1)
                    mm(psm[3][:, 0:16], upto, gdec.rearrange("p b h -> p (b h)"))
                    mm(psm[3][:, 16:32], after, gdec.rearrange("p b h -> p (b h)")).then_inc(cum_ps, 1)

            def gdn(p, s):
                n = p + 1
                if s == 0:
                    if p:
                        pe.wait_ge(z0_done, p)
                        pe.wait_ge(s_done, p)
                if s in (0, 1):
                    k = slice(2 * s, 2 * s + 2)
                    pe.wait_ge(sq_lo_done, 2 * p + s + 1)
                    if p == 0:
                        pe.wait_ge(ones_done, 1)
                    mm(psm[s][:, :], ones_r[:, :], sq_hi[:, k].rearrange("p h t -> p (h t)"), True, False)
                    mm(psm[s][:, :], ones_r[:, :], sq_lo[:, k].rearrange("p h t -> p (h t)"), False, True).then_inc(nsum_ps, 1)
                if s == 1:
                    pe.wait_ge(gu_done, 8 * n)
                    if p:
                        pe.wait_ge(on_done, p)
                        pe.wait_ge(vnew_done, 2 * p)
                    for g in (g_up_hi, g_up_lo):
                        ins = mm(psm[4][:, :], msum[:, 0, :], g.rearrange("p j t -> p (j t)"), g is g_up_hi, g is g_up_lo)
                    ins.then_inc(decay_ps, 1)
                    for g in (g_up_hi, g_up_lo):
                        ins = mm(psm[5][:, 0:T].rearrange("p (h t) -> p h t", h=2), ones_r[:, :],
                                 g.rearrange("p (h b) t -> p h b t", b=2)[:, :, 1, :], g is g_up_hi, g is g_up_lo)
                    ins.then_inc(cumb_ps, 1)
                    pe.wait_ge(silu_done, 3 * n)
                    for j in range(4):
                        h, b = divmod(j, 2)
                        ins = nc.tensor.transpose(psm[2][:, j * P:(j + 1) * P], kqv[:, 4 + h, b * P:(b + 1) * P], ident[:, :])
                    ins.then_inc(vT_ps, 1)
                if s == 3:
                    pe.wait_ge(kq_normed, 2 * p + 1)
                    for j in range(4):
                        h, b = divmod(j, 2)
                        k = kqv[:, h, b * P:(b + 1) * P]
                        ins = nc.tensor.transpose(psm[3][:, j * P:(j + 1) * P], k, ident[:, :])
                    ins.then_inc(kT_ps, 1)
                    for j in range(4):
                        h, b = divmod(j, 2)
                        k = kqv[:, h, b * P:(b + 1) * P]
                        ins = mm(psm[0][:, j * P:(j + 1) * P], k, k)
                    ins.then_inc(kk_ps, 1)
                if s == 4:
                    pe.wait_ge(kq_normed, 2 * n)
                    for j in range(4):
                        h, b = divmod(j, 2)
                        at = slice(b * P, (b + 1) * P)
                        ins = mm(psm[1][:, j * P:(j + 1) * P], kqv[:, h, at], kqv[:, 2 + h, at])
                    ins.then_inc(qk_ps, 1)
                if s == 5:
                    pe.wait_ge(ecum_done, n)
                    for i in range(2):
                        pe.wait_ge(sel_done, 2 * p + i + 1)
                        mm(psm[4 + i][:, 0:LOWER * 4 * (BASE - LOWER * i)], block_neg,
                           sel[i].rearrange("p s j t -> p (s j t)")).then_inc(rows_ps, 1)
                if s == 13:
                    pe.wait_ge(w_done, (1 + LEVELS) * p + 1)
                    pe.wait_ge(vtok_done, n)
                    for j in range(4):
                        ins = nc.tensor.transpose(psm[2][:, j * P:(j + 1) * P], wup[:, j, :], ident[:, :])
                    ins.then_inc(wT_ps, 1)
                if 14 <= s < 20:
                    i = (s - 14) // 2
                    if s % 2 == 0:
                        if i == 0:
                            pe.wait_ge(nmask_done, n)
                        pe.wait_ge(y_done, LEVELS * p + i + 1)
                        pe.wait_ge(ktok_done, n)
                        for j in range(4):
                            o = psm[3][:, j * P:(j + 1) * P]
                            if i == 0:
                                ins = mm(o, nmask[:, j, :], ylow[:, j, :])
                            else:
                                for even, odd in pairs_of(i):
                                    ins = mm(o[odd, even], nmat[even, j, odd], ylow[even, j, even])
                        ins.then_inc(t1_ps, 1)
                    else:
                        pe.wait_ge(t1_done, LEVELS * p + i + 1)
                        pe.wait_ge(w_done, (1 + LEVELS) * p + 1 + i)
                        if i < LEVELS - 1:
                            for j in range(4):
                                o = psm[5][:, j * P:(j + 1) * P]
                                if i == 0:
                                    ins = mm(o, wup[:, j, :], t1[:, j, :])
                                else:
                                    for even, odd in pairs_of(i):
                                        ins = mm(o[odd, even], wup[odd, j, odd], t1[odd, j, even])
                            ins.then_inc(yd_ps, 1)
                        for j in range(4):
                            o = psm[4][:, j * P:(j + 1) * P]
                            if i == 0:
                                ins = mm(o, t1[:, j, :], wup[:, j, :])
                            else:
                                for even, odd in pairs_of(i):
                                    ins = mm(o[even, odd], t1[odd, j, even], wup[odd, j, odd])
                        ins.then_inc(wd_ps, 1)
                if s == 20:
                    pe.wait_ge(w_done, (1 + LEVELS) * n)
                    for h in range(2):
                        ins = mm(psm[0][:, h * P:(h + 1) * P], wup[:, 2 * h, :], vtok[:, 2 * h, :])
                    ins.then_inc(z0_ps, 1)
                if s == 21:
                    pe.wait_ge(z0d_done, 2 * n)
                    pe.wait_ge(attn_done, n)
                    for h in range(2):
                        ins = mm(psm[1][:, h * P:(h + 1) * P], ktok[:, 2 * h, :], z0d[:, h, :])
                    ins.then_inc(s_ps, 1)
                if s == 22:
                    pe.wait_ge(s_done, n)
                    for h in range(2):
                        ins = mm(psm[2][:, h * P:(h + 1) * P], kqv[:, h, P:T], state[:, h, :])
                    ins.then_inc(ks_ps, 1)
                if s == 23:
                    pe.wait_ge(vnew_done, 2 * n)
                    pe.wait_ge(t1_done, LEVELS * n)
                    for h in range(2):
                        ins = mm(psm[3][:, h * P:(h + 1) * P], wup[:, 2 * h + 1, :], vnew[:, h, :])
                    ins.then_inc(z1_ps, 1)
                if s == 24:
                    pe.wait_ge(z1_done, n)
                    pe.wait_ge(qdec_done, n)
                    for h in range(2):
                        o = psm[4][:, h * T:(h + 1) * T]
                        mm(o[:, 0:P], z0[:, h, :], attn[:, 2 * h, :])
                        mm(o[:, P:T], z1[:, h, :], attn[:, 2 * h + 1, :], True, False)
                        ins = mm(o[:, P:T], state[:, h, :], qdec[:, h, :], False, True)
                    ins.then_inc(o_ps, 1)
                if s == 25:
                    pe.wait_ge(osq_done, n)
                    mm(psm[5][:, :], ones[:, :], orms.rearrange("p a t -> p (a t)")).then_inc(osum_ps, 1)

            def gla(g, s):
                for hb in range(4):
                    h, b = divmod(hb, 2)
                    head, n = 2 * g + h, 4 * g + hb
                    s0 = 1 + 6 * hb
                    if s == s0:
                        if n == 0:
                            pe.wait_ge(mask_ready, 1)
                            pe.wait_ge(loga_split, 2)
                            pe.wait_ge(s_done, 4)
                        for k in range(2):
                            if n:
                                pe.wait_ge(gexp_done, 2 * n - 1 + k)
                            sums = msum[:, b + 4 * k:b + 4 * k + 4, :].rearrange("p l t -> p (l t)")
                            mm(psm[k][:, :], loga_hi[:, b, head * P:(head + 1) * P], sums, True, False)
                            mm(psm[k][:, :], loga_lo[:, b, head * P:(head + 1) * P], sums, False, True).then_inc(gsum_ps, 1)
                    if s == s0 + 4:
                        pe.wait_ge(gkd_done, n + 1)
                        pe.wait_ge(gqd_done, n + 1)
                        if n == 0:
                            pe.wait_ge(z1_done, 4)
                        else:
                            pe.wait_ge(prod_done, 2 * n)
                        for lev in range(7):
                            i = lev + 1 - b
                            mm(psm[2 + lev // 4][:, (lev % 4) * P:(lev % 4 + 1) * P], gkd[:, b, i, :], gqd[:, b, i, :])
                        at = slice(b * P, (b + 1) * P)
                        ins = mm(psm[3][:, 3 * P:], gk[:, g, h, at], gq[:, g, h, at])
                        if b:
                            pe.wait_ge(on_done, 4 + head)
                            ins = mm(psm[4][:, 0:P], gkd[:, 0, 0, :], gqd[:, 1, 7, :])
                        ins.then_inc(score_ps, 1)
                    if s == s0 + 7 and b:
                        pe.wait_ge(gattn_done, n + 1)
                        pe.wait_ge(cross_done, head + 1)
                        pe.wait_ge(evicted, evicted_after(16 + 4 * g + 2 + h))
                        for a in range(2):
                            o = psm[5][:, a * T:(a + 1) * T]
                            c = slice(a * P, (a + 1) * P)
                            mm(o, gv[:, head, 0, c], gattn[:, h, 0:2, :].rearrange("p i t -> p (i t)"), a == 0, False)
                            ins = mm(o[:, P:T], gv[:, head, 1, c], gattn[:, h, 2, :], False, True)
                        ins.then_inc(o_ps, 1)
                    if s == s0 + 9 and b:
                        pe.wait_ge(sq_added, head + 1)
                        mm(psm[4][:, T:2 * T], ones[:, :], orms[:, 0, :]).then_inc(osum_ps, 1)

            for ph in range(7):
                for s in range(PHASE_STEPS):
                    blk, half = 4 * ph + s // 8, s % 2
                    u = unit_of(ph, s)
                    if blk == 1 and s == 8:
                        pe.wait_ge(lo_done, NARROW + 1)
                        for k in range(KT):
                            ins = three(psm[5][0:64, 0:T], ring(whi, NARROW, KT)[:, k, :], ring(wlo, NARROW, KT)[:, k, :],
                                        hhi[:, k, :], hlo[:, k, :], k == 0, k == KT - 1)
                        ins.then_inc(unit_used, 1)
                    if s % 8 == 0 and blk >= 2:
                        pe.wait_ge(evicted, evicted_after(blk - 2))
                    if half == 0:
                        pe.wait_ge(lo_done, u + 1)
                        if blk == 0:
                            pe.wait_ge(hT_lo, 2 * u + 2)
                    dense(psd[blk % 2], u, 4 * (s // 2 % 4), half, 16 <= blk < 24 and blk % 4 >= 2)
                    if ph == 0:
                        setup(s)
                    if 1 <= ph <= 4:
                        gdn(ph - 1, s)
                    if ph >= 5:
                        gla(ph - 5, s)

            def dense_rows(banks, u, act_hi, act_lo, tiles, first, last):
                wh, wl = ring(whi, u, 2), ring(wlo, u, 2)
                for b in range(NB):
                    at = slice(b * P, (b + 1) * P)
                    o = banks[b][:, :]
                    for k in range(2):
                        kt = tiles[k]
                        mm(o, act_hi[:, kt, at], wh[:, k, :], first and k == 0, False)
                        mm(o, act_hi[:, kt, at], wl[:, k, :], False, False)
                        ins = mm(o, act_lo[:, kt, at], wh[:, k, :], False, last and k == 1)
                ins.then_inc(unit_used, 1)

            for c in range(4):
                for q in range(OUT_UNITS):
                    u = U_OUT + OUT_UNITS * c + q
                    if q == 0 and c == 0:
                        pe.wait_ge(evicted, NBLK)
                        pe.wait_ge(prod_done, 16)
                    if q == 0 and c == 1:
                        pe.wait_ge(on_done, 8)
                    if q == 0 and c >= 2:
                        pe.wait_ge(res_add, 2 * (c - 1))
                    if q == 0 and c == 2:
                        pe.wait_ge(evicted, NBLK + 1)
                    pe.wait_ge(lo_done, u + 1)
                    if c == 0:
                        kt = OUT_ORDER[2 * q]
                        pe.wait_ge(mix_lo, kt // 2 - 3 if kt >= 8 else 5 + kt // 2)
                    dense_rows(out_banks[c], u, mhi, mlo, OUT_ORDER[2 * q:2 * q + 2], q == 0, q == OUT_UNITS - 1)
                    if c and q == 2:
                        pe.wait_ge(res_add, 2 * c)
                        for b in range(NB):
                            if c == 3:
                                pe.wait_ge(hT_staged, 4 * (8 + b) + 4)
                            turn(b, c - 1, psm[2 * ((c - 1) % 2) + b])

            def gate_or_up(ps, u, q):
                for half in range(2):
                    dense(ps, u, 4 * (q % BLK_UNITS), half)

            for q in range(GU_UNITS):
                u = U_GU + q
                pe.wait_ge(lo_done, u + 1)
                if q == 0:
                    pe.wait_ge(res_add, 6)
                if q < 4:
                    pe.wait_ge(hT_lo, 8 + 2 * (q + 1))
                gate_or_up(psd[q // BLK_UNITS], u, q)
                if q == 1:
                    pe.wait_ge(res_add, 8)
                    for b in range(NB):
                        pe.wait_ge(hT_staged, 4 * (10 + b) + 4)
                        turn(b, 3, psm[2 + b])
                if q == 3:
                    pe.wait_ge(rcol_done, 2)
                    for b in range(NB):
                        ins = mm(psm[0][:, b * P:(b + 1) * P], rb_col[b], ident[:, :])
                    ins.then_inc(rb_ps, 1)
            with pe.Fori(1, PAIRS) as i:
                for q in range(GU_UNITS):
                    if q == 0:
                        pe.wait_ge(g_scaled, i)
                    if q == 4:
                        pe.wait_ge(u_scaled, i)
                    pe.wait_ge(lo_done, i * GU_UNITS + (U_GU + q + 1))
                    gate_or_up(psd[q // BLK_UNITS], U_GU + q, q)

            for c in range(4):
                for q in range(DOWN_UNITS):
                    u = U_DOWN + DOWN_UNITS * c + q
                    if q == 0 and c == 1:
                        pe.wait_ge(u_scaled, PAIRS)
                    if q == 0 and c >= 2:
                        pe.wait_ge(res_add, 8 + 2 * (c - 1))
                    if c == 3 and q >= DOWN_UNITS - LAST:
                        continue
                    pe.wait_ge(lo_done, u + 1)
                    if c == 0:
                        pe.wait_ge(f_lo, q + 1)
                    dense_rows(down_banks[c], u, fhi, flo, (2 * q, 2 * q + 1), q == 0, q == DOWN_UNITS - 1)
            for b in range(NB):
                at = slice(b * P, (b + 1) * P)
                for q in range(DOWN_UNITS - LAST, DOWN_UNITS):
                    u = U_DOWN + 3 * DOWN_UNITS + q
                    wh, wl = ring(whi, u, 2), ring(wlo, u, 2)
                    pe.wait_ge(lo_done, u + 1)
                    for k in range(2):
                        mm(down_banks[3][b][:, :], fhi[:, 2 * q + k, at], wh[:, k, :], False, False)
                        mm(down_banks[3][b][:, :], fhi[:, 2 * q + k, at], wl[:, k, :], False, False)
                        ins = mm(down_banks[3][b][:, :], flo[:, 2 * q + k, at], wh[:, k, :], False, q == DOWN_UNITS - 1 and k == 1)
                ins.then_inc(down_ps, 1)


_INS = ["x", "attn_norm_w", "w_in", "gla_gate_w2", "gla_gate_b", "gla_norm_w", "gdn_conv_w", "gdn_a_log",
        "gdn_dt_bias", "gdn_norm_w", "w_out", "ffn_norm_w", "w_gate", "w_up", "w_down", "final_norm_w"]


def kernel(**inputs):
    import numpy as _np
    import concourse.bacc as _bacc
    from concourse import mybir as _mybir
    from concourse.bass_utils import run_bass_kernel_spmd as _run

    nc = _bacc.Bacc("TRN2", target_bir_lowering=False, num_devices=1)
    arrays, args = {}, []
    for name in _INS:
        a = _np.ascontiguousarray(inputs[name])
        arrays[f"in_{name}_dram"] = a
        args.append(nc.dram_tensor(f"in_{name}_dram", a.shape, _mybir.dt.from_np(a.dtype), kind="ExternalInput").ap())
    args.append(nc.dram_tensor("out_0_dram", (1, T, D), _mybir.dt.float32, kind="ExternalOutput").ap())
    hybrid_block(nc, *args)
    r = _run(nc, [arrays], core_ids=[0])
    return r.results[0]["out_0_dram"]
```
